# Optimizing a Trainium2 kernel written in Bass

```python
import math
import jax, jax.numpy as jnp
from jax import lax
import numpy as np

D_MODEL = 2048
BATCH = 1
SEQ = 256
DEPTH = 1

SGU_WIDTH = D_MODEL // 2
SGU_CHUNK = 128
SGU_GROUPS = 8
SGU_GROUP_DIM = SGU_WIDTH // SGU_GROUPS
HY_WIDTH = D_MODEL // 2
HY_ORDER = 2
HY_SHORT = 3
HY_EMB = 33
HY_BANDS = (HY_EMB - 1) // 2
HY_FILTER_HIDDEN = 64
HY_DIRS = 2
HY_DECAY_TARGET = 1e-2
HY_FAST_DECAY = 0.3
HY_SLOW_DECAY = 1.5
HY_FILTER_INIT_SCALE = 0.05
N_BRANCHES = 2
D_FF = 4 * D_MODEL
IN_WIDTH = 2 * SGU_WIDTH + (HY_ORDER + 1) * HY_WIDTH + N_BRANCHES * D_MODEL
N_MOD = 6
DEEPNORM_ALPHA = (2.0 * DEPTH) ** 0.25
DEEPNORM_BETA = (8.0 * DEPTH) ** -0.25
LN_EPS = 1e-5


def layer_norm(x, g, b):
    xf = x.astype(jnp.float32)
    mu = jnp.mean(xf, axis=-1, keepdims=True)
    var = jnp.mean(jnp.square(xf - mu), axis=-1, keepdims=True)
    y = (xf - mu) * lax.rsqrt(var + LN_EPS) * g.astype(jnp.float32) + b.astype(jnp.float32)
    return y.astype(x.dtype)

def spatial_gating(u, v, ln_g, ln_b, w_s, b_s):
    bsz, s, _ = v.shape
    n_chunks = s // SGU_CHUNK
    vn = layer_norm(v, ln_g, ln_b).reshape(bsz, n_chunks, SGU_CHUNK, SGU_GROUPS, SGU_GROUP_DIM)
    mixed = jnp.einsum('gqp,bnpgc->bnqgc', w_s, vn) + b_s.T[None, None, :, :, None]
    return u * mixed.reshape(bsz, s, SGU_WIDTH)

def short_conv(z, w, b):
    s = z.shape[1]
    pad = HY_SHORT // 2
    zp = jnp.pad(z, ((0, 0), (pad, HY_SHORT - 1 - pad), (0, 0)))
    return sum(w[j] * zp[:, j:j + s] for j in range(HY_SHORT)) + b

def hyena_filters(L, w1, b1, w2, b2, freq, w3):
    f32 = jnp.float32
    t = jnp.linspace(0.0, 1.0, L, dtype=f32)[:, None]
    omega = 2.0 * math.pi * jnp.arange(L, dtype=f32)[:, None] / L
    bands = jnp.linspace(1e-4, HY_BANDS - 1, HY_BANDS, dtype=f32)[None, :]
    feats = jnp.concatenate([t, jnp.cos(bands * omega), -jnp.sin(bands * omega)], axis=-1)
    fr = freq.astype(f32)
    h = jnp.sin(fr * (feats @ w1.astype(f32) + b1.astype(f32)))
    h = jnp.sin(fr * (h @ w2.astype(f32) + b2.astype(f32)))
    h = h @ w3.astype(f32)
    min_decay = math.log(HY_DECAY_TARGET) / HY_SLOW_DECAY
    max_decay = math.log(HY_DECAY_TARGET) / HY_FAST_DECAY
    deltas = jnp.abs(jnp.linspace(min_decay, max_decay, HY_WIDTH, dtype=f32))
    window = jnp.exp(-t * deltas)
    return h.reshape(L, HY_DIRS, HY_ORDER, HY_WIDTH) * window[:, None, None, :]

def two_sided_spectrum(h_fwd, h_bwd):
    L, ch = h_fwd.shape
    k = jnp.concatenate([h_fwd.at[0].add(h_bwd[0]), jnp.zeros((1, ch), h_fwd.dtype), h_bwd[:0:-1]], axis=0)
    return jnp.fft.rfft(k, axis=0)

def fft_long_conv(u, k_spec, skip):
    L = u.shape[1]
    uf = u.astype(jnp.float32)
    y = jnp.fft.irfft(jnp.fft.rfft(uf, n=2 * L, axis=1) * k_spec[None], n=2 * L, axis=1)[:, :L]
    return (y + uf * skip.astype(jnp.float32)).astype(u.dtype)

def hyena(z, conv_w, conv_b, w1, b1, w2, b2, freq, w3, skip):
    z = short_conv(z, conv_w, conv_b)
    v, x1, x2 = jnp.split(z, HY_ORDER + 1, axis=-1)
    filt = hyena_filters(z.shape[1], w1, b1, w2, b2, freq, w3)
    y = v
    for n, gate in enumerate((x1, x2)):
        k_spec = two_sided_spectrum(filt[:, 0, n], filt[:, 1, n])
        y = gate * fft_long_conv(y, k_spec, skip[n])
    return y

def first_inputs(seed: int = 0) -> dict:
    key = jax.random.key(seed)
    keys = iter(jax.random.split(key, 40))
    D = D_MODEL
    L = DEPTH

    def nrm(shape, scale):
        return jax.random.normal(next(keys), shape, jnp.float32) * scale

    return {
        "x": nrm((BATCH, SEQ, D), 1.0),
        "c": nrm((BATCH, D), 1.0),
        "w_ada": nrm((L, D, N_MOD * D), 0.5 * D ** -0.5),
        "b_ada": nrm((L, N_MOD * D), 0.02),
        "w_in": nrm((L, D, IN_WIDTH), D ** -0.5),
        "b_in": nrm((L, IN_WIDTH), 0.02),
        "sgu_ln_g": 1.0 + nrm((L, SGU_WIDTH), 0.05),
        "sgu_ln_b": nrm((L, SGU_WIDTH), 0.02),
        "sgu_w": nrm((L, SGU_GROUPS, SGU_CHUNK, SGU_CHUNK), SGU_CHUNK ** -0.5),
        "sgu_b": 1.0 + nrm((L, SGU_GROUPS, SGU_CHUNK), 0.1),
        "hy_conv_w": nrm((L, HY_SHORT, (HY_ORDER + 1) * HY_WIDTH), HY_SHORT ** -0.5),
        "hy_conv_b": nrm((L, (HY_ORDER + 1) * HY_WIDTH), 0.02),
        "hy_w1": nrm((L, HY_EMB, HY_FILTER_HIDDEN), HY_EMB ** -0.5),
        "hy_b1": nrm((L, HY_FILTER_HIDDEN), 0.1),
        "hy_w2": nrm((L, HY_FILTER_HIDDEN, HY_FILTER_HIDDEN), HY_FILTER_HIDDEN ** -0.5),
        "hy_b2": nrm((L, HY_FILTER_HIDDEN), 0.1),
        "hy_freq": 1.0 + nrm((L, HY_FILTER_HIDDEN), 0.1),
        "hy_w3": nrm((L, HY_FILTER_HIDDEN, HY_DIRS * HY_ORDER * HY_WIDTH), HY_FILTER_INIT_SCALE * HY_FILTER_HIDDEN ** -0.5),
        "hy_skip": nrm((L, HY_ORDER, HY_WIDTH), 0.5),
        "w_branch_a": nrm((L, SGU_WIDTH, D), DEEPNORM_BETA * SGU_WIDTH ** -0.5),
        "w_branch_b": nrm((L, HY_WIDTH, D), DEEPNORM_BETA * HY_WIDTH ** -0.5),
        "w_o": nrm((L, D, D), DEEPNORM_BETA * D ** -0.5),
        "b_o": nrm((L, D), 0.02),
        "ln1_g": 1.0 + nrm((L, D), 0.05),
        "ln1_b": nrm((L, D), 0.02),
        "w_m1": nrm((L, D, D_FF), DEEPNORM_BETA * D ** -0.5),
        "b_m1": nrm((L, D_FF), 0.02),
        "w_m2": nrm((L, D_FF, D), DEEPNORM_BETA * D_FF ** -0.5),
        "b_m2": nrm((L, D), 0.02),
        "ln2_g": 1.0 + nrm((L, D), 0.05),
        "ln2_b": nrm((L, D), 0.02),
    }

def first_block(x, c, w_ada, b_ada, w_in, b_in, sgu_ln_g, sgu_ln_b, sgu_w, sgu_b,
              hy_conv_w, hy_conv_b, hy_w1, hy_b1, hy_w2, hy_b2, hy_freq, hy_w3, hy_skip,
              w_branch_a, w_branch_b, w_o, b_o, ln1_g, ln1_b,
              w_m1, b_m1, w_m2, b_m2, ln2_g, ln2_b):
    split_pts = [SGU_WIDTH, 2 * SGU_WIDTH, 2 * SGU_WIDTH + (HY_ORDER + 1) * HY_WIDTH]
    cond = jax.nn.silu(c)
    for l in range(DEPTH):
        mod = (cond @ w_ada[l] + b_ada[l])[:, None, :]
        sh1, sc1, g1, sh2, sc2, g2 = jnp.split(mod, N_MOD, axis=-1)

        h = x * (1.0 + sc1) + sh1
        z = h @ w_in[l] + b_in[l]
        z_u, z_v, z_h, z_g = jnp.split(z, split_pts, axis=-1)
        y_a = spatial_gating(jax.nn.gelu(z_u, approximate=False), jax.nn.gelu(z_v, approximate=False),
                             sgu_ln_g[l], sgu_ln_b[l], sgu_w[l], sgu_b[l]) @ w_branch_a[l]
        y_b = hyena(z_h, hy_conv_w[l], hy_conv_b[l], hy_w1[l], hy_b1[l], hy_w2[l], hy_b2[l],
                    hy_freq[l], hy_w3[l], hy_skip[l]) @ w_branch_b[l]
        gate_a, gate_b = jnp.split(jax.nn.sigmoid(z_g), N_BRANCHES, axis=-1)
        mix = (gate_a * y_a + gate_b * y_b) @ w_o[l] + b_o[l]
        x = layer_norm(DEEPNORM_ALPHA * x + g1 * mix, ln1_g[l], ln1_b[l])

        h = x * (1.0 + sc2) + sh2
        f = jnp.square(jax.nn.relu(h @ w_m1[l] + b_m1[l])) @ w_m2[l] + b_m2[l]
        x = layer_norm(DEEPNORM_ALPHA * x + g2 * f, ln2_g[l], ln2_b[l])
    return x


DEPTH_2 = 2

PLE_DIM = 256
POOL_EXPAND = 2
E_POOL = POOL_EXPAND * D_MODEL
POOL_WINDOWS = (2, 4, 8, 16)
N_POOL_GROUPS = len(POOL_WINDOWS)
G_POOL = E_POOL // N_POOL_GROUPS
N_HEADS = D_MODEL // 128
Q_RANK = 512
KV_RANK = 512
NOPE_DIM = 128
ROPE_DIM = 64
V_DIM = 128
QK_DIM = NOPE_DIM + ROPE_DIM
E_MLA = N_HEADS * V_DIM
ROPE_THETA = 10000.0
Q_BLOCK = 128
SM_SCALE = QK_DIM ** -0.5
NEG_INF = -1e30
EPS = 1e-6
N_POOL_LAYERS = (DEPTH_2 + 1) // 2
N_MLA_LAYERS = DEPTH_2 // 2
MLA_IN_DIM = Q_RANK + KV_RANK + ROPE_DIM + E_MLA


def rms_norm(x, g):
    xf = x.astype(jnp.float32)
    y = xf * lax.rsqrt(jnp.mean(xf * xf, axis=-1, keepdims=True) + EPS)
    return (y * g.astype(jnp.float32)).astype(x.dtype)

def rope(x, cos, sin):
    x1, x2 = jnp.split(x.astype(jnp.float32), 2, axis=-1)
    out = jnp.concatenate([x1 * cos - x2 * sin, x2 * cos + x1 * sin], axis=-1)
    return out.astype(x.dtype)

def pool_mixer(xn, w_in, w_group, scale, w_out):
    B, S, _ = xn.shape
    z = xn @ w_in
    u, g = jnp.split(z, 2, axis=-1)
    uf = u.astype(jnp.float32)
    csum = jnp.concatenate([jnp.zeros((B, 1, E_POOL), jnp.float32), jnp.cumsum(uf, axis=1)], axis=1)
    t = jnp.arange(S)
    pooled = []
    for j, w in enumerate(POOL_WINDOWS):
        sl = slice(j * G_POOL, (j + 1) * G_POOL)
        c = csum[:, :, sl]
        lagged = jnp.concatenate([jnp.zeros((B, w - 1, G_POOL), jnp.float32), c[:, :S - w + 1]], axis=1)
        count = jnp.minimum(t + 1, w).astype(jnp.float32)[None, :, None]
        pooled.append((c[:, 1:] - lagged) / count - uf[:, :, sl])
    pooled = jnp.stack(pooled, axis=2).astype(xn.dtype)
    mixed = jnp.einsum('bsgc,gcd->bsgd', pooled, w_group).reshape(B, S, E_POOL)
    return (mixed * scale * jax.nn.silu(g)) @ w_out

def causal_block_attention(q, k, v):
    B, S, H, Dq = q.shape
    nb = S // Q_BLOCK
    qb = q.reshape(B, nb, Q_BLOCK, H, Dq).transpose(1, 0, 2, 3, 4)
    kpos = jnp.arange(S)

    def one_block(args):
        qi, blk = args
        qpos = blk * Q_BLOCK + jnp.arange(Q_BLOCK)
        s = jnp.einsum('bqhd,bkhd->bhqk', qi, k, preferred_element_type=jnp.float32) * SM_SCALE
        s = jnp.where(kpos[None, :] <= qpos[:, None], s, NEG_INF)
        pr = jax.nn.softmax(s, axis=-1).astype(v.dtype)
        return jnp.einsum('bhqk,bkhd->bqhd', pr, v)

    out = lax.map(one_block, (qb, jnp.arange(nb)))
    return out.transpose(1, 0, 2, 3, 4).reshape(B, S, H, V_DIM)

def mla_mixer(xn, cos, sin, w_in, q_norm, w_uq, kv_norm, w_ukv, w_out):
    B, S, _ = xn.shape
    z = xn @ w_in
    q_lat = z[..., :Q_RANK]
    kv_lat = z[..., Q_RANK:Q_RANK + KV_RANK]
    k_pe = z[..., Q_RANK + KV_RANK:Q_RANK + KV_RANK + ROPE_DIM]
    g = z[..., Q_RANK + KV_RANK + ROPE_DIM:]
    q = (rms_norm(q_lat, q_norm) @ w_uq).reshape(B, S, N_HEADS, QK_DIM)
    kv = (rms_norm(kv_lat, kv_norm) @ w_ukv).reshape(B, S, N_HEADS, NOPE_DIM + V_DIM)
    q_nope, q_pe = q[..., :NOPE_DIM], q[..., NOPE_DIM:]
    k_nope, v = kv[..., :NOPE_DIM], kv[..., NOPE_DIM:]
    q_pe = rope(q_pe, cos[:, :, None, :], sin[:, :, None, :])
    k_pe = rope(k_pe, cos, sin)
    q = jnp.concatenate([q_nope, q_pe], axis=-1)
    k = jnp.concatenate([k_nope, jnp.broadcast_to(k_pe[:, :, None, :], (B, S, N_HEADS, ROPE_DIM))], axis=-1)
    o = causal_block_attention(q, k, v).reshape(B, S, E_MLA)
    return (o * jax.nn.silu(g)) @ w_out

def second_inputs(seed: int = 0) -> dict:
    key = jax.random.key(seed)
    ks = jax.random.split(key, 24)
    f32 = jnp.float32

    def nrm(k, shape, fan_in):
        return jax.random.normal(k, shape, f32) * (fan_in ** -0.5)

    def gain(k, shape):
        return 1.0 + 0.02 * jax.random.normal(k, shape, f32)

    offs = jax.random.randint(ks[2], (BATCH, 1), 0, 1024, dtype=jnp.int32)
    positions = offs + jnp.arange(SEQ, dtype=jnp.int32)[None, :]
    return {
        "x": jax.random.normal(ks[0], (BATCH, SEQ, D_MODEL), f32),
        "p": jax.random.normal(ks[1], (DEPTH_2, BATCH, SEQ, PLE_DIM), f32),
        "positions": positions,
        "pre_norm": gain(ks[3], (DEPTH_2, D_MODEL)),
        "post_norm": gain(ks[4], (DEPTH_2, D_MODEL)),
        "pool_w_in": nrm(ks[5], (N_POOL_LAYERS, D_MODEL, 2 * E_POOL), D_MODEL),
        "pool_w_group": nrm(ks[6], (N_POOL_LAYERS, N_POOL_GROUPS, G_POOL, G_POOL), G_POOL),
        "pool_scale": gain(ks[7], (N_POOL_LAYERS, E_POOL)),
        "pool_w_out": nrm(ks[8], (N_POOL_LAYERS, E_POOL, D_MODEL), E_POOL),
        "mla_w_in": nrm(ks[9], (N_MLA_LAYERS, D_MODEL, MLA_IN_DIM), D_MODEL),
        "mla_q_norm": gain(ks[10], (N_MLA_LAYERS, Q_RANK)),
        "mla_w_uq": nrm(ks[11], (N_MLA_LAYERS, Q_RANK, N_HEADS * QK_DIM), Q_RANK),
        "mla_kv_norm": gain(ks[12], (N_MLA_LAYERS, KV_RANK)),
        "mla_w_ukv": nrm(ks[13], (N_MLA_LAYERS, KV_RANK, N_HEADS * (NOPE_DIM + V_DIM)), KV_RANK),
        "mla_w_out": nrm(ks[14], (N_MLA_LAYERS, E_MLA, D_MODEL), E_MLA),
        "ple_norm": gain(ks[15], (DEPTH_2, D_MODEL)),
        "ple_w_gate": nrm(ks[16], (DEPTH_2, D_MODEL, D_MODEL), D_MODEL),
        "ple_w_proj": nrm(ks[17], (DEPTH_2, PLE_DIM, D_MODEL), PLE_DIM),
    }

def second_block(x, p, positions, pre_norm, post_norm, pool_w_in, pool_w_group, pool_scale, pool_w_out,
              mla_w_in, mla_q_norm, mla_w_uq, mla_kv_norm, mla_w_ukv, mla_w_out,
              ple_norm, ple_w_gate, ple_w_proj):
    inv_freq = ROPE_THETA ** (-jnp.arange(0, ROPE_DIM, 2, dtype=jnp.float32) / ROPE_DIM)
    ang = positions.astype(jnp.float32)[..., None] * inv_freq
    cos, sin = jnp.cos(ang), jnp.sin(ang)
    h = x
    for i in range(DEPTH_2):
        xn = rms_norm(h, pre_norm[i])
        j = i // 2
        if i % 2 == 0:
            out = pool_mixer(xn, pool_w_in[j], pool_w_group[j], pool_scale[j], pool_w_out[j])
        else:
            out = mla_mixer(xn, cos, sin, mla_w_in[j], mla_q_norm[j], mla_w_uq[j],
                            mla_kv_norm[j], mla_w_ukv[j], mla_w_out[j])
        h = h + rms_norm(out, post_norm[i])
        gate = jax.nn.sigmoid(rms_norm(h, ple_norm[i]) @ ple_w_gate[i])
        h = h + (p[i] @ ple_w_proj[i]) * gate
    return h


def setup_inputs(seed=0):
    out = dict(first_inputs(seed))
    for name, value in second_inputs(seed + 1).items():
        if name != "x":
            out[name + "_2"] = value
    return out


def reference(
    x, c, w_ada, b_ada, w_in, b_in, sgu_ln_g, sgu_ln_b, sgu_w, sgu_b, hy_conv_w, hy_conv_b,
    hy_w1, hy_b1, hy_w2, hy_b2, hy_freq, hy_w3, hy_skip, w_branch_a, w_branch_b, w_o, b_o,
    ln1_g, ln1_b, w_m1, b_m1, w_m2, b_m2, ln2_g, ln2_b, p_2, positions_2, pre_norm_2,
    post_norm_2, pool_w_in_2, pool_w_group_2, pool_scale_2, pool_w_out_2, mla_w_in_2,
    mla_q_norm_2, mla_w_uq_2, mla_kv_norm_2, mla_w_ukv_2, mla_w_out_2, ple_norm_2, ple_w_gate_2,
    ple_w_proj_2,
):
    x = first_block(
        x, c, w_ada, b_ada, w_in, b_in, sgu_ln_g, sgu_ln_b, sgu_w, sgu_b, hy_conv_w, hy_conv_b,
        hy_w1, hy_b1, hy_w2, hy_b2, hy_freq, hy_w3, hy_skip, w_branch_a, w_branch_b, w_o, b_o,
        ln1_g, ln1_b, w_m1, b_m1, w_m2, b_m2, ln2_g, ln2_b,
    )
    return second_block(
        x, p_2, positions_2, pre_norm_2, post_norm_2, pool_w_in_2, pool_w_group_2, pool_scale_2,
        pool_w_out_2, mla_w_in_2, mla_q_norm_2, mla_w_uq_2, mla_kv_norm_2, mla_w_ukv_2,
        mla_w_out_2, ple_norm_2, ple_w_gate_2, ple_w_proj_2,
    )


_drawn_inputs = setup_inputs


def setup_inputs(seed=0):
    import zlib

    import numpy as np

    out = dict(_drawn_inputs(seed))
    spreads = {}
    factors = {'b_ada': 4.589,
     'b_in': 8.0,
     'sgu_ln_g': 8.0,
     'sgu_ln_b': 8.0,
     'sgu_b': 8.0,
     'hy_conv_b': 8.0,
     'hy_w1': 5.372,
     'hy_b1': 8.0,
     'hy_w2': 4.528,
     'hy_b2': 8.0,
     'hy_freq': 8.0,
     'hy_w3': 4.513,
     'b_o': 4.278,
     'b_m1': 8.0,
     'b_m2': 3.976,
     'post_norm_2': 2.74,
     'pool_scale_2': 3.306,
     'mla_q_norm_2': 5.577,
     'mla_kv_norm_2': 3.804,
     'ple_norm_2': 23.172}
    for name, (base, spread) in spreads.items():
        noise = np.random.default_rng([zlib.crc32(name.encode()), seed]).standard_normal(out[name].shape)
        drawn = base * np.exp(spread * noise) if base else spread * noise
        out[name] = __import__('jax').numpy.asarray(drawn.astype(out[name].dtype))
    for name, factor in factors.items():
        out[name] = (out[name] * factor).astype(out[name].dtype)
    return out
```

```python
from contextlib import ExitStack

import math

import numpy as np

import concourse.bass as bass
from concourse import mybir
from concourse.alu_op_type import AluOpType as ALU

F32 = mybir.dt.float32
F32R = mybir.dt.float32r
I32 = mybir.dt.int32
ACT = mybir.ActivationFunctionType
AX = mybir.AxisListType
ds = bass.ds

P = 128
S = 256
D = 2048
KT = D // P
W1 = D // 2
FF = 4 * D
CH = 512
UNIT = 2048
HALF = UNIT // 2
SLOTS = 4
ALPHA = 2.0 ** 0.25
LN_EPS = 1e-5
RMS_EPS = 1e-6
HEADS = 16
NOPE, ROPE, VD = 128, 64, 128
QK = NOPE + ROPE
SM_SCALE = QK ** -0.5
NEG = -1e30
HID = 64
EMB = 33
E_POOL = 4096
MAGIC = 1.5 * 2.0 ** 23
INV_2PI = 1.0 / (2.0 * math.pi)
TWO_PI = (6.28125, 0.0019340515136718750, 2.0 * math.pi - 6.28125 - 0.0019340515136718750)
SIN_MAX = 3.1415925
KB = 1024


def tables():
    f32 = np.float32
    t = np.arange(S)[:, None].astype(np.float64)
    w = 2.0 * np.pi * (np.arange(S)[None, :] + 0.5) / (2 * S)
    cos_tf, sin_tf = np.cos(t * w), np.sin(t * w)
    dft = np.stack([cos_tf, -sin_tf, (cos_tf / S).T, (-sin_tf / S).T])
    bands = (EMB - 1) // 2
    lin = np.linspace(0.0, 1.0, S)[:, None]
    omega = 2.0 * np.pi * np.arange(S)[:, None] / S
    band = np.linspace(1e-4, bands - 1, bands)[None, :]
    feats = np.concatenate([lin, np.cos(band * omega), -np.sin(band * omega)], axis=1).T
    deltas = np.abs(np.linspace(math.log(1e-2) / 1.5, math.log(1e-2) / 0.3, W1))[None, :]
    window = np.exp(-lin * deltas)
    pool = np.zeros((4, S, S))
    for j, width in enumerate((2, 4, 8, 16)):
        for to in range(S):
            n = min(to + 1, width)
            pool[j, to - n + 1:to + 1, to] = 1.0 / n
            pool[j, to, to] -= 1.0
    freq = (10000.0 ** (-np.arange(0, ROPE, 2, dtype=np.float32) / ROPE))[None, :]
    return {
        "k_dft": dft.astype(f32), "k_feats": feats.astype(f32), "k_window": window.astype(f32),
        "k_pool": pool.astype(f32), "k_freq": freq.astype(f32), "k_ident": np.eye(P, dtype=f32),
    }


A2 = [("wwa", "wwa")] * 2
W2 = [("ww", "ww")] * 2
STREAM = [
    ("ada", 8, [("aaaa", "")]),
    ("in_vu", 2, A2), ("in_h", 2, A2), ("in_h2", 1, W2), ("in_g", 4, A2),
    ("mix", 4, [("wa", "wa")] * 2), ("w_o", 2, W2),
    ("m1a", 4, [("ww", "awwa")] * 2), ("m1b", 4, W2), ("m2", 8, W2),
    ("pool_u", 4, W2), ("pool_g", 4, [("w", "w"), ("ww", "ww")] * 2), ("pool_out", 4, W2),
    ("proj0", 1, [("ww", "")]), ("gate0", 2, W2),
    ("mla_in", 3, W2), ("k_pe", 1, [("w", "")]), ("w_uq", 1, [("w", "")] * 6), ("w_ukv", 1, [("w", "")] * 8),
    ("w_out", 2, W2), ("proj1", 1, [("ww", "")]), ("gate1", 2, W2),
]


class Stage:

    def __init__(self, kinds, first, rounds, chunks):
        self.first, self.rounds, self.chunks = first, rounds, chunks
        self.pattern = "".join(f + r for f, r in chunks)
        self.length = len(self.pattern)
        self.kinds = kinds
        self.size = UNIT
        assert rounds == 1 or self.length % SLOTS == 0

    def _line(self, of, i, at_least=False):
        values = [of(r) for r in range(self.rounds)]
        if isinstance(i, int):
            return values[i]
        slope = of(self.rounds - 1) - of(self.rounds - 2) if self.rounds > 1 else 0
        offset = max(v - slope * r for r, v in enumerate(values) if r)
        assert at_least or all(v == offset + slope * r for r, v in enumerate(values))
        return i * slope + offset

    def load(self, i, j):
        return self._line(lambda r: self.first + r * self.length + j, i)

    def before(self, kind, i, j):
        return self._line(lambda r: self.kinds[:self.first + r * self.length + j].count(kind), i)

    def slot(self, j):
        return (self.first + j) % SLOTS

    def landed(self, i, j):
        return self._line(lambda r: 16 * ((self.first + r * self.length + j) // SLOTS + 1), i)

    def freed(self, kind, i, j):
        return self._line(lambda r: self.kinds[:max(self.first + r * self.length + j - SLOTS + 1, 0)].count(kind),
                          i, at_least=True)

    def half(self, i, j):
        return self._line(lambda r: 2 * self.kinds[:self.first + r * self.length + j].count("w"), i)

    def half_slot(self, j, half):
        return (2 * self.kinds[:self.first + j].count("w") + half) % SLOTS


def stages():
    out, kinds = {}, "".join("".join(f + r for f, r in chunks) * n for _, n, chunks in STREAM)
    first = 0
    for name, rounds, chunks in STREAM:
        out[name] = Stage(kinds, first, rounds, chunks)
        first += rounds * out[name].length
    out["k_pe"].size = KT * ROPE
    return out


def rounds(eng, stage, body, last=False):
    n = stage.rounds
    end = n - 1 if last else n
    body(0)
    if end > 1:
        with eng.Fori(1, end) as i:
            body(i)
    if last and n > 1:
        body(n - 1)


def block_kernel(nc, a, out):
    ctx = ExitStack()
    ST = stages()

    def sem(name):
        return ctx.enter_context(nc.semaphore(name))

    ctx.enter_context(nc.sbuf_tensor("slab", [P, 207 * KB // 4], F32))

    def at(name, kb, shape, dt=F32):
        return nc.alloc_sbuf_tensor_at(name, [P, *shape], dt, offset=16512 + int(kb * KB))

    raw = [at(f"raw{i}", 8 * i, [UNIT]) for i in range(SLOTS)]
    w_hi = [at(f"w_hi{i}", 32 + 4 * i, [HALF], F32R) for i in range(SLOTS)]
    w_lo = [at(f"w_lo{i}", 48 + 4 * i, [HALF], F32R) for i in range(SLOTS)]
    res = at("res", 64, [2, D])
    x_hi = at("x_hi", 80, [KT, S], F32R)
    x_lo = at("x_lo", 96, [KT, S], F32R)
    ya_hi = at("ya_hi", 64, [W1 // P, S], F32R)
    ya_lo = at("ya_lo", 72, [W1 // P, S], F32R)

    acc = [at("ada_acc0", 112, [D]), at("ada_acc1", 120, [D])]
    dft = at("dft", 128, [4, 2, S])
    sgu_wT = at("sgu_wT", 136, [8, P])
    window = at("window", 140, [2, W1])
    w3 = at("w3", 148, [4 * W1])
    feats = at("feats", 164, [S])
    w1 = at("w1", 165, [HID])
    w2 = at("w2", 165.25, [HID])
    hid_arg = at("hid_arg", 166, [S])
    hid_n = at("hid_n", 167, [S])
    h_fwd = at("h_fwd", 168, [2, CH])
    h_bwd = at("h_bwd", 172, [2, CH])
    h_sum = at("h_sum", 176, [2, CH])
    spec_out = at("spec_out", 180, [4, CH])
    vu = at("vu", 140, [2, 2, W1])
    sgu_g = at("sgu_g", 156, [W1])
    sgu_b = at("sgu_b", 160, [W1])
    zh_out = [at(f"zh_out{i}", 164 + 4 * i, [2, CH]) for i in range(2)]
    conv_in = at("conv_in", 136, [3, 2, CH])
    conv_w = at("conv_w", 148, [4, CH])
    spec = at("spec", 136, [4, CH])
    prod = at("prod", 144, [4, CH])
    part = at("part", 152, [2, CH])
    hy = [at(f"hy{i}", 156 + 4 * i, [2, CH]) for i in range(3)]
    yb_hi = at("yb_hi", 172, [W1 // P, S], F32R)
    yb_lo = at("yb_lo", 180, [W1 // P, S], F32R)
    gate_out = [at(f"gate_out{i}", 120 + 4 * i, [2, CH]) for i in range(2)]
    skip = at("skip", 188, [CH])
    gate_in = [at(f"gate_in{i}", 136 + 8 * i, [2, 2, CH]) for i in range(2)]
    mixed = [at(f"mixed{i}", 152 + 4 * i, [2, CH]) for i in range(2)]
    mix_b = at("mix_b", 160, [2, CH])
    normed = at("normed", 136, [2, D])
    bias_o = at("bias_o", 128, [D])
    ln_g = at("ln_g", 152, [D])
    ln_b = at("ln_b", 160, [D])
    tmp = at("tmp", 168, [2, D])

    ff = at("ff", 120, [FF // P, S])
    ff_stage = [at("ff_stage0", 184, [2, CH]), at("ff_stage1", 198, [2, CH])]
    bias_ff = at("bias_ff", 190, [D])
    ln2_b = at("ln2_b", 120, [D])
    ln2_g = at("ln2_g", 128, [D])
    pool_m = at("pool_m", 112, [4, 2, S])
    u_stage = [at(f"u_stage{i}", 120 + 4 * i, [2, CH]) for i in range(2)]
    post_g = at("post_g", 128, [D])
    pooled = at("pooled", 152, [E_POOL // P, S])
    g_hi = at("g_hi", 136, [8, S], F32R)
    g_lo = at("g_lo", 144, [8, S], F32R)
    group_out = at("group_out", 120, [2, CH])
    pool_gate = at("pool_gate", 124, [2, CH])
    pool_stage = [at("pool_stage0", 184, [2, CH]), at("pool_stage1", 198, [2, CH])]
    p_tm = at("p_tm", 112, [4, S])
    p_lo = at("p_lo", 112, [4, S], F32R)
    p_hi = at("p_hi", 116, [4, S], F32R)
    proj = at("proj", 152, [2, D])
    q_tm = at("q_tm", 120, [2, HEADS, QK])
    kv_tm = at("kv_tm", 144, [2, HEADS, NOPE + VD])
    lat = at("lat", 144, [2, 2, CH])
    mla_gate_out = [at(f"mla_gate_out{i}", 168 + 4 * i, [2, CH]) for i in range(2)]
    rope_t = at("rope_t", 176, [4, HEADS, ROPE // 2])
    mla_sig = [at(f"mla_sig{i}", 176 + 4 * i, [2, CH]) for i in range(2)]
    lat_junk = at("lat_junk", 152, [4, CH])
    k_pe = at("k_pe", 198, [2, ROPE])
    k_peT = at("k_peT", 189, [S])
    qk_fm = [at(f"qk_fm{i}", 176 + 2 * i, [2, S]) for i in range(2)]
    q_peT = [at(f"q_peT{i}", 180 + i, [S]) for i in range(2)]
    score = [at(f"score{i}", 182 + 1.5 * i, [3, P]) for i in range(2)]
    probT = [at(f"probT{i}", 185 + 1.5 * i, [3, P]) for i in range(2)]
    prob = [at(f"prob{i}", 198.5 + 1.5 * i, [3, P]) for i in range(2)]
    g_tm = at("g_tm", 80, [2, D])
    mask = at("mask", 96, [3, P])
    post_g1 = at("post_g1", 128, [D])

    y_fm = [at(f"y_fm{i}", 190 + 4 * i, [4, S]) for i in range(2)]
    sgu_raw = at("sgu_raw", 190, [8, P])
    rows_a = at("rows_a", 194, [P])
    rows_b = at("rows_b", 194.5, [P])
    zero = at("zero", 205.5, [3 * W1 // P])
    bias_bc = [at(f"bias_bc{i}", 198 + 2 * i, [CH]) for i in range(2)]
    ident = at("ident", 202, [P])
    fm_a = at("fm_a", 202.5, [P])
    fm_b = at("fm_b", 203, [P])
    mod = at("mod", 203.5, [6, KT])
    cond = at("cond", 204, [KT])
    sig_c = at("sig_c", 204.0625, [KT])
    ones = at("ones", 204.125, [2])
    stats = at("stats", 204.25, [2, 4, 6])
    mv = at("mv", 204.5, [2, 2])
    rstd = at("rstd", 204.5625, [2, 2])
    ones_m = at("ones_m", 205, [P])
    pos_i = at("pos_i", 188, [P], I32)
    pos_f = at("pos_f", 188.5, [P])
    pos = at("pos", 205.625, [2])
    freq = at("freq", 189, [ROPE // 2])
    ang_n = at("ang_n", 189.25, [2, ROPE // 2])
    rope_cos = at("rope_cos", 205.75, [2, ROPE // 2])
    rope_sin = at("rope_sin", 206, [2, ROPE // 2])
    eps = at("eps", 204.59375, [2])
    lat_ss = at("lat_ss", 206.875, [3, 4])
    sm_max = at("sm_max", 206.75, [4, 2])
    sm_sum = at("sm_sum", 206.78125, [4, 2])
    sm_inv = at("sm_inv", 206.8125, [4, 2])
    ss = at("ss", 206.84375, [2, 2])
    COL = dict(pool_scale=0, q_norm=32, kv_norm=36, sgu_b=40, c=48, ln1_g=64, ln1_b=80, b1=96, b2=97, freq=98)

    ps = ctx.enter_context(nc.psum_tensor("ps", [P, 8, CH], F32))
    fm_ps = [ps[:, 4 + 2 * g:6 + 2 * g, :].rearrange("p a (b s) -> p (a b) s", s=S) for g in range(2)]

    spec_dram = nc.dram_tensor("spec_dram", [2, 2, P, 4 * CH], F32).ap()
    zh_dram = nc.dram_tensor("zh_dram", [S + 2, 3 * W1], F32).ap()
    gate_dram = nc.dram_tensor("gate_dram", [S, 2 * D], F32).ap()

    raw_full = [sem(f"raw_full{i}") for i in range(SLOTS)]
    hi_split = sem("hi_split")
    lo_split = sem("lo_split")
    half_used = sem("half_used")
    ada_added = sem("ada_added")
    acc_zeroed = sem("acc_zeroed")
    acc_ready = [sem(f"acc_ready{i}") for i in range(2)]
    ada_summed = sem("ada_summed")
    mod_ready = sem("mod_ready")
    pair_empty = sem("pair_empty")
    wide_empty = sem("wide_empty")
    fm_full = sem("fm_full")
    fm_empty = sem("fm_empty")
    fm_hi = sem("fm_hi")
    fm_lo = sem("fm_lo")
    consts = sem("consts")
    x_loaded = sem("x_loaded")
    vectors_out = sem("vectors_out")
    sgu_wT_out = sem("sgu_wT_out")
    setup_tr = sem("setup_tr")
    rows_zeroed = sem("rows_zeroed")
    ones_set = sem("ones_set")
    c_sig = sem("c_sig")
    cond_ready = sem("cond_ready")
    hid_mm = sem("hid_mm")
    hid_red = sem("hid_red")
    hid_sin = sem("hid_sin")
    filt_mm = sem("filt_mm")
    filt_win = sem("filt_win")
    filt_sum = sem("filt_sum")
    spec_mm = sem("spec_mm")
    spec_copied = sem("spec_copied")
    spec_stored = sem("spec_stored")
    bias_full = [sem(f"bias_full{i}") for i in range(2)]
    gelu_done = sem("gelu_done")
    sgu_consts = sem("sgu_consts")
    v_step = sem("v_step")
    s_step = sem("s_step")
    g_step = sem("g_step")
    var_ready = sem("var_ready")
    std_ready = sem("std_ready")
    vn_ready = sem("vn_ready")
    sgu_mm = sem("sgu_mm")
    sgu_out = sem("sgu_out")
    zh_stored = [sem(f"zh_stored{i}") for i in range(2)]
    zh_edges = sem("zh_edges")
    conv_loaded = sem("conv_loaded")
    conv_done = sem("conv_done")
    spec_in = sem("spec_in")
    skip_in = sem("skip_in")
    hy_f = sem("hy_f")
    hy_prod = sem("hy_prod")
    hy_i = sem("hy_i")
    hy_gated = sem("hy_gated")
    gate_sig = sem("gate_sig")
    gate_stored = [sem(f"gate_stored{i}") for i in range(2)]
    gate_loaded = [sem(f"gate_loaded{i}") for i in range(2)]
    mix_ready = sem("mix_ready")
    mix_turned = sem("mix_turned")
    x_again = sem("x_again")
    ln_consts = sem("ln_consts")
    pre_ready = sem("pre_ready")
    normed_ready = sem("normed_ready")
    x1_ready = sem("x1_ready")
    bias_o_in = sem("bias_o_in")
    g2_ready = sem("g2_ready")
    bias_ff_in = sem("bias_ff_in")
    ff_ready = sem("ff_ready")
    ln2_in = sem("ln2_in")
    res_ready = sem("res_ready")
    squares = sem("squares")
    mean_sq = sem("mean_sq")
    roots = sem("roots")
    pool_in = sem("pool_in")
    post_in = [sem(f"post_in{i}") for i in range(2)]
    pool_gated = sem("pool_gated")
    silu_ready = sem("silu_ready")
    product_ready = sem("product_ready")
    p_loaded = sem("p_loaded")
    gate_read = sem("gate_read")
    lat_ready = sem("lat_ready")
    lat_sq = sem("lat_sq")
    mla_silu = sem("mla_silu")
    mla_gate_stored = [sem(f"mla_gate_stored{i}") for i in range(2)]
    g_loaded = sem("g_loaded")
    angles = sem("angles")
    sines = sem("sines")
    pos_ready = sem("pos_ready")
    pos_turned = sem("pos_turned")
    mask_ready = sem("mask_ready")
    k_peT_ready = sem("k_peT_ready")
    qk_turned = sem("qk_turned")
    qk_out = sem("qk_out")
    qpe_out = sem("qpe_out")
    scored = sem("scored")
    score_ready = sem("score_ready")
    prob_ready = sem("prob_ready")
    prob_turned = sem("prob_turned")
    probT_out = sem("probT_out")
    k_peT_out = sem("k_peT_out")
    o_mm = sem("o_mm")
    o_ready = sem("o_ready")
    out_stored = sem("out_stored")
    RES_END = 10

    block = ctx.enter_context(nc.Block())

    N_SETUP = 23
    ADA_COLS = [0, 1, 3, 2, 4, 5]
    ADA_ACC = [0, 1, 1, 0, 1, 0]
    ADA_NTH = [1, 1, 2, 2, 3, 3]
    IN_COLS = ([W1, W1 + CH, 0, CH] + [2 * W1 + CH * n for n in range(6)] + [5 * W1 + CH * n for n in range(8)])

    def chunk_end(st, i, c):
        pattern = "".join(f + r for f, r in st.chunks[:c + 1])
        return st.half(i, pattern.rindex("w")) + 2

    def end(st):
        return st.half(st.rounds - 1, st.length - 1) + 2

    def wait_apart(eng, semaphore, value):
        if not isinstance(value, int):
            eng.wait_ge(ones_set, 4)
        eng.wait_ge(semaphore, value)

    def wide_bank(t):
        return ps[:, 4 * t:4 * t + 4, :].rearrange("p a n -> p (a n)")

    @block.sync
    def _(sync):
        def load(st, i, j, src):
            slot = st.slot(j)
            kind = st.pattern[j]
            used_w, used_a = st.freed("w", i, j) * 2, st.freed("a", i, j)
            if not isinstance(used_w, int) or used_w > 0:
                wait_apart(sync, lo_split, used_w)
            if not isinstance(used_a, int) or used_a > 0:
                wait_apart(sync, ada_added, used_a)
            size = 1
            for n in src.shape[1:]:
                size *= n
            dst = raw[slot][:, 0:size]
            if len(src.shape) == 3:
                dst = dst.rearrange("p (k n) -> p k n", k=src.shape[1])
            sync.dma_start(dst, src).then_inc(raw_full[slot], 16)

        def by_chunk(w, q, col, kts=4, width=CH):
            return w.rearrange("(k p) n -> p k n", p=P)[:, kts * q:kts * (q + 1), ds(col, width)]

        def by_row(w, k):
            return w.rearrange("(k p) n -> p k n", p=P)[:, ds(k, 1), :]

        w_ada = a["w_ada"][0].rearrange("(k p) n -> p k n", p=P)

        def ada(n, block_n):
            col = ADA_COLS[block_n] * D
            return w_ada[:, ds(n, 1), col:col + D]

        def load_bias(n, col):
            slot = n % 2 if isinstance(n, int) else None
            if n >= 2:
                sync.wait_ge(pair_empty, n - 1)
            sync.dma_start(bias_bc[slot][:], a["b_in"][0, col:col + CH].partition_broadcast(P)) \
                .then_inc(bias_full[slot], 16)

        st = ST["ada"]
        for i in range(8):
            for j in range(4):
                load(st, i, j, ada(4 * (i % 4) + j, i // 4))

        w_in = a["w_in"][0]
        chunk = 0
        kk = 0
        for name in ("in_vu", "in_h", "in_h2", "in_g"):
            st = ST[name]
            for i in range(st.rounds):
                w = 0
                for j, kind in enumerate(st.pattern):
                    if kind == "a":
                        load(st, i, j, ada(kk % 16, 2 + kk // 16))
                        kk += 1
                        continue
                    load(st, i, j, by_chunk(w_in, w % 4, IN_COLS[chunk]))
                    if w % 4 == 2:
                        load_bias(chunk, IN_COLS[chunk])
                    w += 1
                    chunk += w % 4 == 0
        st = ST["mix"]

        def mix_round(i):
            w = b = 0
            for j, kind in enumerate(st.pattern):
                if kind == "a":
                    load(st, i, j, ada(i * 4 + b, 4))
                    b += 1
                else:
                    src = a["w_branch_a"][0] if w < 2 else a["w_branch_b"][0]
                    load(st, i, j, by_chunk(src, w % 2, i * CH))
                    w += 1
        for i in range(4):
            mix_round(i)

        def rows(st, w):
            rounds(sync, st, lambda i: [load(st, i, j, by_row(w, i * st.length + j)) for j in range(st.length)])

        rows(ST["w_o"], a["w_o"][0])
        w_m1 = a["w_m1"][0]

        def m1(name, before, with_ada):
            st = ST[name]

            def body(i):
                w = b = 0
                for j, kind in enumerate(st.pattern):
                    if kind == "a":
                        load(st, i, j, ada(i * 4 + b, 5))
                        b += 1
                    else:
                        load(st, i, j, by_chunk(w_m1, w % 4, i * (2 * CH) + (before + w // 4) * CH))
                        w += 1
            if with_ada:
                for i in range(st.rounds):
                    body(i)
            else:
                rounds(sync, st, body)
        m1("m1a", 0, True)
        m1("m1b", 8, False)
        rows(ST["m2"], a["w_m2"][0])

        def chunks(st, w, col):
            per = KT // 4
            rounds(sync, st, lambda i: [load(st, i, j, by_chunk(w, j % per, i * (2 * CH) + (j // per) * CH + col))
                                        for j in range(st.length)])

        w_pool = a["pool_w_in_2"][0]
        chunks(ST["pool_u"], w_pool, 0)
        st = ST["pool_g"]
        w_group = a["pool_w_group_2"][0].rearrange("g (k p) n -> p g k n", p=P)

        def pool_round(i):
            j = 0
            for c in range(2):
                for q in range(2):
                    src = w_group[:, ds(i, 1), 4 * q:4 * q + 4, c * CH:(c + 1) * CH].rearrange("p g k n -> p (g k) n")
                    load(st, i, j, src)
                    j += 1
                for q in range(4):
                    load(st, i, j, by_chunk(w_pool, q, i * (2 * CH) + E_POOL + c * CH))
                    j += 1
        rounds(sync, st, pool_round)
        rows(ST["pool_out"], a["pool_w_out_2"][0])
        rows(ST["proj0"], a["ple_w_proj_2"][0])
        rows(ST["gate0"], a["ple_w_gate_2"][0])
        st = ST["mla_in"]
        w_mla = a["mla_w_in_2"][0]
        for i in range(3):
            for j in range(8):
                n = 2 * i + j // 4
                load(st, i, j, by_chunk(w_mla, j % 4, n * CH + (ROPE if n >= 2 else 0)))
        load(ST["k_pe"], 0, 0, by_chunk(w_mla, 0, 2 * CH, KT, ROPE))
        for n in range(6):
            load(ST["w_uq"], 0, n, by_chunk(a["mla_w_uq_2"][0], 0, n * CH))
        for n in range(8):
            load(ST["w_ukv"], 0, n, by_chunk(a["mla_w_ukv_2"][0], 0, n * CH))
        rows(ST["w_out"], a["mla_w_out_2"][0])
        rows(ST["proj1"], a["ple_w_proj_2"][1])
        rows(ST["gate1"], a["ple_w_gate_2"][1])
        sync.wait_ge(res_ready, RES_END)
        sync.dma_start(out[0].rearrange("(t p) n -> p t n", p=P), res[:]).then_inc(out_stored, 16)
        sync.wait_ge(out_stored, 16)

    @block.gpsimd
    def _(pool):
        steps = [0]

        def then(ins):
            steps[0] += 1
            ins.then_inc(g_step, 1)
            pool.wait_ge(g_step, steps[0])

        then(nc.gpsimd.memset(rows_b[:], 0.0))
        nc.gpsimd.memset(ones[:], 1.0).then_inc(ones_set, 1)
        nc.gpsimd.memset(ones_m[:], 1.0).then_inc(ones_set, 1)
        nc.gpsimd.memset(eps[:, 0:1], RMS_EPS).then_inc(ones_set, 1)
        nc.gpsimd.memset(eps[:, 1:2], LN_EPS).then_inc(ones_set, 1)
        dmas = 0

        def const(dst, src):
            nonlocal dmas
            dmas += 1
            pool.dma_start(dst, src).then_inc(consts, 16)

        const(ident[:], a["k_ident"])
        const(rows_b[48:64, :], a["c"].rearrange("a (k p) -> (a k) p", p=P))
        const(rows_a[0:64, :], a["b_m1"].rearrange("a (k p) -> (a k) p", p=P))
        const(rows_a[64:96, :], a["pre_norm_2"].rearrange("a (k p) -> (a k) p", p=P))
        const(rows_a[96:128, :], a["ple_norm_2"].rearrange("a (k p) -> (a k) p", p=P))
        const(rows_b[0:32, :], a["pool_scale_2"].rearrange("a (k p) -> (a k) p", p=P))
        const(rows_b[32:36, :], a["mla_q_norm_2"].rearrange("a (k p) -> (a k) p", p=P))
        const(rows_b[36:40, :], a["mla_kv_norm_2"].rearrange("a (k p) -> (a k) p", p=P))
        const(rows_b[40:48, :], a["sgu_b"][0])
        const(rows_b[64:80, :], a["ln1_g"].rearrange("a (k p) -> (a k) p", p=P))
        const(rows_b[80:96, :], a["ln1_b"].rearrange("a (k p) -> (a k) p", p=P))
        const(rows_b[96:97, 0:HID], a["hy_b1"])
        const(rows_b[97:98, 0:HID], a["hy_b2"])
        const(rows_b[98:99, 0:HID], a["hy_freq"])
        const(feats[0:EMB, :], a["k_feats"])
        const(w1[0:EMB, :], a["hy_w1"][0])
        const(w2[0:HID, :], a["hy_w2"][0])
        const(w3[0:HID, :], a["hy_w3"][0])
        const(window[:], a["k_window"].rearrange("(t p) n -> p t n", p=P))
        const(dft[:], a["k_dft"].rearrange("m (t p) n -> p m t n", p=P))
        const(sgu_raw[:], a["sgu_w"][0].rearrange("g q p -> q g p"))
        const(pos_i[0:2, :], a["positions_2"].rearrange("a (t p) -> (a t) p", p=P))
        const(freq[:], a["k_freq"][0].partition_broadcast(P))
        assert dmas == N_SETUP
        def start_acc(b):
            buf = acc[ADA_ACC[b]]
            nc.gpsimd.memset(buf[:], 0.0).then_inc(acc_zeroed, 1)
            pool.wait_ge(acc_zeroed, b + 1)
            col = ADA_COLS[b] * D
            pool.dma_start(buf[0:1, :], a["b_ada"][:, col:col + D]).then_inc(acc_ready[ADA_ACC[b]], 16)

        start_acc(0)
        start_acc(1)
        pool.dma_start(res[:], a["x"][0].rearrange("(t p) n -> p t n", p=P)).then_inc(x_loaded, 16)

        for it in range(4):
            pool.wait_ge(filt_win, it + 1)
            if it:
                pool.wait_ge(spec_mm, it)
            then(nc.gpsimd.tensor_tensor(h_sum[:], h_fwd[:], h_bwd[:], ALU.add))
            nc.gpsimd.tensor_tensor(h_bwd[:], h_fwd[:], h_bwd[:], ALU.subtract).then_inc(filt_sum, 1)
        pool.wait_ge(spec_mm, 4)
        pool.dma_start(sgu_g[:], a["sgu_ln_g"][0].partition_broadcast(P)).then_inc(sgu_consts, 16)
        pool.dma_start(sgu_b[:], a["sgu_ln_b"][0].partition_broadcast(P)).then_inc(sgu_consts, 16)
        then(nc.gpsimd.memset(zero[:], 0.0))
        for r in (0, S + 1):
            pool.dma_start(zh_dram[r].rearrange("(p n) -> p n", p=P), zero[:]).then_inc(zh_edges, 16)
        pool.wait_ge(mod_ready, 2)
        start_acc(2)
        for n in range(6):
            pool.wait_ge(pair_empty, 4 + n + 1)
            pool.dma_start(zh_dram[1:S + 1, n * CH:(n + 1) * CH].rearrange("(t p) n -> p t n", p=P),
                           zh_out[n % 2][:]).then_inc(zh_stored[n % 2], 16)
            if n == 1:
                start_acc(3)
        pool.wait_ge(zh_edges, 32)
        pool.wait_ge(zh_stored[0], 48)
        pool.wait_ge(zh_stored[1], 48)
        pool.wait_ge(fm_full, 6)
        loads = 0
        for b in range(2):
            if b:
                pool.wait_ge(hy_gated, 2)
                pool.wait_ge(fm_full, 7)
            for part_n in range(3):
                col = part_n * W1 + b * CH
                for j in range(3):
                    pool.dma_start(conv_in[:, j], zh_dram[j:j + S, col:col + CH].rearrange("(t p) n -> p t n", p=P)) \
                        .then_inc(conv_loaded, 16)
                    pool.dma_start(conv_w[:, j], a["hy_conv_w"][0, j, col:col + CH].partition_broadcast(P)) \
                        .then_inc(conv_loaded, 16)
                pool.dma_start(conv_w[:, 3], a["hy_conv_b"][0, col:col + CH].partition_broadcast(P)) \
                    .then_inc(conv_loaded, 16)
                loads += 7
                pool.wait_ge(conv_loaded, 16 * loads)
                w = [conv_w[:, j:j + 1, :].to_broadcast([P, 2, CH]) for j in range(4)]
                then(nc.gpsimd.tensor_tensor(hy[part_n][:], conv_in[:, 0], w[0], ALU.mult))
                then(nc.gpsimd.tensor_tensor(conv_in[:, 1], conv_in[:, 1], w[1], ALU.mult))
                then(nc.gpsimd.tensor_tensor(conv_in[:, 2], conv_in[:, 2], w[2], ALU.mult))
                then(nc.gpsimd.tensor_tensor(hy[part_n][:], hy[part_n][:], conv_in[:, 1], ALU.add))
                then(nc.gpsimd.tensor_tensor(hy[part_n][:], hy[part_n][:], conv_in[:, 2], ALU.add))
                ins = nc.gpsimd.tensor_tensor(hy[part_n][:], hy[part_n][:], w[3], ALU.add)
                ins.then_inc(conv_done, 1)
                pool.wait_ge(conv_done, 3 * b + part_n + 1)
            for o in range(2):
                if o:
                    pool.wait_ge(hy_gated, 2 * b + 1)
                pool.wait_ge(spec_stored, 64)
                pool.dma_start(spec[:].rearrange("p a n -> p (a n)"), spec_dram[o, b]).then_inc(spec_in, 16)
                pool.dma_start(skip[:], a["hy_skip"][0, o, b * CH:(b + 1) * CH].partition_broadcast(P)) \
                    .then_inc(skip_in, 16)
        pool.wait_ge(hy_gated, 4)
        pool.wait_ge(fm_full, 8)
        for i in range(4):
            if i >= 2:
                pool.wait_ge(mix_ready, i - 1)
            if i == 0:
                for g in range(2):
                    pool.wait_ge(gate_stored[g], 64)
            for g in range(2):
                pool.dma_start(gate_in[i % 2][:, g],
                               gate_dram[:, g * D + i * CH:g * D + (i + 1) * CH].rearrange("(t p) n -> p t n", p=P)) \
                    .then_inc(gate_loaded[i % 2], 16)
            if i == 0:
                start_acc(4)
        pool.dma_start(bias_o[:], a["b_o"][0].partition_broadcast(P)).then_inc(bias_o_in, 16)
        pool.wait_ge(half_used, ST["mix"].half(3, 7) )
        pool.dma_start(res[:], a["x"][0].rearrange("(t p) n -> p t n", p=P)).then_inc(x_again, 16)
        pool.wait_ge(fm_full, 12)
        pool.wait_ge(mix_ready, 4)
        pool.dma_start(ln_g[:], a["ln1_g"][0].partition_broadcast(P)).then_inc(ln_consts, 16)
        pool.dma_start(ln_b[:], a["ln1_b"][0].partition_broadcast(P)).then_inc(ln_consts, 16)

        def pre_add(bias, gate, ready):
            then(nc.gpsimd.tensor_tensor(bias[:], bias[:], gate[:], ALU.mult))
            for t in range(2):
                then(nc.gpsimd.tensor_scalar(res[:, t], res[:, t], ALPHA, 1.0, ALU.mult, ALU.mult))
                nc.gpsimd.tensor_tensor(res[:, t], res[:, t], bias[:], ALU.add).then_inc(pre_ready, 1)
        pool.wait_ge(mod_ready, 4)
        pool.wait_ge(bias_o_in, 16)
        pool.wait_ge(x_again, 16)
        pre_add(bias_o, acc[0], 0)
        pool.wait_ge(ln_consts, 32)
        pool.wait_ge(wide_empty, 2)
        start_acc(5)
        for t in range(2):
            pool.wait_ge(normed_ready, t + 1)
            then(nc.gpsimd.tensor_tensor(res[:, t], normed[:, t], ln_g[:], ALU.mult))
            nc.gpsimd.tensor_tensor(res[:, t], res[:, t], ln_b[:], ALU.add).then_inc(x1_ready, 1)
        pool.wait_ge(x1_ready, 2)
        pool.wait_ge(fm_lo, 16)
        pool.dma_start(bias_ff[:], a["b_m2"][0].partition_broadcast(P)).then_inc(bias_ff_in, 16)
        pool.wait_ge(g2_ready, 1)
        pool.wait_ge(bias_ff_in, 16)
        pre_add(bias_ff, acc[0], 2)
        pool.wait_ge(fm_lo, 20)
        pool.dma_start(ln2_g[:], a["ln2_g"][0].partition_broadcast(P)).then_inc(ln2_in, 16)
        pool.dma_start(ln2_b[:], a["ln2_b"][0].partition_broadcast(P)).then_inc(ln2_in, 16)
        pool.wait_ge(wide_empty, 4)
        pool.dma_start(pool_m[:], a["k_pool"].rearrange("g (t p) n -> p g t n", p=P)).then_inc(pool_in, 16)
        pool.wait_ge(normed_ready, 4)
        pool.dma_start(post_g[:], a["post_norm_2"][0].partition_broadcast(P)).then_inc(post_in[0], 16)
        pool.wait_ge(fm_full, 44)
        pool.dma_start(p_tm[:].rearrange("p (l t) n -> p l t n", t=2),
                       a["p_2"][:, 0].rearrange("l (t p) n -> p l t n", p=P)).then_inc(p_loaded, 16)
        pool.wait_ge(half_used, ST["w_ukv"].half(0, 7) + 2)
        then(nc.gpsimd.memset(mask[:], 0.0))
        for b in (0, 2):
            nc.gpsimd.affine_select(out=mask[:, b], in_=mask[:, b], compare_op=ALU.is_ge, fill=NEG, base=0,
                                    pattern=[[-1, P]], channel_multiplier=1).then_inc(mask_ready, 1)
        for g in range(2):
            pool.wait_ge(mla_gate_stored[g], 32)
        pool.dma_start(g_tm[:], gate_dram[:, 0:D].rearrange("(t p) n -> p t n", p=P)).then_inc(g_loaded, 16)
        pool.wait_ge(fm_full, 67)
        pool.dma_start(post_g1[:], a["post_norm_2"][1].partition_broadcast(P)).then_inc(post_in[1], 16)

    @block.tensor
    def _(pe):
        mm = nc.tensor.matmul

        def products(st, i, j, half, kt, hi, lo, banks, first, last):
            slot = st.half_slot(j, half)
            pe.wait_ge(lo_split, st.half(i, j) + half + 1)
            for c in range(2):
                wh, wl = (w[slot][:, c * CH:(c + 1) * CH] for w in (w_hi, w_lo))
                k = kt + c if isinstance(kt, int) else kt[0]
                start, stop = (first and c == 0, last and c == 1) if isinstance(kt, int) else (first, last)
                for t in range(2):
                    bank = banks(c, t)
                    xh, xl = (x[:, k, t * P:(t + 1) * P] for x in (hi, lo))
                    mm(bank, xh, wl, start=start, stop=False)
                    mm(bank, xh, wh, start=False, stop=False)
                    ins = mm(bank, xl, wh, start=False, stop=stop)
            ins.then_inc(half_used, 1)

        def pair(m):
            return lambda c, t: ps[:, 2 * m + t, :]

        def wide(half):
            return lambda c, t: ps[:, 4 * t + 2 * half + c, :]

        def chunk(st, i, c, m, m_static, hi, lo, kts=KT):
            j = sum(len(f + r) for f, r in st.chunks[:c])
            if not isinstance(m, int) or m >= 2:
                pe.wait_ge(pair_empty, m - 1)
            kt = 0
            for kind in "".join(st.chunks[c]):
                if kind == "w":
                    for half in range(2):
                        products(st, i, j, half, kt, hi, lo, pair(m_static % 2), kt == 0, kt + 2 == kts)
                        kt += 2
                j += 1

        def turn(g, src, q, slot=None):
            slot = g % 2 if slot is None else slot
            if not isinstance(g, int) or g >= 2:
                pe.wait_ge(fm_empty, g - 1)
            for k in range(4):
                for t in range(2):
                    ins = nc.tensor.transpose(fm_ps[slot][:, k, t * P:(t + 1) * P],
                                              src[:, t, (4 * q + k) * P:(4 * q + k + 1) * P], ident[:])
            ins.then_inc(fm_full, 1)

        def wide_products(st, s, hi, lo, kts, jit=False, kt0=0):
            def body(i):
                j = 0
                for c, kinds in enumerate(st.chunks):
                    n = i * len(st.chunks) + c
                    if s is not None:
                        pe.wait_ge(fm_lo, n + s + 1)
                    for q in range(len("".join(kinds))):
                        kt = 4 * (c % 2) + q if jit else kt0 + 4 * n + q
                        for half in range(2):
                            products(st, i, j, half, [kt], hi, lo, wide(half),
                                     isinstance(i, int) and i == 0 and j == 0,
                                     isinstance(i, int) and i == st.rounds - 1 and j == st.length - 1)
                        j += 1
            if jit:
                rounds(pe, st, body, last=True)
            else:
                for i in range(st.rounds):
                    body(i)

        def turn_heads(g, q):
            pe.wait_ge(fm_empty, g - 1)
            for k in range(4):
                for t in range(2):
                    ins = nc.tensor.transpose(fm_ps[g % 2][:, k, t * P:(t + 1) * P],
                                              q_tm[:, t, 4 * q + k, 0:VD], ident[:])
            ins.then_inc(fm_full, 1)

        pe.wait_ge(consts, 16 * N_SETUP)
        pe.wait_ge(pos_ready, 1)
        nc.tensor.transpose(ps[:, 7, 0:2], pos_f[0:2, :], ident[0:2, 0:2]).then_inc(pos_turned, 1)
        nc.tensor.transpose(ps[:, 4, 0:P], rows_a[:], ident[:])
        nc.tensor.transpose(ps[:, 4, P:2 * P], rows_b[:], ident[:])
        for g in range(8):
            ins = nc.tensor.transpose(ps[:, 5 + g // 4, (g % 4) * P:(g % 4 + 1) * P], sgu_raw[:, g], ident[:])
        ins.then_inc(setup_tr, 1)
        pe.wait_ge(vectors_out, 1)
        mm(ps[0:HID, 0, 0:S], w1[0:EMB, :], feats[0:EMB, :], start=True, stop=True).then_inc(hid_mm, 1)
        pe.wait_ge(hid_sin, 1)
        mm(ps[0:HID, 0, 0:S], w2[0:HID, :], hid_arg[0:HID, :], start=True, stop=True).then_inc(hid_mm, 1)
        pe.wait_ge(hid_sin, 2)
        pe.wait_ge(sgu_wT_out, 1)
        for it in range(4):
            o, c = it // 2, it % 2
            if it:
                pe.wait_ge(filt_win, it)
            for d in range(2):
                for t in range(2):
                    col = (2 * d + o) * W1 + c * CH
                    ins = mm(ps[:, 4 + 2 * d + t, :], hid_arg[0:HID, t * P:(t + 1) * P], w3[0:HID, col:col + CH],
                             start=True, stop=True)
            ins.then_inc(filt_mm, 1)
            pe.wait_ge(filt_sum, it + 1)
            if it:
                pe.wait_ge(spec_copied, it)
            for m, src in ((0, h_sum), (1, h_bwd)):
                for f in range(2):
                    for t in range(2):
                        ins = mm(ps[:, 2 * m + f, :], dft[:, m, t, f * P:(f + 1) * P], src[:, t, :],
                                 start=t == 0, stop=t == 1)
            ins.then_inc(spec_mm, 1)
        pe.wait_ge(x_loaded, 16)
        pe.wait_ge(filt_win, 4)
        turn(0, res, 0)
        turn(1, res, 1)

        def ada_sum(b, bank):
            pe.wait_ge(ada_added, 16 * (b + 1))
            for k in range(KT):
                ins = mm(ps[:, bank, k:k + 1], acc[ADA_ACC[b]][:, k * P:(k + 1) * P], ones[:, 0:1],
                         start=True, stop=True)
            ins.then_inc(ada_summed, 1)

        pe.wait_ge(spec_copied, 4)
        pe.wait_ge(ones_set, 2)
        ada_sum(0, 0)
        ada_sum(1, 1)
        turn(2, res, 2)
        turn(3, res, 3)

        def first_chunk(st, groups, kts=KT):
            for g in range(4):
                pe.wait_ge(fm_lo, groups + g + 1)
                for half in range(2):
                    products(st, 0, FIRST[st][g], half, 4 * g + 2 * half, x_hi, x_lo, pair(0),
                             g == 0 and half == 0, g == 3 and half == 1)

        FIRST = {st: [j for j, k in enumerate(st.pattern) if k == "w"][:4] for st in ST.values()}

        st = ST["in_vu"]
        pe.wait_ge(mod_ready, 2)
        first_chunk(st, 0)
        chunk(st, 0, 1, 1, 1, x_hi, x_lo)
        chunk(st, 1, 0, 2, 2, x_hi, x_lo)
        chunk(st, 1, 1, 3, 3, x_hi, x_lo)
        st = ST["in_h"]
        for i in range(2):
            for c in range(2):
                chunk(st, i, c, 4 + 2 * i + c, c, x_hi, x_lo)
        pe.wait_ge(vn_ready, 2)
        for t in range(2):
            for g in range(8):
                ins = mm(ps[:, 4 + 2 * t + g // 4, (g % 4) * P:(g % 4 + 1) * P], sgu_wT[:, g],
                         vu[:, 0, t, g * P:(g + 1) * P], start=True, stop=True)
            ins.then_inc(sgu_mm, 1)
        st = ST["in_h2"]
        for c in range(2):
            chunk(st, 0, c, 8 + c, c, x_hi, x_lo)
        pe.wait_ge(sgu_out, 1)
        turn(4, vu[:, 1], 0)
        turn(5, vu[:, 1], 1)
        pe.wait_ge(fm_empty, 5)
        ada_sum(2, 4)

        def forward(n):
            b, o = n // 2, n % 2
            if o == 0:
                pe.wait_ge(conv_done, 3 * b + 1)
            else:
                pe.wait_ge(hy_gated, n)
            if n == 0:
                pe.wait_ge(mod_ready, 3)
                pe.wait_ge(fm_empty, 6)
            else:
                pe.wait_ge(hy_gated, n)
            if n == 2:
                pe.wait_ge(fm_empty, 7)
            for m in range(2):
                for f in range(2):
                    for t in range(2):
                        ins = mm(ps[:, 4 + 2 * m + f, :], dft[:, m, t, f * P:(f + 1) * P], hy[0][:, t, :],
                                 start=t == 0, stop=t == 1)
            ins.then_inc(hy_f, 1)

        def inverse(n):
            pe.wait_ge(hy_prod, n + 1)
            for t in range(2):
                for m in range(2):
                    for f in range(2):
                        ins = mm(ps[:, 4 + t, :], dft[:, 2 + m, f, t * P:(t + 1) * P], prod[:, 2 * m + f, :],
                                 start=m + f == 0, stop=m + f == 2)
            ins.then_inc(hy_i, 1)

        st = ST["in_g"]
        for n in range(8):
            chunk(st, n // 2, n % 2, 10 + n, n, x_hi, x_lo)
            if n == 1:
                forward(0)
            if n == 2:
                inverse(0)
            if n == 3:
                forward(1)
            if n == 4:
                inverse(1)
                pe.wait_ge(hy_gated, 2)
                turn(6, hy[0], 0)
            if n == 6:
                forward(2)
            if n == 7:
                inverse(2)
        forward(3)
        inverse(3)
        pe.wait_ge(hy_gated, 4)
        turn(7, hy[0], 0)

        st = ST["mix"]
        pe.wait_ge(fm_lo, 8)

        def mix_round(i):
            chunk(st, i, 0, i * 2 + 18, 0, ya_hi, ya_lo, W1 // P)
            chunk(st, i, 1, i * 2 + 19, 1, yb_hi, yb_lo, W1 // P)
        for i in range(4):
            mix_round(i)
            if i:
                pe.wait_ge(mix_ready, i)
                turn(8 + i - 1, mixed[(i - 1) % 2], 0)
        pe.wait_ge(mix_ready, 4)
        turn(11, mixed[1], 0)
        pe.wait_ge(pair_empty, 26)
        pe.wait_ge(ada_added, 16 * 4)
        for n in range(4):
            ins = mm(ps[:, n, :], ones_m[:], acc[0][:, n * CH:(n + 1) * CH], start=True, stop=True)
        ins.then_inc(ada_summed, 1)
        pe.wait_ge(fm_empty, 11)
        ada_sum(4, 4)

        st = ST["w_o"]
        pe.wait_ge(mod_ready, 5)
        pe.wait_ge(fm_empty, 12)
        wide_products(st, 8, x_hi, x_lo, KT)

        pe.wait_ge(normed_ready, 2)
        for q in range(4):
            turn(12 + q, normed, q)
        st = ST["m1a"]

        def m1_round(st, before):
            def body(i):
                for c in range(2):
                    n = i * 2 + (before + c)
                    if isinstance(n, int) and n == 0:
                        first_chunk(st, 12)
                    else:
                        chunk(st, i, c, n + 26, c, x_hi, x_lo)
                    if not isinstance(n, int) or n > 0:
                        pe.wait_ge(pair_empty, n + 26)
                        turn(n + 15, ff_stage[1 - c], 0, slot=(1 + c) % 2)
            return body
        rounds(pe, st, m1_round(st, 0))
        rounds(pe, ST["m1b"], m1_round(ST["m1b"], 8))
        pe.wait_ge(pair_empty, 42)
        turn(31, ff_stage[1], 0)
        pe.wait_ge(ada_added, 96)
        for n in range(4):
            ins = mm(ps[:, n, :], ones_m[:], acc[0][:, n * CH:(n + 1) * CH], start=True, stop=True)
        ins.then_inc(ada_summed, 1)
        pe.wait_ge(g2_ready, 1)
        pe.wait_ge(fm_empty, 32)
        wide_products(ST["m2"], 16, x_hi, x_lo, FF // P, jit=True)

        pe.wait_ge(normed_ready, 4)
        for q in range(4):
            turn(32 + q, normed, q)
        st = ST["pool_u"]

        def pool_turn(g, n_group, c):
            pe.wait_ge(fm_empty, g - 1)
            slot = (g % 2) if isinstance(g, int) else c
            u = u_stage[c]
            for k in range(4):
                f = slice(k * P, (k + 1) * P)
                m = pool_m[:, ds(n_group, 1)].rearrange("p a t s -> p (a t) s")
                mm(fm_ps[slot][:, k, 0:P], u[:, 0, f], m[:, 0, 0:P], start=True, stop=True)
                mm(fm_ps[slot][:, k, P:S], u[:, 0, f], m[:, 0, P:S], start=True, stop=False)
                ins = mm(fm_ps[slot][:, k, P:S], u[:, 1, f], m[:, 1, P:S], start=False, stop=True)
            ins.then_inc(fm_full, 1)

        def pool_u_round(i):
            for c in range(2):
                n = i * 2 + c
                if isinstance(n, int) and n == 0:
                    first_chunk(st, 32)
                    pe.wait_ge(pool_in, 16)
                else:
                    chunk(st, i, c, n + 42, c, x_hi, x_lo)
                    pe.wait_ge(pair_empty, n + 42)
                    pool_turn(n + 35, i if c else i - 1, 1 - c)
        rounds(pe, st, pool_u_round)
        pe.wait_ge(pair_empty, 50)
        pool_turn(43, 3, 1)
        st_g = ST["pool_g"]

        def pool_g_round(i):
            pe.wait_ge(fm_lo, i * 2 + 38)
            for c in range(4):
                m = i * 4 + (50 + c)
                if c % 2 == 0:
                    chunk(st_g, i, c, m, c, g_hi, g_lo, 8)
                else:
                    chunk(st_g, i, c, m, c, x_hi, x_lo)
                    if c == 3 or not isinstance(i, int) or i > 0:
                        n = i * 2 + (0 if c == 3 else -1)
                        pe.wait_ge(product_ready, n + 1)
                        turn(n + 44, pool_stage[0 if c == 3 else 1], 0, slot=0 if c == 3 else 1)
        rounds(pe, st_g, pool_g_round)
        pe.wait_ge(product_ready, 8)
        turn(51, pool_stage[1], 0)
        pe.wait_ge(p_loaded, 16)
        pe.wait_ge(fm_empty, 51)
        for layer in range(2):
            for k in range(2):
                for t in range(2):
                    ins = nc.tensor.transpose(fm_ps[0][:, 2 * layer + k, t * P:(t + 1) * P],
                                              p_tm[:, 2 * layer + t, k * P:(k + 1) * P], ident[:])
        ins.then_inc(fm_full, 1)
        pe.wait_ge(pair_empty, 66)
        pe.wait_ge(fm_empty, 53)
        wide_products(ST["pool_out"], 45, x_hi, x_lo, E_POOL // P, jit=True)
        pe.wait_ge(wide_empty, 6)
        wide_products(ST["proj0"], None, p_hi, p_lo, 2)
        pe.wait_ge(wide_empty, 8)
        pe.wait_ge(normed_ready, 6)
        for q in range(4):
            turn(53 + q, normed, q)
        pe.wait_ge(fm_empty, 57)
        wide_products(ST["gate0"], 53, x_hi, x_lo, KT)

        pe.wait_ge(wide_empty, 10)
        pe.wait_ge(normed_ready, 8)
        for q in range(4):
            turn(57 + q, normed, q)
        st = ST["mla_in"]
        first_chunk(st, 57)
        for n in range(1, 6):
            chunk(st, n // 2, n % 2, 66 + n, n, x_hi, x_lo)
        st = ST["k_pe"]
        pe.wait_ge(pair_empty, 71)
        for half in range(2):
            pe.wait_ge(lo_split, st.half(0, 0) + half + 1)
            slot = st.half_slot(0, half)
            for q in range(8):
                wh, wl = (w[slot][:, q * ROPE:(q + 1) * ROPE] for w in (w_hi, w_lo))
                k = 8 * half + q
                for t in range(2):
                    xh, xl = (x[:, k, t * P:(t + 1) * P] for x in (x_hi, x_lo))
                    bank = ps[:, t, 0:ROPE]
                    mm(bank, xh, wl, start=k == 0, stop=False)
                    mm(bank, xh, wh, start=False, stop=False)
                    ins = mm(bank, xl, wh, start=False, stop=k == KT - 1)
            ins.then_inc(half_used, 1)
        pe.wait_ge(lat_ready, 2)
        for which in range(2):
            turn(61 + which, lat[:, :, which], 0)
        for name, which, kts, m in (("w_uq", 0, 6, 73), ("w_ukv", 1, 8, 79)):
            st = ST[name]
            pe.wait_ge(fm_lo, 62 + which)
            for n in range(kts):
                pe.wait_ge(pair_empty, m + n - 1)
                for half in range(2):
                    products(st, 0, n, half, 4 * which + 2 * half, x_hi, x_lo, pair((m + n) % 2),
                             half == 0, half == 1)

        def head_turn(h):
            if h >= 2:
                pe.wait_ge(qk_out, h - 1)
            for t in range(2):
                nc.tensor.transpose(ps[:, h % 2, t * P:(t + 1) * P], q_tm[:, t, h, 0:NOPE], ident[:])
                nc.tensor.transpose(ps[:, h % 2, (2 + t) * P:(3 + t) * P], kv_tm[:, t, h, 0:NOPE], ident[:])
            if h >= 1:
                pe.wait_ge(qpe_out, h)
            for t in range(2):
                ins = nc.tensor.transpose(ps[0:ROPE, 2, t * P:(t + 1) * P], q_tm[:, t, h, NOPE:QK],
                                          ident[:])
            ins.then_inc(qk_turned, 1)

        def head_score(h):
            pe.wait_ge(qk_out, h + 1)
            pe.wait_ge(qpe_out, h + 1)
            if h >= 2:
                pe.wait_ge(score_ready, h - 1)
            qk, qp = qk_fm[h % 2], q_peT[h % 2]
            for t in range(2):
                keys = slice(0, (t + 1) * P)
                bank = ps[:, 3 + h % 2, t * P:(2 * t + 1) * P]
                mm(bank, qk[:, 0, t * P:(t + 1) * P], qk[:, 1, keys], start=True, stop=False)
                ins = mm(bank, qp[0:ROPE, t * P:(t + 1) * P], k_peT[0:ROPE, keys], start=False, stop=True)
            ins.then_inc(scored, 1)

        def head_prob(h):
            pe.wait_ge(prob_ready, 2 * (h + 1))
            if h >= 2:
                pe.wait_ge(probT_out, h - 1)
            for b in range(3):
                ins = nc.tensor.transpose(ps[:, 5 + h % 2, b * P:(b + 1) * P], prob[h % 2][:, b], ident[:])
            ins.then_inc(prob_turned, 1)

        def head_value(h):
            pe.wait_ge(probT_out, h + 1)
            if h >= 1:
                pe.wait_ge(o_ready, h)
            v = kv_tm[:, :, h, NOPE:NOPE + VD]
            pt = probT[h % 2]
            mm(ps[:, 7, 0:P], pt[:, 0], v[:, 0], start=True, stop=True)
            mm(ps[:, 7, P:2 * P], pt[:, 1], v[:, 0], start=True, stop=False)
            mm(ps[:, 7, P:2 * P], pt[:, 2], v[:, 1], start=False, stop=True).then_inc(o_mm, 1)

        pe.wait_ge(pair_empty, 87)
        pe.wait_ge(fm_empty, 63)
        for t in range(2):
            ins = nc.tensor.transpose(ps[0:ROPE, 7, t * P:(t + 1) * P], k_pe[:, t, :], ident[:])
        ins.then_inc(k_peT_ready, 1)
        for step in range(HEADS + 3):
            if step < HEADS:
                head_turn(step)
            if step == 0:
                pe.wait_ge(k_peT_out, 1)
            if 0 <= step - 1 < HEADS:
                head_score(step - 1)
            if 0 <= step - 2 < HEADS:
                head_prob(step - 2)
            if 0 <= step - 3 < HEADS:
                head_value(step - 3)
        pe.wait_ge(o_ready, HEADS)
        for q in range(4):
            turn_heads(63 + q, q)
        pe.wait_ge(fm_empty, 67)
        wide_products(ST["w_out"], 63, x_hi, x_lo, KT)
        pe.wait_ge(wide_empty, 12)
        wide_products(ST["proj1"], None, p_hi, p_lo, 2, kt0=2)
        pe.wait_ge(wide_empty, 14)
        pe.wait_ge(normed_ready, 10)
        for q in range(4):
            turn(67 + q, normed, q)
        pe.wait_ge(fm_empty, 71)
        wide_products(ST["gate1"], 67, x_hi, x_lo, KT)

    @block.scalar
    def _(act):
        steps = [0]

        def then(ins):
            steps[0] += 1
            ins.then_inc(s_step, 1)
            act.wait_ge(s_step, steps[0])

        def round_unit(st, i, j):
            for half in range(2):
                h = st.half(i, j) + half
                if half == 0:
                    act.wait_ge(raw_full[st.slot(j)], st.landed(i, j))
                if not isinstance(h, int) or h >= SLOTS:
                    act.wait_ge(half_used, h - (SLOTS - 1))
                n = st.size // 2
                nc.scalar.copy(w_hi[st.half_slot(j, half)][:, 0:n], raw[st.slot(j)][:, half * n:(half + 1) * n]) \
                    .then_inc(hi_split, 1)

        def run(st, i, hook):
            j = 0
            for c, (front, rest) in enumerate(st.chunks):
                for n, kind in enumerate(front + rest):
                    if n == len(front):
                        hook(i, c)
                    if kind == "w":
                        round_unit(st, i, j)
                    j += 1
                if not rest:
                    hook(i, c)

        def no(i, c):
            pass

        def group(g, s, hi, read):
            y = y_fm[s % 2]
            act.wait_ge(fm_full, g + 1)
            if s >= 2:
                act.wait_ge(fm_lo, s - 1)
            ps_g = fm_ps[g % 2]
            if read is None:
                ins = nc.scalar.copy(y[:], ps_g)
            else:
                for k in range(4):
                    ins = read(k, y[:, k], ps_g[:, k])
            ins.then_inc(fm_empty, 1)
            act.wait_ge(fm_empty, g + 1)
            nc.scalar.copy(hi, y[:]).then_inc(fm_hi, 1)

        def affine(scale, bias, q):
            def read(k, o, i):
                n = 4 * q + k
                if bias is None:
                    return nc.scalar.activation(o, i, ACT.Copy, scale=scale[:, n:n + 1])
                return nc.scalar.activation(o, i, ACT.Identity, scale=scale[:, n:n + 1], bias=bias[:, n:n + 1])
            return read

        act.wait_ge(setup_tr, 1)
        nc.scalar.copy(sgu_wT[:].rearrange("p g q -> p (g q)"),
                       ps[:, 5:7, :].rearrange("p a n -> p (a n)")).then_inc(sgu_wT_out, 1)
        act.wait_ge(vectors_out, 1)
        nc.scalar.activation(sig_c[:], fm_b[:, COL["c"]:COL["c"] + KT], ACT.Sigmoid).then_inc(c_sig, 1)
        for layer in range(2):
            act.wait_ge(hid_red, layer + 1)
            nc.scalar.activation(hid_arg[0:HID, :], hid_arg[0:HID, :], ACT.Sin).then_inc(hid_sin, 1)
        act.wait_ge(angles, 1)
        for table in (rope_cos, rope_sin):
            nc.scalar.activation(table[:], table[:], ACT.Sin).then_inc(sines, 1)
        for it in range(4):
            act.wait_ge(spec_mm, it + 1)
            if it:
                act.wait_ge(spec_stored, 16 * it)
            nc.scalar.copy(spec_out[:].rearrange("p a n -> p (a n)"), ps[:, 0:4, :].rearrange("p a n -> p (a n)")) \
                .then_inc(spec_copied, 1)
            act.wait_ge(spec_copied, it + 1)
            act.dma_start(spec_dram[it // 2, it % 2], spec_out[:].rearrange("p a n -> p (a n)")) \
                .then_inc(spec_stored, 16)
        act.wait_ge(mod_ready, 2)
        for q in range(4):
            group(q, q, x_hi[:, 4 * q:4 * q + 4, :], affine(mod[:, 1], mod[:, 0], q))

        def gelu(n):
            act.wait_ge(pair_empty, n + 1)
            part = vu[:, n // 2, :, (n % 2) * CH:(n % 2 + 1) * CH]
            nc.scalar.activation(part, part, ACT.Gelu).then_inc(gelu_done, 1)

        st = ST["in_vu"]
        for i in range(2):
            run(st, i, lambda i, c: gelu(2 * i + c - 1) if i or c else None)

        def sgu_std(i, c):
            n = 2 * i + c
            if n == 0:
                gelu(3)
            if n == 2:
                act.wait_ge(var_ready, 1)
                nc.scalar.activation(rstd[:, 0], rstd[:, 0], ACT.Sqrt).then_inc(std_ready, 1)
        st = ST["in_h"]
        for i in range(2):
            run(st, i, sgu_std)
        run(ST["in_h2"], 0, no)

        def gate(n):
            act.wait_ge(pair_empty, 10 + n + 1)
            nc.scalar.activation(gate_out[n % 2][:], gate_out[n % 2][:], ACT.Sigmoid).then_inc(gate_sig, 1)
            act.wait_ge(gate_sig, n + 1)
            act.dma_start(gate_dram[:, n * CH:(n + 1) * CH].rearrange("(t p) n -> p t n", p=P), gate_out[n % 2][:]) \
                .then_inc(gate_stored[n % 2], 16)

        def in_g(i, c):
            n = 2 * i + c
            if n == 0:
                for q in range(2):
                    group(4 + q, 4 + q, ya_hi[:, 4 * q:4 * q + 4, :], None)
            else:
                gate(n - 1)
            if n == 5:
                group(6, 6, yb_hi[:, 0:4, :], None)
        st = ST["in_g"]
        for i in range(4):
            run(st, i, in_g)
        gate(7)
        group(7, 7, yb_hi[:, 4:8, :], None)

        st = ST["mix"]
        for i in range(4):
            run(st, i, lambda i, c: group(8 + i - 2, 8 + i - 2, x_hi[:, 4 * (i - 2):4 * (i - 1), :], None)
                if c == 0 and i >= 2 else None)
        st = ST["w_o"]
        run(st, 0, lambda i, c: [group(g, g, x_hi[:, 4 * (g - 8):4 * (g - 7), :], None) for g in (10, 11)]
            if c == 0 else None)
        run(st, 1, no)

        sums = [0]

        def root(t, src):
            sums[0] += 1
            nc.scalar.activation(normed[:, t], src, ACT.Square, accum_out=ss[:, t, 0:1]).then_inc(squares, 1)
            act.wait_ge(squares, sums[0])
            nc.scalar.activation(ss[:, t, 1:2], ss[:, t, 0:1], ACT.Sqrt, scale=1.0 / D, bias=eps[:, 0:1]) \
                .then_inc(roots, 1)

        def root_of_var(n):
            for t in range(2):
                act.wait_ge(var_ready, n + t + 1)
                nc.scalar.activation(rstd[:, 0, t:t + 1], mv[:, t, 1:2], ACT.Sqrt, bias=eps[:, 1:2]) \
                    .then_inc(std_ready, 1)

        def root_of_res(n):
            for t in range(2):
                act.wait_ge(res_ready, n + t + 1)
                root(t, res[:, t])

        def four_groups(g, scale, bias):
            for q in range(4):
                group(g + q, g + q, x_hi[:, 4 * q:4 * q + 4, :], affine(scale, bias, q))

        def relu2(n, c):
            wait_apart(act, fm_full, n + 17)
            for k in range(4):
                ins = nc.scalar.activation(ff[:, ds(n * 4 + k, 1)], fm_ps[c][:, k:k + 1], ACT.Relu,
                                           bias=fm_a[:, ds(n * 4 + k, 1)])
            ins.then_inc(fm_empty, 1)
            wait_apart(act, fm_empty, n + 17)
            nc.scalar.activation(ff[:, ds(n * 4, 4)], ff[:, ds(n * 4, 4)], ACT.Square).then_inc(ff_ready, 1)

        def m1_hook(base):
            def hook(i, c):
                if base == 0 and isinstance(i, int) and i == 0:
                    if c == 0:
                        root_of_var(1)
                        four_groups(12, mod[:, 4], mod[:, 5])
                        act.wait_ge(x1_ready, 2)
                    return
                relu2(i * 2 + (base + c - 2), c)
            return hook
        rounds(act, ST["m1a"], lambda i: run(ST["m1a"], i, m1_hook(0)))
        rounds(act, ST["m1b"], lambda i: run(ST["m1b"], i, m1_hook(8)))

        def jit(src, n, c):
            nc.scalar.copy(x_hi[:, 4 * c:4 * c + 4], src[:, ds(n * 4, 4)]).then_inc(fm_hi, 1)

        def m2_hook(i, c):
            if isinstance(i, int) and i == 0 and c == 0:
                relu2(14, 0)
                jit(ff, 0, 0)
                relu2(15, 1)
            if not (isinstance(i, int) and i == 7 and c == 1):
                wait_apart(act, ff_ready, i * 2 + (c + 2))
                jit(ff, i * 2 + (c + 1), 1 - c)
        rounds(act, ST["m2"], lambda i: run(ST["m2"], i, m2_hook), last=True)

        def pool_copy(n, c):
            wait_apart(act, fm_full, n + 37)
            nc.scalar.copy(pooled[:, ds(n * 4, 4)], fm_ps[c]).then_inc(fm_empty, 1)

        def pool_u_hook(i, c):
            if isinstance(i, int) and i == 0:
                if c == 0:
                    root_of_var(3)
                    root_of_res(0)
                    four_groups(32, fm_a[:, 64:80], None)
                return
            pool_copy(i * 2 + (c - 2), c)
        rounds(act, ST["pool_u"], lambda i: run(ST["pool_u"], i, pool_u_hook))

        def jit_group(i):
            for c in range(2):
                nc.scalar.copy(g_hi[:, 4 * c:4 * c + 4], pooled[:, ds(i * 8 + 4 * c, 4)]).then_inc(fm_hi, 1)

        def pool_sigmoid(i, c):
            n = i * 2 + c
            act.wait_ge(half_used, chunk_end(ST["pool_g"], i, 2 * c + 1))
            if not isinstance(n, int) or n >= 1:
                act.wait_ge(product_ready, n)
            nc.scalar.activation(pool_gate[:], ps[:, 2:4, :], ACT.Sigmoid).then_inc(silu_ready, 1)

        def pool_scaled(i, c):
            n = i * 2 + c
            act.wait_ge(fm_full, n + 45)
            wait_apart(act, fm_lo, i * 2 + 38)
            for k in range(4):
                ins = nc.scalar.activation(pooled[:, ds(n * 4 + k, 1)], fm_ps[c][:, k:k + 1], ACT.Copy,
                                           scale=fm_b[:, ds(n * 4 + (COL["pool_scale"] + k), 1)])
            ins.then_inc(fm_empty, 1)

        def pool_g_hook(i, c):
            first = isinstance(i, int) and i == 0
            if c == 0:
                if first:
                    pool_copy(6, 0)
                    jit_group(0)
                    pool_copy(7, 1)
                else:
                    pool_sigmoid(i - 1, 1)
                    pool_scaled(i - 1, 0)
            if c == 2:
                pool_sigmoid(i, 0)
                if not first:
                    pool_scaled(i - 1, 1)
            if c == 3 and not (isinstance(i, int) and i == 3):
                wait_apart(act, half_used, chunk_end(ST["pool_g"], i, 2))
                jit_group(i + 1)
        rounds(act, ST["pool_g"], lambda i: run(ST["pool_g"], i, pool_g_hook), last=True)

        def pool_out_hook(i, c):
            if isinstance(i, int) and i == 0 and c == 0:
                pool_sigmoid(3, 1)
                pool_scaled(3, 0)
                pool_scaled(3, 1)
                group(52, 44, p_hi[:], None)
                jit(pooled, 0, 0)
            if not (isinstance(i, int) and i == 3 and c == 1):
                jit(pooled, i * 2 + (c + 1), 1 - c)
        rounds(act, ST["pool_out"], lambda i: run(ST["pool_out"], i, pool_out_hook), last=True)

        def mixer_out(mixer, n):
            act.wait_ge(half_used, end(mixer))
            for t in range(2):
                root(t, wide_bank(t))
            root_of_res(n)

        def gate_sigmoid(st, n):
            act.wait_ge(half_used, end(st))
            for t in range(2):
                nc.scalar.activation(tmp[:, t], wide_bank(t), ACT.Sigmoid).then_inc(gate_read, 1)

        run(ST["proj0"], 0, lambda i, c: mixer_out(ST["pool_out"], 2))
        for i in range(2):
            run(ST["gate0"], i, lambda i, c: four_groups(53, fm_a[:, 96:112], None) if i + c == 0 else None)

        def mla_sigmoid(n):
            act.wait_ge(half_used, chunk_end(ST["mla_in"], n // 2, n % 2))
            if n >= 4:
                act.wait_ge(pair_empty, 66 + n - 1)
            nc.scalar.activation(mla_sig[n % 2][:], ps[:, 2 * (n % 2):2 * (n % 2) + 2, :], ACT.Sigmoid) \
                .then_inc(mla_silu, 1)

        def mla_gate_store(n):
            act.wait_ge(pair_empty, 66 + n + 1)
            act.dma_start(gate_dram[:, (n - 2) * CH:(n - 1) * CH].rearrange("(t p) n -> p t n", p=P),
                          mla_gate_out[n % 2][:]).then_inc(mla_gate_stored[n % 2], 16)

        def mla_in_hook(i, c):
            n = 2 * i + c
            if n == 0:
                gate_sigmoid(ST["gate0"], 0)
                root_of_res(4)
                four_groups(57, fm_a[:, 80:96], None)
            if n == 3:
                act.wait_ge(pair_empty, 68)
                for w in range(4):
                    ins = nc.scalar.activation(lat_junk[:, w], lat[:, w % 2, w // 2], ACT.Square,
                                               accum_out=lat_ss[:, 0, w:w + 1])
                then(ins)
                nc.scalar.activation(lat_ss[:, 1], lat_ss[:, 0], ACT.Sqrt, scale=1.0 / CH, bias=eps[:, 0:1]) \
                    .then_inc(lat_sq, 1)
            if n >= 3:
                mla_sigmoid(n - 1)
            if n >= 4:
                mla_gate_store(n - 2)
        for i in range(3):
            run(ST["mla_in"], i, mla_in_hook)

        def k_pe_hook(i, c):
            mla_sigmoid(5)
            mla_gate_store(4)
            mla_gate_store(5)
        run(ST["k_pe"], 0, k_pe_hook)

        def w_uq_hook(i, c):
            if c == 0:
                group(61, 61, x_hi[:, 0:4, :], affine(fm_b[:, COL["q_norm"]:COL["q_norm"] + 4], None, 0))
                group(62, 62, x_hi[:, 4:8, :], affine(fm_b[:, COL["kv_norm"]:COL["kv_norm"] + 4], None, 0))
        run(ST["w_uq"], 0, w_uq_hook)
        run(ST["w_ukv"], 0, no)

        def head_turned(h):
            act.wait_ge(qk_turned, h + 1)
            if h >= 2:
                act.wait_ge(scored, h - 1)
            nc.scalar.copy(qk_fm[h % 2][:].rearrange("p a s -> p (a s)"), ps[:, h % 2, :]).then_inc(qk_out, 1)

        def head_exp(h):
            act.wait_ge(score_ready, h + 1)
            if h >= 2:
                act.wait_ge(prob_turned, h - 1)
            for t in range(2):
                blocks = slice(t, 2 * t + 1)
                nc.scalar.activation(prob[h % 2][:, blocks], score[h % 2][:, blocks], ACT.Exp,
                                     bias=sm_max[:, h % 4, t:t + 1], accum_out=sm_sum[:, h % 4, t:t + 1]) \
                    .then_inc(prob_ready, 1)

        def head_probT(h):
            act.wait_ge(prob_turned, h + 1)
            if h >= 2:
                act.wait_ge(o_mm, h - 1)
            nc.scalar.copy(probT[h % 2][:].rearrange("p b k -> p (b k)"), ps[:, 5 + h % 2, 0:3 * P]) \
                .then_inc(probT_out, 1)

        def w_out_hook(i, c):
            if i or c:
                return
            act.wait_ge(pair_empty, 87)
            for step in range(HEADS + 2):
                if step < HEADS:
                    head_turned(step)
                if 0 <= step - 1 < HEADS:
                    head_exp(step - 1)
                if 0 <= step - 2 < HEADS:
                    head_probT(step - 2)
            for q in range(4):
                group(63 + q, 63 + q, x_hi[:, 4 * q:4 * q + 4, :], None)
        for i in range(2):
            run(ST["w_out"], i, w_out_hook)
        run(ST["proj1"], 0, lambda i, c: mixer_out(ST["w_out"], 6))
        for i in range(2):
            run(ST["gate1"], i, lambda i, c: four_groups(67, fm_a[:, 112:128], None) if i + c == 0 else None)
        gate_sigmoid(ST["gate1"], 0)

    @block.vector
    def _(dve):
        steps = [0]
        tt, tsc, stt = nc.vector.tensor_tensor, nc.vector.tensor_scalar, nc.vector.scalar_tensor_tensor

        def then(ins):
            steps[0] += 1
            ins.then_inc(v_step, 1)
            dve.wait_ge(v_step, steps[0])

        def rest_unit(st, i, j):
            for half in range(2):
                dve.wait_ge(hi_split, st.half(i, j) + half + 1)
                n = st.size // 2
                slot = st.half_slot(j, half)
                tt(w_lo[slot][:, 0:n], raw[st.slot(j)][:, half * n:(half + 1) * n],
                   w_hi[slot][:, 0:n].bitcast(F32), ALU.subtract).then_inc(lo_split, 1)

        def add_ada(st, i, j, block_n, kk):
            dve.wait_ge(raw_full[st.slot(j)], st.landed(i, j))
            done = st.before("a", i, j)
            if isinstance(done, int) and done % 16 == 0:
                dve.wait_ge(acc_ready[ADA_ACC[block_n]], 16 * ADA_NTH[block_n])
            if not isinstance(done, int) or done > 0:
                dve.wait_ge(ada_added, done)
            buf = acc[ADA_ACC[block_n]]
            stt(out=buf[:], in0=raw[st.slot(j)][:], scalar=cond[:, ds(kk, 1)], in1=buf[:], op0=ALU.mult,
                op1=ALU.add).then_inc(ada_added, 1)

        def run(st, i, hook, ada=None):
            j = n_a = 0
            for c, (front, rest) in enumerate(st.chunks):
                for n, kind in enumerate(front + rest):
                    if n == len(front):
                        hook(i, c)
                    if kind == "w":
                        rest_unit(st, i, j)
                    else:
                        block_n, kk = ada(i, n_a)
                        add_ada(st, i, j, block_n, kk)
                        n_a += 1
                    j += 1
                if not rest:
                    hook(i, c)

        def no(i, c):
            pass

        def group_rest(s, hi, lo):
            dve.wait_ge(fm_hi, s + 1)
            tt(lo, y_fm[s % 2][:], hi.bitcast(F32), ALU.subtract).then_inc(fm_lo, 1)

        dve.wait_ge(consts, 16 * N_SETUP)
        nc.vector.tensor_copy(pos_f[0:2, :], pos_i[0:2, :]).then_inc(pos_ready, 1)
        dve.wait_ge(setup_tr, 1)
        then(nc.vector.tensor_copy(pos[:], ps[:, 7, 0:2]))
        nc.vector.tensor_copy(fm_a[:], ps[:, 4, 0:P])
        nc.vector.tensor_copy(fm_b[:], ps[:, 4, P:2 * P]).then_inc(vectors_out, 1)
        dve.wait_ge(vectors_out, 1)
        dve.wait_ge(c_sig, 1)
        then(tt(cond[:], sig_c[:], fm_b[:, COL["c"]:COL["c"] + KT], ALU.mult))

        def sine_arg(buf, n, k):
            then(tsc(n, buf, INV_2PI, MAGIC, ALU.mult, ALU.add))
            then(tsc(n, n, MAGIC, None, ALU.subtract))
            for c in TWO_PI:
                then(stt(out=buf, in0=n, scalar=-c, in1=buf, op0=ALU.mult, op1=ALU.add))
            return tsc(buf, buf, SIN_MAX, -SIN_MAX, ALU.min, ALU.max)

        def hidden(layer):
            dve.wait_ge(hid_mm, layer + 1)
            bias = fm_b[0:HID, COL["b1"] + layer:COL["b1"] + layer + 1]
            freq = fm_b[0:HID, COL["freq"]:COL["freq"] + 1]
            then(tsc(hid_arg[0:HID, :], ps[0:HID, 0, 0:S], bias, freq, ALU.add, ALU.mult))
            sine_arg(hid_arg[0:HID, :], hid_n[0:HID, :], layer).then_inc(hid_red, 1)

        def filters(it):
            c = it % 2
            dve.wait_ge(filt_mm, it + 1)
            if it:
                dve.wait_ge(spec_mm, it)
            win = window[:, :, c * CH:(c + 1) * CH]
            tt(h_fwd[:], ps[:, 4:6, :], win, ALU.mult)
            tt(h_bwd[:], ps[:, 6:8, :], win, ALU.mult).then_inc(filt_win, 1)

        hidden(0)
        for t in range(2):
            then(tsc(rope_sin[:, t], freq[:], pos[:, t:t + 1], None, ALU.mult))
        then(sine_arg(rope_sin[:], ang_n[:], 0))
        then(tsc(rope_cos[:], rope_sin[:], math.pi / 2, None, ALU.add))
        sine_arg(rope_cos[:], ang_n[:], 0).then_inc(angles, 1)
        st = ST["ada"]
        for i in range(8):
            for j in range(4):
                add_ada(st, i, j, i // 4, 4 * (i % 4) + j)
            if i == 0:
                hidden(1)
            if 1 <= i <= 4:
                filters(i - 1)
        dve.wait_ge(ada_summed, 1)
        nc.vector.tensor_copy(mod[:, 0], ps[:, 0, 0:KT]).then_inc(mod_ready, 1)
        dve.wait_ge(ada_summed, 2)
        tsc(mod[:, 1], ps[:, 1, 0:KT], 1.0, None, ALU.add).then_inc(mod_ready, 1)
        for q in range(4):
            group_rest(q, x_hi[:, 4 * q:4 * q + 4, :], x_lo[:, 4 * q:4 * q + 4, :])

        def out_of_pair(st, i, c, m, out_):
            dve.wait_ge(half_used, chunk_end(st, i, c))
            dve.wait_ge(bias_full[m % 2], 16 * (m // 2 + 1))
            bias = bias_bc[m % 2][:].unsqueeze(1).to_broadcast([P, 2, CH])
            tt(out_, ps[:, 2 * (m % 2):2 * (m % 2) + 2, :], bias, ALU.add).then_inc(pair_empty, 1)

        def vu_out(m):
            out_of_pair(ST["in_vu"], m // 2, m % 2, m, vu[:, m // 2, :, (m % 2) * CH:(m % 2 + 1) * CH])

        def zh_out_(n):
            st, i = (ST["in_h"], n // 2) if n < 4 else (ST["in_h2"], 0)
            if n >= 2:
                dve.wait_ge(zh_stored[n % 2], 16 * (n // 2))
            out_of_pair(st, i, n % 2, 4 + n, zh_out[n % 2][:])

        def gate_out_(n):
            if n >= 2:
                dve.wait_ge(gate_stored[n % 2], 16 * (n // 2))
            out_of_pair(ST["in_g"], n // 2, n % 2, 10 + n, gate_out[n % 2][:])

        st = ST["in_vu"]
        for i in range(2):
            run(st, i, lambda i, c: vu_out(2 * i + c - 1) if i or c else None,
                lambda i, n: (2, 4 * i + n))

        def moments(src, width, t):
            for n in range(width // CH):
                ins = nc.vector.bn_stats(stats[:, t, n, :], src[:, t, n * CH:(n + 1) * CH])
            then(ins)
            then(nc.vector.bn_aggr(mv[:, t], stats[:, t, 0:width // CH, :].rearrange("p a b -> p (a b)")))

        def sgu_norm():
            dve.wait_ge(gelu_done, 2)
            for t in range(2):
                moments(vu[:, 0], W1, t)
            tsc(rstd[:, 0], mv[:, :, 1], LN_EPS, None, ALU.add).then_inc(var_ready, 1)

        def sgu_norm2():
            dve.wait_ge(std_ready, 1)
            then(nc.vector.reciprocal(rstd[:, 1], rstd[:, 0]))
            dve.wait_ge(sgu_consts, 32)
            for t in range(2):
                v = vu[:, 0, t]
                then(tsc(v, v, mv[:, t, 0:1], rstd[:, 1, t:t + 1], ALU.subtract, ALU.mult))
                then(tt(v, v, sgu_g[:], ALU.mult))
                tt(v, v, sgu_b[:], ALU.add).then_inc(vn_ready, 1)

        def in_h(i, c):
            n = 2 * i + c
            if n == 0:
                vu_out(3)
            else:
                zh_out_(n - 1)
            if n == 1:
                sgu_norm()
            if n == 3:
                sgu_norm2()
        st = ST["in_h"]
        for i in range(2):
            run(st, i, in_h, lambda i, n: (2, 8 + 4 * i + n))

        def sgu_gate():
            dve.wait_ge(gelu_done, 4)
            for t in range(2):
                dve.wait_ge(sgu_mm, t + 1)
                for g in range(8):
                    u = vu[:, 1, t, g * P:(g + 1) * P]
                    ins = stt(out=u, in0=ps[:, 4 + 2 * t + g // 4, (g % 4) * P:(g % 4 + 1) * P],
                              scalar=fm_b[:, COL["sgu_b"] + g:COL["sgu_b"] + g + 1], in1=u, op0=ALU.add, op1=ALU.mult)
            ins.then_inc(sgu_out, 1)

        def in_h2(i, c):
            zh_out_(3 + c)
            if c == 0:
                sgu_gate()
        run(ST["in_h2"], 0, in_h2)

        def multiply(n):
            dve.wait_ge(hy_f, n + 1)
            dve.wait_ge(spec_in, 16 * (n + 1))
            re, im = ps[:, 4:6, :], ps[:, 6:8, :]
            k_re, k_im, o_re, o_im = spec[:, 0:2], spec[:, 2:4], prod[:, 0:2], prod[:, 2:4]
            tt(o_re, re, k_re, ALU.mult)
            then(tt(part[:], im, k_im, ALU.mult))
            then(tt(o_re, o_re, part[:], ALU.subtract))
            tt(o_im, re, k_im, ALU.mult)
            then(tt(part[:], im, k_re, ALU.mult))
            tt(o_im, o_im, part[:], ALU.add).then_inc(hy_prod, 1)

        def regate(n):
            o = n % 2
            dve.wait_ge(hy_i, n + 1)
            dve.wait_ge(skip_in, 16 * (n + 1))
            dve.wait_ge(conv_done, 3 * (n // 2) + 2 + o)
            y = hy[0][:]
            then(tt(y, y, skip[:].unsqueeze(1).to_broadcast([P, 2, CH]), ALU.mult))
            then(tt(y, y, ps[:, 4:6, :], ALU.add))
            tt(y, y, hy[1 + o][:], ALU.mult).then_inc(hy_gated, 1)

        def in_g(i, c):
            n = 2 * i + c
            if n == 0:
                zh_out_(5)
                for q in range(2):
                    group_rest(4 + q, ya_hi[:, 4 * q:4 * q + 4, :], ya_lo[:, 4 * q:4 * q + 4, :])
                dve.wait_ge(ada_summed, 3)
                nc.vector.tensor_copy(mod[:, 2], ps[:, 4, 0:KT]).then_inc(mod_ready, 1)
            else:
                gate_out_(n - 1)
            if n == 2:
                multiply(0)
            if n == 3:
                regate(0)
            if n == 4:
                multiply(1)
            if n == 5:
                regate(1)
                group_rest(6, yb_hi[:, 0:4, :], yb_lo[:, 0:4, :])
            if n == 7:
                multiply(2)
        st = ST["in_g"]
        for i in range(4):
            run(st, i, in_g, lambda i, n: (3, 4 * i + n))
        gate_out_(7)
        regate(2)
        multiply(3)
        regate(3)
        group_rest(7, yb_hi[:, 4:8, :], yb_lo[:, 4:8, :])

        st = ST["mix"]

        def mix_out(i, branch):
            n = i % 2
            dve.wait_ge(half_used, chunk_end(ST["mix"], i, branch))
            banks = ps[:, 2 * branch:2 * branch + 2, :]
            if branch == 0:
                dve.wait_ge(gate_loaded[n], 32 * (i // 2 + 1))
                if i >= 2:
                    dve.wait_ge(fm_full, 8 + i - 1)
                tt(mixed[n][:], banks, gate_in[n][:, 0], ALU.mult).then_inc(pair_empty, 1)
            else:
                tt(mix_b[:], banks, gate_in[n][:, 1], ALU.mult).then_inc(pair_empty, 1)
                dve.wait_ge(pair_empty, 18 + 2 * i + 2)
                tt(mixed[n][:], mixed[n][:], mix_b[:], ALU.add).then_inc(mix_ready, 1)

        def mix_hook(i, c):
            if c == 1:
                mix_out(i, 0)
            elif i:
                mix_out(i - 1, 1)
                if i >= 2:
                    group_rest(8 + i - 2, x_hi[:, 4 * (i - 2):4 * (i - 1), :], x_lo[:, 4 * (i - 2):4 * (i - 1), :])
        for i in range(4):
            run(st, i, mix_hook, lambda i, n: (4, 4 * i + n))

        def w_o_hook(i, c):
            n = 2 * i + c
            if n == 0:
                mix_out(3, 1)
                group_rest(10, x_hi[:, 8:12, :], x_lo[:, 8:12, :])
                group_rest(11, x_hi[:, 12:16, :], x_lo[:, 12:16, :])
                dve.wait_ge(ada_summed, 4)
                nc.vector.tensor_copy(acc[0][:], wide_bank(0)).then_inc(mod_ready, 1)
                dve.wait_ge(ada_summed, 5)
                tsc(mod[:, 3], ps[:, 4, 0:KT], 1.0, None, ALU.add).then_inc(mod_ready, 1)
                dve.wait_ge(mod_ready, 5)
                tt(mod[:, 4], mod[:, 3], fm_b[:, COL["ln1_g"]:COL["ln1_g"] + KT], ALU.mult)
                then(tt(mod[:, 5], mod[:, 3], fm_b[:, COL["ln1_b"]:COL["ln1_b"] + KT], ALU.mult))
                then(tt(mod[:, 5], mod[:, 5], mod[:, 2], ALU.add))

        def branch_out(st, n):
            dve.wait_ge(half_used, end(st))
            dve.wait_ge(pre_ready, n + 2)
            for t in range(2):
                tt(tmp[:, t], wide_bank(t), acc[0][:], ALU.mult).then_inc(wide_empty, 1)
                dve.wait_ge(wide_empty, n + t + 1)
                then(tt(res[:, t], res[:, t], tmp[:, t], ALU.add))
                for k in range(D // CH):
                    ins = nc.vector.bn_stats(stats[:, t, k, :], res[:, t, k * CH:(k + 1) * CH])
                then(ins)
                nc.vector.bn_aggr(mv[:, t], stats[:, t].rearrange("p a b -> p (a b)")).then_inc(var_ready, 1)

        def normalized(n, t, to):
            dve.wait_ge(std_ready, n + t + 2)
            then(nc.vector.reciprocal(rstd[:, 1, t:t + 1], rstd[:, 0, t:t + 1]))
            return tsc(to, res[:, t], mv[:, t, 0:1], rstd[:, 1, t:t + 1], ALU.subtract, ALU.mult)

        def four_rests(g):
            for q in range(4):
                group_rest(g + q, x_hi[:, 4 * q:4 * q + 4, :], x_lo[:, 4 * q:4 * q + 4, :])

        def copy_pair(st, i, c, slot, to, free=None):
            dve.wait_ge(half_used, chunk_end(st, i, c))
            if free is not None:
                dve.wait_ge(fm_full, free)
            nc.vector.tensor_copy(to, ps[:, 2 * slot:2 * slot + 2, :]).then_inc(pair_empty, 1)

        def m1_out(st, i, c, n):
            copy_pair(st, i, c, c, ff_stage[c][:], n + 15 if not isinstance(n, int) or n >= 2 else None)

        st = ST["w_o"]
        for i in range(2):
            run(st, i, w_o_hook)

        def m1_hook(st, base):
            def hook(i, c):
                if c:
                    m1_out(st, i, 0, i * 2 + base)
                elif not isinstance(i, int) or i:
                    m1_out(st, i - 1, 1, i * 2 + (base - 1))
                elif base:
                    m1_out(ST["m1a"], 3, 1, 7)
                else:
                    branch_out(ST["w_o"], 0)
                    for t in range(2):
                        normalized(0, t, normed[:, t]).then_inc(normed_ready, 1)
                    four_rests(12)
            return hook
        rounds(dve, ST["m1a"], lambda i: run(ST["m1a"], i, m1_hook(ST["m1a"], 0), lambda i, n: (5, i * 4 + n)))
        rounds(dve, ST["m1b"], lambda i: run(ST["m1b"], i, m1_hook(ST["m1b"], 8)))

        def jit_rest(s, src, n, c):
            dve.wait_ge(fm_hi, n + (s + 1))
            tt(x_lo[:, 4 * c:4 * c + 4], src[:, ds(n * 4, 4)], x_hi[:, 4 * c:4 * c + 4].bitcast(F32),
               ALU.subtract).then_inc(fm_lo, 1)

        def m2_hook(i, c):
            if isinstance(i, int) and i == 0 and c == 0:
                m1_out(ST["m1b"], 3, 1, 15)
                jit_rest(16, ff, 0, 0)
                dve.wait_ge(ada_summed, 6)
                nc.vector.tensor_copy(acc[0][:], wide_bank(0)).then_inc(g2_ready, 1)
            if not (isinstance(i, int) and i == 7 and c == 1):
                jit_rest(16, ff, i * 2 + (c + 1), 1 - c)
        rounds(dve, ST["m2"], lambda i: run(ST["m2"], i, m2_hook), last=True)

        root_n = [0]

        def inv_rms(t):
            root_n[0] += 1
            dve.wait_ge(roots, root_n[0])
            then(nc.vector.reciprocal(rstd[:, 1, t:t + 1], ss[:, t, 1:2]))
            return rstd[:, 1, t:t + 1]

        def norm_res():
            for t in range(2):
                tsc(normed[:, t], res[:, t], inv_rms(t), None, ALU.mult).then_inc(normed_ready, 1)

        def pool_u_hook(i, c):
            st = ST["pool_u"]
            if c:
                copy_pair(st, i, 0, 0, u_stage[0][:], i * 2 + 35 if not isinstance(i, int) or i else None)
            elif not isinstance(i, int) or i:
                copy_pair(st, i - 1, 1, 1, u_stage[1][:], i * 2 + 34 if not isinstance(i, int) or i > 1 else None)
            else:
                branch_out(ST["m2"], 2)
                dve.wait_ge(ln2_in, 32)
                for t in range(2):
                    then(normalized(2, t, tmp[:, t]))
                    then(tt(tmp[:, t], tmp[:, t], ln2_g[:], ALU.mult))
                    tt(res[:, t], tmp[:, t], ln2_b[:], ALU.add).then_inc(res_ready, 1)
                norm_res()
                four_rests(32)
        rounds(dve, ST["pool_u"], lambda i: run(ST["pool_u"], i, pool_u_hook))

        def jit_group_rest(i):
            for c in range(2):
                dve.wait_ge(fm_hi, i * 2 + (37 + c))
                tt(g_lo[:, 4 * c:4 * c + 4], pooled[:, ds(i * 8 + 4 * c, 4)], g_hi[:, 4 * c:4 * c + 4].bitcast(F32),
                   ALU.subtract).then_inc(fm_lo, 1)

        def pool_product(i, c):
            n = i * 2 + c
            dve.wait_ge(silu_ready, n + 1)
            gate = pool_gate[:]
            if not isinstance(n, int) or n >= 2:
                dve.wait_ge(fm_full, n + 43)
            tt(pool_stage[c][:], ps[:, 2:4, :], gate, ALU.mult).then_inc(pair_empty, 1)
            dve.wait_ge(pair_empty, i * 4 + (52 + 2 * c))
            tt(pool_stage[c][:], pool_stage[c][:], group_out[:], ALU.mult).then_inc(product_ready, 1)

        def pool_g_hook(i, c):
            st = ST["pool_g"]
            first = isinstance(i, int) and i == 0
            if c == 0:
                if first:
                    copy_pair(ST["pool_u"], 3, 1, 1, u_stage[1][:], 42)
                    jit_group_rest(0)
                else:
                    pool_product(i - 1, 1)
            if c == 1:
                if first:
                    dve.wait_ge(fm_full, 44)
                copy_pair(st, i, 0, 0, group_out[:])
            if c == 2:
                pool_product(i, 0)
            if c == 3:
                copy_pair(st, i, 2, 0, group_out[:])
                if not (isinstance(i, int) and i == 3):
                    jit_group_rest(i + 1)
        rounds(dve, ST["pool_g"], lambda i: run(ST["pool_g"], i, pool_g_hook), last=True)

        def pool_out_hook(i, c):
            if isinstance(i, int) and i == 0 and c == 0:
                pool_product(3, 1)
                group_rest(44, p_hi[:], p_lo[:])
                jit_rest(45, pooled, 0, 0)
            if not (isinstance(i, int) and i == 3 and c == 1):
                jit_rest(45, pooled, i * 2 + (c + 1), 1 - c)
        rounds(dve, ST["pool_out"], lambda i: run(ST["pool_out"], i, pool_out_hook), last=True)

        wide = [4]

        def wide_read(ins):
            wide[0] += 1
            ins.then_inc(wide_empty, 1)

        def mixer_out(layer, gain, proj_st):
            dve.wait_ge(post_in[layer], 16)
            for t in range(2):
                wide_read(stt(out=tmp[:, t], in0=wide_bank(t), scalar=inv_rms(t), in1=gain[:], op0=ALU.mult,
                              op1=ALU.mult))
            for t in range(2):
                dve.wait_ge(wide_empty, wide[0] - 1 + t)
                tt(res[:, t], res[:, t], tmp[:, t], ALU.add).then_inc(res_ready, 1)
            norm_res()
            dve.wait_ge(half_used, end(proj_st))
            for t in range(2):
                wide_read(nc.vector.tensor_copy(proj[:, t], wide_bank(t)))

        def gate_out_wide(n):
            for t in range(2):
                dve.wait_ge(gate_read, n + t + 1)
                if t == 0:
                    dve.wait_ge(wide_empty, wide[0])
                wide_read(tt(proj[:, t], proj[:, t], tmp[:, t], ALU.mult))
            for t in range(2):
                dve.wait_ge(wide_empty, wide[0] - 1 + t)
                tt(res[:, t], res[:, t], proj[:, t], ALU.add).then_inc(res_ready, 1)

        run(ST["proj0"], 0, lambda i, c: mixer_out(0, post_g, ST["proj0"]))
        for i in range(2):
            run(ST["gate0"], i, lambda i, c: four_rests(53) if i + c == 0 else None)

        def latent_norm():
            dve.wait_ge(lat_sq, 1)
            then(nc.vector.reciprocal(lat_ss[:, 2], lat_ss[:, 1]))
            for w in range(4):
                part_w = lat[:, w % 2, w // 2]
                ins = tsc(part_w, part_w, lat_ss[:, 2, w:w + 1], None, ALU.mult)
                if w % 2:
                    ins.then_inc(lat_ready, 1)

        def mla_out(n):
            if n < 2:
                copy_pair(ST["mla_in"], n // 2, n % 2, n % 2, lat[:, :, n])
                return
            dve.wait_ge(mla_silu, n - 1)
            if n >= 4:
                dve.wait_ge(mla_gate_stored[n % 2], 16)
            tt(mla_gate_out[n % 2][:], ps[:, 2 * (n % 2):2 * (n % 2) + 2, :], mla_sig[n % 2][:], ALU.mult) \
                .then_inc(pair_empty, 1)

        def mla_in_hook(i, c):
            n = 2 * i + c
            if n == 0:
                gate_out_wide(0)
                norm_res()
                four_rests(57)
            else:
                mla_out(n - 1)
            if n == 4:
                latent_norm()
        for i in range(3):
            run(ST["mla_in"], i, mla_in_hook)
        run(ST["k_pe"], 0, lambda i, c: mla_out(5))

        q_flat = q_tm[:].rearrange("p t h d -> p t (h d)")
        kv_flat = kv_tm[:].rearrange("p t h d -> p t (h d)")

        def latent_out(st, n, m, to):
            copy_pair(st, 0, n, m % 2, to[:, :, n * CH:(n + 1) * CH])

        def rotate(x1, x2, cos, sin, scratch):
            for out_, x, table in ((0, x1, cos), (1, x2, sin), (2, x2, cos), (3, x1, sin)):
                ins = tt(scratch(out_), x, table, ALU.mult)
            then(ins)
            tt(x1, scratch(0), scratch(1), ALU.subtract)
            then(tt(x2, scratch(2), scratch(3), ALU.add))

        def rotate_heads(t):
            x = q_tm[:, t, :, NOPE:QK]
            cos, sin = (tb[:, t].unsqueeze(1).to_broadcast([P, HEADS, ROPE // 2]) for tb in (rope_cos, rope_sin))
            rotate(x[:, :, 0:ROPE // 2], x[:, :, ROPE // 2:ROPE], cos, sin, lambda n: rope_t[:, n])

        def w_uq_hook(i, c):
            if c == 0:
                dve.wait_ge(half_used, end(ST["k_pe"]))
                nc.vector.tensor_copy(k_pe[:], ps[:, 0:2, 0:ROPE]).then_inc(pair_empty, 1)
                group_rest(61, x_hi[:, 0:4, :], x_lo[:, 0:4, :])
                group_rest(62, x_hi[:, 4:8, :], x_lo[:, 4:8, :])
            else:
                latent_out(ST["w_uq"], c - 1, 73 + c - 1, q_flat)
        run(ST["w_uq"], 0, w_uq_hook)

        def w_ukv_hook(i, c):
            if c == 0:
                latent_out(ST["w_uq"], 5, 78, q_flat)
                for slot in mla_gate_stored:
                    dve.wait_ge(slot, 32)
                dve.wait_ge(sines, 2)
            else:
                latent_out(ST["w_ukv"], c - 1, 79 + c - 1, kv_flat)
            if c in (2, 4):
                dve.wait_ge(pair_empty, 79)
                rotate_heads(c // 2 - 1)
            if c == 6:
                rotate(k_pe[:, :, 0:ROPE // 2], k_pe[:, :, ROPE // 2:ROPE], rope_cos[:], rope_sin[:],
                       lambda n: rope_t[:, n, 0:2])
        run(ST["w_ukv"], 0, w_ukv_hook)

        def head_qpe(h):
            dve.wait_ge(qk_turned, h + 1)
            if h >= 2:
                dve.wait_ge(scored, h - 1)
            nc.vector.tensor_copy(q_peT[h % 2][0:ROPE, :], ps[0:ROPE, 2, 0:S]).then_inc(qpe_out, 1)

        def head_scores(h):
            dve.wait_ge(scored, h + 1)
            if h >= 2:
                dve.wait_ge(prob_ready, 2 * (h - 1))
            then(stt(out=score[h % 2][:].rearrange("p b k -> p (b k)"), in0=ps[:, 3 + h % 2, 0:3 * P],
                     scalar=SM_SCALE, in1=mask[:].rearrange("p b k -> p (b k)"), op0=ALU.mult, op1=ALU.add))
            nc.vector.reduce_max(sm_max[:, h % 4, 0:1], score[h % 2][:, 0], axis=AX.X)
            then(nc.vector.reduce_max(sm_max[:, h % 4, 1:2], score[h % 2][:, 1:3].rearrange("p b k -> p (b k)"),
                                      axis=AX.X))
            tsc(sm_max[:, h % 4], sm_max[:, h % 4], -1.0, None, ALU.mult).then_inc(score_ready, 1)

        def head_out(h):
            dve.wait_ge(o_mm, h + 1)
            then(nc.vector.reciprocal(sm_inv[:, h % 4], sm_sum[:, h % 4]))
            for t in range(2):
                ins = stt(out=q_tm[:, t, h, 0:VD], in0=ps[:, 7, t * P:(t + 1) * P], scalar=sm_inv[:, h % 4, t:t + 1],
                          in1=g_tm[:, t, h * VD:(h + 1) * VD], op0=ALU.mult, op1=ALU.mult)
            ins.then_inc(o_ready, 1)

        def w_out_hook(i, c):
            if i or c:
                return
            copy_pair(ST["w_ukv"], 0, 7, 0, kv_flat[:, :, 7 * CH:8 * CH])
            dve.wait_ge(pair_empty, 87)
            dve.wait_ge(k_peT_ready, 1)
            nc.vector.tensor_copy(k_peT[0:ROPE, :], ps[0:ROPE, 7, 0:S]).then_inc(k_peT_out, 1)
            dve.wait_ge(mask_ready, 2)
            for step in range(HEADS + 3):
                if step < HEADS:
                    head_qpe(step)
                if 0 <= step - 1 < HEADS:
                    head_scores(step - 1)
                if 0 <= step - 3 < HEADS:
                    if step == 3:
                        dve.wait_ge(g_loaded, 16)
                    head_out(step - 3)
            four_rests(63)
        for i in range(2):
            run(ST["w_out"], i, w_out_hook)
        run(ST["proj1"], 0, lambda i, c: mixer_out(1, post_g1, ST["proj1"]))
        for i in range(2):
            run(ST["gate1"], i, lambda i, c: four_rests(67) if i + c == 0 else None)
        gate_out_wide(2)


def kernel(**inputs):
    import numpy as _np
    import concourse.bacc as _bacc
    from concourse import mybir as _mybir
    from concourse.bass_utils import run_bass_kernel_spmd as _run

    nc = _bacc.Bacc("TRN2", target_bir_lowering=False, num_devices=1)
    arrays, aps = {}, {}
    for name, value in {**inputs, **tables()}.items():
        v = _np.ascontiguousarray(value)
        arrays[f"in_{name}"] = v
        aps[name] = nc.dram_tensor(f"in_{name}", v.shape, _mybir.dt.from_np(v.dtype), kind="ExternalInput").ap()
    out = nc.dram_tensor("out", (1, S, D), _mybir.dt.float32, kind="ExternalOutput").ap()
    block_kernel(nc, aps, out)
    return _run(nc, [arrays], core_ids=[0]).results[0]["out"]
```

```python
from contextlib import ExitStack

import math

import numpy as np

import concourse.bass as bass
from concourse import mybir
from concourse.alu_op_type import AluOpType as ALU

F32 = mybir.dt.float32
F32R = mybir.dt.float32r
I32 = mybir.dt.int32
ACT = mybir.ActivationFunctionType
AX = mybir.AxisListType
ds = bass.ds

P = 128
S = 256
D = 2048
KT = D // P
W1 = D // 2
FF = 4 * D
CH = 512
UNIT = 2048
HALF = UNIT // 2
SLOTS = 4
ALPHA = 2.0 ** 0.25
LN_EPS = 1e-5
RMS_EPS = 1e-6
HEADS = 16
NOPE, ROPE, VD = 128, 64, 128
QK = NOPE + ROPE
SM_SCALE = QK ** -0.5
NEG = -1e30
HID = 64
EMB = 33
E_POOL = 4096
MAGIC = 1.5 * 2.0 ** 23
INV_2PI = 1.0 / (2.0 * math.pi)
TWO_PI = (6.28125, 0.0019340515136718750, 2.0 * math.pi - 6.28125 - 0.0019340515136718750)
SIN_MAX = 3.1415925
KB = 1024


def tables():
    f32 = np.float32
    t = np.arange(S)[:, None].astype(np.float64)
    w = 2.0 * np.pi * (np.arange(S)[None, :] + 0.5) / (2 * S)
    cos_tf, sin_tf = np.cos(t * w), np.sin(t * w)
    dft = np.stack([cos_tf, -sin_tf, (cos_tf / S).T, (-sin_tf / S).T])
    bands = (EMB - 1) // 2
    lin = np.linspace(0.0, 1.0, S)[:, None]
    omega = 2.0 * np.pi * np.arange(S)[:, None] / S
    band = np.linspace(1e-4, bands - 1, bands)[None, :]
    feats = np.concatenate([lin, np.cos(band * omega), -np.sin(band * omega)], axis=1).T
    deltas = np.abs(np.linspace(math.log(1e-2) / 1.5, math.log(1e-2) / 0.3, W1))[None, :]
    window = np.exp(-lin * deltas)
    pool = np.zeros((4, S, S))
    for j, width in enumerate((2, 4, 8, 16)):
        for to in range(S):
            n = min(to + 1, width)
            pool[j, to - n + 1:to + 1, to] = 1.0 / n
            pool[j, to, to] -= 1.0
    freq = (10000.0 ** (-np.arange(0, ROPE, 2, dtype=np.float32) / ROPE))[None, :]
    return {
        "k_dft": dft.astype(f32), "k_feats": feats.astype(f32), "k_window": window.astype(f32),
        "k_pool": pool.astype(f32), "k_freq": freq.astype(f32), "k_ident": np.eye(P, dtype=f32),
    }


A2 = [("wwa", "wwa")] * 2
W2 = [("ww", "ww")] * 2
STREAM = [
    ("ada", 8, [("aaaa", "")]),
    ("in_vu", 2, A2), ("in_h", 2, A2), ("in_h2", 1, W2), ("in_g", 4, A2),
    ("mix", 1, [("w", "wa")] * 8), ("w_o", 2, A2),
    ("m1a", 4, [("ww", "awwa")] * 2), ("m1b", 4, W2), ("m2", 8, W2),
    ("pool_u", 4, W2), ("pool_g", 4, [("w", "w"), ("ww", "ww")] * 2), ("pool_out", 4, W2),
    ("proj0", 1, [("ww", "")]), ("gate0", 2, W2),
    ("mla_in", 3, W2), ("k_pe", 1, [("w", "")]), ("w_uq", 1, [("w", "")] * 6), ("w_ukv", 1, [("w", "")] * 8),
    ("w_out", 2, W2), ("proj1", 1, [("ww", "")]), ("gate1", 2, W2),
]


class Stage:

    def __init__(self, kinds, first, rounds, chunks):
        self.first, self.rounds, self.chunks = first, rounds, chunks
        self.pattern = "".join(f + r for f, r in chunks)
        self.length = len(self.pattern)
        self.kinds = kinds
        self.size = UNIT
        assert rounds == 1 or self.length % SLOTS == 0

    def _line(self, of, i, at_least=False):
        values = [of(r) for r in range(self.rounds)]
        if isinstance(i, int):
            return values[i]
        slope = of(self.rounds - 1) - of(self.rounds - 2) if self.rounds > 1 else 0
        offset = max(v - slope * r for r, v in enumerate(values) if r)
        assert at_least or all(v == offset + slope * r for r, v in enumerate(values))
        return i * slope + offset

    def load(self, i, j):
        return self._line(lambda r: self.first + r * self.length + j, i)

    def before(self, kind, i, j):
        return self._line(lambda r: self.kinds[:self.first + r * self.length + j].count(kind), i)

    def slot(self, j):
        return (self.first + j) % SLOTS

    def landed(self, i, j):
        return self._line(lambda r: 16 * ((self.first + r * self.length + j) // SLOTS + 1), i)

    def freed(self, kind, i, j):
        return self._line(lambda r: self.kinds[:max(self.first + r * self.length + j - SLOTS + 1, 0)].count(kind),
                          i, at_least=True)

    def half(self, i, j):
        return self._line(lambda r: 2 * self.kinds[:self.first + r * self.length + j].count("w"), i)

    def half_slot(self, j, half):
        return (2 * self.kinds[:self.first + j].count("w") + half) % SLOTS


def stages():
    out, kinds = {}, "".join("".join(f + r for f, r in chunks) * n for _, n, chunks in STREAM)
    first = 0
    for name, rounds, chunks in STREAM:
        out[name] = Stage(kinds, first, rounds, chunks)
        first += rounds * out[name].length
    out["k_pe"].size = KT * ROPE
    return out


def rounds(eng, stage, body, last=False):
    n = stage.rounds
    end = n - 1 if last else n
    body(0)
    if end > 1:
        with eng.Fori(1, end) as i:
            body(i)
    if last and n > 1:
        body(n - 1)


def block_kernel(nc, a, out):
    ctx = ExitStack()
    ST = stages()

    def sem(name):
        return ctx.enter_context(nc.semaphore(name))

    ctx.enter_context(nc.sbuf_tensor("slab", [P, 207 * KB // 4], F32))

    def at(name, kb, shape, dt=F32):
        return nc.alloc_sbuf_tensor_at(name, [P, *shape], dt, offset=16512 + int(kb * KB))

    raw = [at(f"raw{i}", 8 * i, [UNIT]) for i in range(SLOTS)]
    w_hi = [at(f"w_hi{i}", 32 + 4 * i, [HALF], F32R) for i in range(SLOTS)]
    w_lo = [at(f"w_lo{i}", 48 + 4 * i, [HALF], F32R) for i in range(SLOTS)]
    res = at("res", 64, [2, D])
    x_hi = at("x_hi", 80, [KT, S], F32R)
    x_lo = at("x_lo", 96, [KT, S], F32R)
    ya_hi = at("ya_hi", 64, [W1 // P, S], F32R)
    ya_lo = at("ya_lo", 72, [W1 // P, S], F32R)

    acc = [at("ada_acc0", 112, [D]), at("ada_acc1", 120, [D])]
    dft = at("dft", 128, [4, 2, S])
    sgu_wT = at("sgu_wT", 136, [8, P])
    window = at("window", 140, [2, W1])
    w3 = at("w3", 148, [4 * W1])
    feats = at("feats", 164, [S])
    w1 = at("w1", 165, [HID])
    w2 = at("w2", 165.25, [HID])
    hid_arg = at("hid_arg", 166, [S])
    hid_n = at("hid_n", 167, [S])
    h_fwd = at("h_fwd", 168, [2, CH])
    h_bwd = at("h_bwd", 172, [2, CH])
    h_sum = at("h_sum", 176, [2, CH])
    spec_out = at("spec_out", 180, [4, CH])
    vu = at("vu", 140, [2, 2, W1])
    sgu_g = at("sgu_g", 156, [W1])
    sgu_b = at("sgu_b", 160, [W1])
    zh_out = [at(f"zh_out{i}", 164 + 4 * i, [2, CH]) for i in range(2)]
    conv_in = at("conv_in", 64, [3, 2, CH])
    conv_out = at("conv_out", 76, [2, CH])
    conv_w = at("conv_w", 172, [4, CH])
    spec = at("spec", 136, [4, CH])
    prod = at("prod", 144, [4, CH])
    part = at("part", 152, [2, CH])
    hy_v = [at(f"hy_v{i}", 156 + 12 * i, [2, CH]) for i in range(2)]
    hy_x = [at(f"hy_x{i}", 160 + 4 * i, [2, CH]) for i in range(2)]
    yb_hi = at("yb_hi", 172, [W1 // P, S], F32R)
    yb_lo = at("yb_lo", 180, [W1 // P, S], F32R)
    gate_out = [at(f"gate_out{i}", 180 + 4 * i, [2, CH]) for i in range(2)]
    skip = at("skip", 188, [CH])
    gate_in = [at(f"gate_in{i}", 136 + 8 * i, [2, 2, CH]) for i in range(2)]
    mixed = [at(f"mixed{i}", 152 + 4 * i, [2, CH]) for i in range(2)]
    mix_b = at("mix_b", 160, [2, CH])
    normed = at("normed", 136, [2, D])
    bias_o = at("bias_o", 128, [D])
    ln_g = at("ln_g", 152, [D])
    ln_b = at("ln_b", 160, [D])
    tmp = at("tmp", 168, [2, D])

    ff = at("ff", 120, [FF // P, S])
    ff_stage = [at("ff_stage0", 184, [2, CH]), at("ff_stage1", 198, [2, CH])]
    bias_ff = at("bias_ff", 190, [D])
    ln2_b = at("ln2_b", 120, [D])
    ln2_g = at("ln2_g", 128, [D])
    pool_m = at("pool_m", 112, [4, 2, S])
    u_stage = [at(f"u_stage{i}", 120 + 4 * i, [2, CH]) for i in range(2)]
    post_g = at("post_g", 128, [D])
    pooled = at("pooled", 152, [E_POOL // P, S])
    g_hi = at("g_hi", 136, [8, S], F32R)
    g_lo = at("g_lo", 144, [8, S], F32R)
    group_out = at("group_out", 120, [2, CH])
    pool_gate = at("pool_gate", 124, [2, CH])
    pool_stage = [at("pool_stage0", 184, [2, CH]), at("pool_stage1", 198, [2, CH])]
    p_tm = at("p_tm", 112, [4, S])
    p_lo = at("p_lo", 112, [4, S], F32R)
    p_hi = at("p_hi", 116, [4, S], F32R)
    proj = at("proj", 152, [2, D])
    q_tm = at("q_tm", 120, [2, HEADS, QK])
    kv_tm = at("kv_tm", 144, [2, HEADS, NOPE + VD])
    lat = at("lat", 144, [2, 2, CH])
    mla_gate_out = [at(f"mla_gate_out{i}", 168 + 4 * i, [2, CH]) for i in range(2)]
    rope_t = at("rope_t", 176, [4, HEADS, ROPE // 2])
    mla_sig = [at(f"mla_sig{i}", 176 + 4 * i, [2, CH]) for i in range(2)]
    lat_junk = at("lat_junk", 152, [4, CH])
    k_pe = at("k_pe", 198, [2, ROPE])
    k_peT = at("k_peT", 189, [S])
    qk_fm = [at(f"qk_fm{i}", 176 + 2 * i, [2, S]) for i in range(2)]
    q_peT = [at(f"q_peT{i}", 180 + i, [S]) for i in range(2)]
    score = [at(f"score{i}", 182 + 1.5 * i, [3, P]) for i in range(2)]
    probT = [at(f"probT{i}", 185 + 1.5 * i, [3, P]) for i in range(2)]
    prob = [at(f"prob{i}", 198.5 + 1.5 * i, [3, P]) for i in range(2)]
    g_tm = at("g_tm", 80, [2, D])
    mask = at("mask", 96, [3, P])
    post_g1 = at("post_g1", 128, [D])

    y_fm = [at(f"y_fm{i}", 190 + 4 * i, [4, S]) for i in range(2)]
    sgu_raw = at("sgu_raw", 190, [8, P])
    rows_a = at("rows_a", 194, [P])
    rows_b = at("rows_b", 194.5, [P])
    zero = at("zero", 205.5, [3 * W1 // P])
    bias_bc = [at(f"bias_bc{i}", 198 + 2 * i, [CH]) for i in range(2)]
    ident = at("ident", 202, [P])
    fm_a = at("fm_a", 202.5, [P])
    fm_b = at("fm_b", 203, [P])
    mod = at("mod", 203.5, [6, KT])
    cond = at("cond", 204, [KT])
    sig_c = at("sig_c", 204.0625, [KT])
    ones = at("ones", 204.125, [2])
    stats = at("stats", 204.25, [2, 4, 6])
    mv = at("mv", 204.5, [2, 2])
    rstd = at("rstd", 204.5625, [2, 2])
    ones_m = at("ones_m", 205, [P])
    pos_i = at("pos_i", 188, [P], I32)
    pos_f = at("pos_f", 188.5, [P])
    pos = at("pos", 205.625, [2])
    freq = at("freq", 189, [ROPE // 2])
    ang_n = at("ang_n", 189.25, [2, ROPE // 2])
    rope_cos = at("rope_cos", 205.75, [2, ROPE // 2])
    rope_sin = at("rope_sin", 206, [2, ROPE // 2])
    eps = at("eps", 204.59375, [2])
    lat_ss = at("lat_ss", 206.875, [3, 4])
    sm_max = at("sm_max", 206.75, [4, 2])
    sm_sum = at("sm_sum", 206.78125, [4, 2])
    sm_inv = at("sm_inv", 206.8125, [4, 2])
    ss = at("ss", 206.84375, [2, 2])
    COL = dict(pool_scale=0, q_norm=32, kv_norm=36, sgu_b=40, c=48, ln1_g=64, ln1_b=80, b1=96, b2=97, freq=98)

    ps = ctx.enter_context(nc.psum_tensor("ps", [P, 8, CH], F32))
    fm_ps = [ps[:, 4 + 2 * g:6 + 2 * g, :].rearrange("p a (b s) -> p (a b) s", s=S) for g in range(2)]

    spec_dram = nc.dram_tensor("spec_dram", [2, 2, P, 4 * CH], F32).ap()
    zh_dram = nc.dram_tensor("zh_dram", [S + 2, 3 * W1], F32).ap()
    conv_dram = nc.dram_tensor("conv_dram", [6, P, 2 * CH], F32).ap()
    gate_dram = nc.dram_tensor("gate_dram", [S, 2 * D], F32).ap()

    raw_full = [sem(f"raw_full{i}") for i in range(SLOTS)]
    hi_split = sem("hi_split")
    lo_split = sem("lo_split")
    first_done = sem("first_done")
    half_used = sem("half_used")
    ada_added = sem("ada_added")
    acc_zeroed = sem("acc_zeroed")
    acc_ready = [sem(f"acc_ready{i}") for i in range(2)]
    ada_summed = sem("ada_summed")
    mod_ready = sem("mod_ready")
    pair_empty = sem("pair_empty")
    wide_empty = sem("wide_empty")
    fm_full = sem("fm_full")
    fm_empty = sem("fm_empty")
    fm_hi = sem("fm_hi")
    fm_lo = sem("fm_lo")
    vectors_in = sem("vectors_in")
    hidden_in = sem("hidden_in")
    matrices_in = sem("matrices_in")
    sgu_turned = sem("sgu_turned")
    x_loaded = sem("x_loaded")
    vectors_out = sem("vectors_out")
    sgu_wT_out = sem("sgu_wT_out")
    setup_tr = sem("setup_tr")
    rows_zeroed = sem("rows_zeroed")
    ones_set = sem("ones_set")
    c_sig = sem("c_sig")
    cond_ready = sem("cond_ready")
    hid_mm = sem("hid_mm")
    hid_red = sem("hid_red")
    hid_sin = sem("hid_sin")
    filt_mm = sem("filt_mm")
    filt_win = sem("filt_win")
    filt_sum = sem("filt_sum")
    spec_mm = sem("spec_mm")
    spec_copied = sem("spec_copied")
    spec_stored = sem("spec_stored")
    bias_full = [sem(f"bias_full{i}") for i in range(2)]
    gelu_done = sem("gelu_done")
    sgu_consts = sem("sgu_consts")
    v_step = sem("v_step")
    s_step = sem("s_step")
    g_step = sem("g_step")
    var_ready = sem("var_ready")
    std_ready = sem("std_ready")
    vn_ready = sem("vn_ready")
    sgu_mm = sem("sgu_mm")
    sgu_out = sem("sgu_out")
    zh_stored = [sem(f"zh_stored{i}") for i in range(2)]
    zh_edges = sem("zh_edges")
    conv_loaded = sem("conv_loaded")
    conv_done = sem("conv_done")
    conv_w_in = sem("conv_w_in")
    conv_stored = sem("conv_stored")
    hy_v_in = sem("hy_v_in")
    hy_x_in = [sem(f"hy_x_in{i}") for i in range(2)]
    spec_in = sem("spec_in")
    skip_in = sem("skip_in")
    hy_f = sem("hy_f")
    hy_prod = sem("hy_prod")
    hy_i = sem("hy_i")
    hy_gated = sem("hy_gated")
    gate_sig = sem("gate_sig")
    gate_stored = [sem(f"gate_stored{i}") for i in range(2)]
    gate_loaded = [sem(f"gate_loaded{i}") for i in range(2)]
    mix_ready = sem("mix_ready")
    mix_turned = sem("mix_turned")
    x_again = sem("x_again")
    ln_consts = sem("ln_consts")
    pre_ready = sem("pre_ready")
    normed_ready = sem("normed_ready")
    x1_ready = sem("x1_ready")
    bias_o_in = sem("bias_o_in")
    g2_ready = sem("g2_ready")
    bias_ff_in = sem("bias_ff_in")
    ff_ready = sem("ff_ready")
    ln2_in = sem("ln2_in")
    res_ready = sem("res_ready")
    squares = sem("squares")
    mean_sq = sem("mean_sq")
    roots = sem("roots")
    pool_in = sem("pool_in")
    post_in = [sem(f"post_in{i}") for i in range(2)]
    pool_gated = sem("pool_gated")
    silu_ready = sem("silu_ready")
    product_ready = sem("product_ready")
    p_loaded = sem("p_loaded")
    gate_read = sem("gate_read")
    proj_out = sem("proj_out")
    lat_ready = sem("lat_ready")
    lat_sq = sem("lat_sq")
    mla_silu = sem("mla_silu")
    mla_gate_stored = [sem(f"mla_gate_stored{i}") for i in range(2)]
    g_loaded = sem("g_loaded")
    angles = sem("angles")
    sines = sem("sines")
    pos_ready = sem("pos_ready")
    mask_ready = sem("mask_ready")
    k_peT_ready = sem("k_peT_ready")
    qk_turned = sem("qk_turned")
    qk_out = sem("qk_out")
    qpe_out = sem("qpe_out")
    scored = sem("scored")
    score_ready = sem("score_ready")
    prob_ready = sem("prob_ready")
    prob_turned = sem("prob_turned")
    probT_out = sem("probT_out")
    k_peT_out = sem("k_peT_out")
    o_mm = sem("o_mm")
    o_ready = sem("o_ready")
    out_stored = sem("out_stored")
    RES_END = 10

    block = ctx.enter_context(nc.Block())

    N_VECTORS = 15
    ADA_COLS = [0, 1, 3, 2, 4, 5]
    ADA_ACC = [0, 1, 1, 0, 1, 0]
    ADA_NTH = [1, 1, 2, 2, 3, 3]
    IN_COLS = ([W1, W1 + CH, 0, CH] + [2 * W1 + W1 * part_n + CH * b for b in range(2) for part_n in range(3)] +
               [5 * W1 + CH * n for n in range(8)])

    def chunk_end(st, i, c):
        pattern = "".join(f + r for f, r in st.chunks[:c + 1])
        return st.half(i, pattern.rindex("w")) + 2

    def end(st):
        return chunk_end(st, st.rounds - 1, len(st.chunks) - 1)

    def wait_apart(eng, semaphore, value):
        if not isinstance(value, int):
            eng.wait_ge(ones_set, 4)
        eng.wait_ge(semaphore, value)

    WIDE = ("w_o", "m2", "pool_out", "proj0", "gate0", "w_out", "proj1", "gate1")

    def wait_product(eng, st, t):
        if t == 0:
            eng.wait_ge(first_done, 1 + [ST[name] for name in WIDE].index(st))
        else:
            eng.wait_ge(half_used, end(st))

    def wide_bank(t):
        return ps[:, 4 * t:4 * t + 4, :].rearrange("p a n -> p (a n)")

    @block.sync
    def _(sync):
        def load(st, i, j, src):
            slot = st.slot(j)
            kind = st.pattern[j]
            used_w, used_a = st.freed("w", i, j) * 2, st.freed("a", i, j)
            if not isinstance(used_w, int) or used_w > 0:
                wait_apart(sync, lo_split, used_w)
            if not isinstance(used_a, int) or used_a > 0:
                wait_apart(sync, ada_added, used_a)
            size = 1
            for n in src.shape[1:]:
                size *= n
            dst = raw[slot][:, 0:size]
            if len(src.shape) == 3:
                dst = dst.rearrange("p (k n) -> p k n", k=src.shape[1])
            sync.dma_start(dst, src).then_inc(raw_full[slot], 16)

        def by_chunk(w, q, col, kts=4, width=CH):
            return w.rearrange("(k p) n -> p k n", p=P)[:, kts * q:kts * (q + 1), ds(col, width)]

        def by_row(w, k):
            return w.rearrange("(k p) n -> p k n", p=P)[:, ds(k, 1), :]

        w_ada = a["w_ada"][0].rearrange("(k p) n -> p k n", p=P)

        def ada(n, block_n):
            col = ADA_COLS[block_n] * D
            return w_ada[:, ds(n, 1), col:col + D]

        def load_bias(n, col):
            slot = n % 2 if isinstance(n, int) else None
            if n >= 2:
                sync.wait_ge(pair_empty, n - 1)
            sync.dma_start(bias_bc[slot][:], a["b_in"][0, col:col + CH].partition_broadcast(P)) \
                .then_inc(bias_full[slot], 16)

        st = ST["ada"]
        for i in range(8):
            for j in range(4):
                load(st, i, j, ada(4 * (i % 4) + j, i // 4))

        w_in = a["w_in"][0]
        chunk = 0
        kk = 0
        for name in ("in_vu", "in_h", "in_h2", "in_g"):
            st = ST[name]
            for i in range(st.rounds):
                w = 0
                for j, kind in enumerate(st.pattern):
                    if kind == "a":
                        load(st, i, j, ada(kk % 16, 2 + kk // 16))
                        kk += 1
                        continue
                    load(st, i, j, by_chunk(w_in, w % 4, IN_COLS[chunk]))
                    if w % 4 == 2:
                        load_bias(chunk, IN_COLS[chunk])
                    w += 1
                    chunk += w % 4 == 0
        st = ST["mix"]
        w = b = 0
        for j, kind in enumerate(st.pattern):
            if kind == "a":
                load(st, 0, j, ada(b, 4))
                b += 1
            else:
                src = a["w_branch_a"][0] if w % 4 < 2 else a["w_branch_b"][0]
                load(st, 0, j, by_chunk(src, w % 2, w // 4 * CH))
                w += 1

        def rows(st, w):
            rounds(sync, st, lambda i: [load(st, i, j, by_row(w, i * st.length + j)) for j in range(st.length)])

        st = ST["w_o"]
        w = 0
        for i in range(2):
            for j, kind in enumerate(st.pattern):
                if kind == "a":
                    load(st, i, j, ada(b, 4))
                    b += 1
                else:
                    load(st, i, j, by_row(a["w_o"][0], w))
                    w += 1
        w_m1 = a["w_m1"][0]

        def m1(name, before, with_ada):
            st = ST[name]

            def body(i):
                w = b = 0
                for j, kind in enumerate(st.pattern):
                    if kind == "a":
                        load(st, i, j, ada(i * 4 + b, 5))
                        b += 1
                    else:
                        load(st, i, j, by_chunk(w_m1, w % 4, i * (2 * CH) + (before + w // 4) * CH))
                        w += 1
            if with_ada:
                for i in range(st.rounds):
                    body(i)
            else:
                rounds(sync, st, body)
        m1("m1a", 0, True)
        m1("m1b", 8, False)
        rows(ST["m2"], a["w_m2"][0])

        def chunks(st, w, col):
            per = KT // 4
            rounds(sync, st, lambda i: [load(st, i, j, by_chunk(w, j % per, i * (2 * CH) + (j // per) * CH + col))
                                        for j in range(st.length)])

        w_pool = a["pool_w_in_2"][0]
        chunks(ST["pool_u"], w_pool, 0)
        st = ST["pool_g"]
        w_group = a["pool_w_group_2"][0].rearrange("g (k p) n -> p g k n", p=P)

        def pool_round(i):
            j = 0
            for c in range(2):
                for q in range(2):
                    src = w_group[:, ds(i, 1), 4 * q:4 * q + 4, c * CH:(c + 1) * CH].rearrange("p g k n -> p (g k) n")
                    load(st, i, j, src)
                    j += 1
                for q in range(4):
                    load(st, i, j, by_chunk(w_pool, q, i * (2 * CH) + E_POOL + c * CH))
                    j += 1
        rounds(sync, st, pool_round)
        rows(ST["pool_out"], a["pool_w_out_2"][0])
        rows(ST["proj0"], a["ple_w_proj_2"][0])
        rows(ST["gate0"], a["ple_w_gate_2"][0])
        st = ST["mla_in"]
        w_mla = a["mla_w_in_2"][0]
        for i in range(3):
            for j in range(8):
                n = 2 * i + j // 4
                load(st, i, j, by_chunk(w_mla, j % 4, n * CH + (ROPE if n >= 2 else 0)))
        load(ST["k_pe"], 0, 0, by_chunk(w_mla, 0, 2 * CH, KT, ROPE))
        for n in range(6):
            load(ST["w_uq"], 0, n, by_chunk(a["mla_w_uq_2"][0], 0, n * CH))
        for n in range(8):
            load(ST["w_ukv"], 0, n, by_chunk(a["mla_w_ukv_2"][0], 0, n * CH))
        rows(ST["w_out"], a["mla_w_out_2"][0])
        rows(ST["proj1"], a["ple_w_proj_2"][1])
        rows(ST["gate1"], a["ple_w_gate_2"][1])
        sync.wait_ge(res_ready, RES_END)
        sync.dma_start(out[0].rearrange("(t p) n -> p t n", p=P), res[:]).then_inc(out_stored, 16)
        sync.wait_ge(out_stored, 16)

    @block.gpsimd
    def _(pool):
        steps = [0]

        def then(ins):
            steps[0] += 1
            ins.then_inc(g_step, 1)
            pool.wait_ge(g_step, steps[0])

        nc.gpsimd.memset(rows_b[:], 0.0).then_inc(rows_zeroed, 1)
        nc.gpsimd.memset(ones[:], 1.0).then_inc(ones_set, 1)
        nc.gpsimd.memset(ones_m[:], 1.0).then_inc(ones_set, 1)
        nc.gpsimd.memset(eps[:, 0:1], RMS_EPS).then_inc(ones_set, 1)
        nc.gpsimd.memset(eps[:, 1:2], LN_EPS).then_inc(ones_set, 1)

        def start_acc(b):
            buf = acc[ADA_ACC[b]]
            nc.gpsimd.memset(buf[:], 0.0).then_inc(acc_zeroed, 1)
            pool.wait_ge(acc_zeroed, b + 1)
            col = ADA_COLS[b] * D
            pool.dma_start(buf[0:1, :], a["b_ada"][:, col:col + D]).then_inc(acc_ready[ADA_ACC[b]], 16)

        start_acc(0)
        start_acc(1)
        pool.dma_start(res[:], a["x"][0].rearrange("(t p) n -> p t n", p=P)).then_inc(x_loaded, 16)

        for it in range(4):
            pool.wait_ge(filt_win, it + 1)
            if it:
                pool.wait_ge(spec_mm, it)
            then(nc.gpsimd.tensor_tensor(h_sum[:], h_fwd[:], h_bwd[:], ALU.add))
            nc.gpsimd.tensor_tensor(h_bwd[:], h_fwd[:], h_bwd[:], ALU.subtract).then_inc(filt_sum, 1)
        pool.wait_ge(spec_mm, 4)
        pool.dma_start(sgu_g[:], a["sgu_ln_g"][0].partition_broadcast(P)).then_inc(sgu_consts, 16)
        pool.dma_start(sgu_b[:], a["sgu_ln_b"][0].partition_broadcast(P)).then_inc(sgu_consts, 16)
        then(nc.gpsimd.memset(zero[:], 0.0))
        for r in (0, S + 1):
            pool.dma_start(zh_dram[r].rearrange("(p n) -> p n", p=P), zero[:]).then_inc(zh_edges, 16)
        pool.wait_ge(mod_ready, 2)
        start_acc(2)
        def load_conv_w(n):
            col = IN_COLS[4 + n] - 2 * W1
            pool.dma_start(conv_w[:, 0:3], a["hy_conv_w"][0, :, col:col + CH].partition_broadcast(P)) \
                .then_inc(conv_w_in, 16)
            pool.dma_start(conv_w[:, 3], a["hy_conv_b"][0, col:col + CH].partition_broadcast(P)) \
                .then_inc(conv_w_in, 16)

        def load_block(n, dst, done):
            pool.dma_start(dst.rearrange("p t n -> p (t n)"), conv_dram[n]).then_inc(done, 16)

        def load_spec(n):
            b, o = n // 2, n % 2
            pool.dma_start(spec[:].rearrange("p a n -> p (a n)"), spec_dram[o, b]).then_inc(spec_in, 16)

        def load_skip(n):
            b, o = n // 2, n % 2
            pool.dma_start(skip[:], a["hy_skip"][0, o, b * CH:(b + 1) * CH].partition_broadcast(P)) \
                .then_inc(skip_in, 16)

        pool.wait_ge(zh_edges, 32)
        pool.wait_ge(fm_full, 4)
        load_conv_w(0)
        for n in range(6):
            if n == 1:
                start_acc(3)
            pool.wait_ge(zh_stored[n % 2], 16 * (n // 2 + 1))
            col = IN_COLS[4 + n] - 2 * W1
            for j in range(3):
                pool.dma_start(conv_in[:, j], zh_dram[j:j + S, col:col + CH].rearrange("(t p) n -> p t n", p=P)) \
                    .then_inc(conv_loaded, 16)
            if n == 3:
                pool.wait_ge(vn_ready, 2)
                load_block(0, hy_v[0][:], hy_v_in)
                load_block(1, hy_x[0][:], hy_x_in[0])
            if n == 4:
                pool.wait_ge(fm_full, 6)
                load_spec(0)
                load_skip(0)
            pool.wait_ge(conv_w_in, 32 * (n + 1))
            pool.wait_ge(conv_loaded, 48 * (n + 1))
            w = [conv_w[:, j:j + 1, :].to_broadcast([P, 2, CH]) for j in range(4)]
            for j in range(3):
                ins = nc.gpsimd.tensor_tensor(conv_in[:, j], conv_in[:, j], w[j], ALU.mult)
            then(ins)
            then(nc.gpsimd.tensor_tensor(conv_in[:, 0], conv_in[:, 0], conv_in[:, 1], ALU.add))
            then(nc.gpsimd.tensor_tensor(conv_in[:, 0], conv_in[:, 0], conv_in[:, 2], ALU.add))
            if n:
                pool.wait_ge(conv_stored, 16 * n)
            nc.gpsimd.tensor_tensor(conv_out[:], conv_in[:, 0], w[3], ALU.add).then_inc(conv_done, 1)
            pool.wait_ge(conv_done, n + 1)
            pool.dma_start(conv_dram[n], conv_out[:].rearrange("p t n -> p (t n)")).then_inc(conv_stored, 16)
            if n < 5:
                load_conv_w(n + 1)
            if n == 4:
                load_block(2, hy_x[1][:], hy_x_in[1])
        load_block(3, hy_v[1][:], hy_v_in)
        pool.wait_ge(mod_ready, 3)
        start_acc(4)
        for n in range(1, 4):
            pool.wait_ge(hy_prod, n)
            load_spec(n)
            pool.wait_ge(hy_gated, n)
            load_skip(n)
            if n == 1:
                pool.wait_ge(conv_stored, 96)
                load_block(4, hy_x[0][:], hy_x_in[0])
            if n == 2:
                load_block(5, hy_x[1][:], hy_x_in[1])
        for i in range(4):
            if i >= 2:
                pool.wait_ge(mix_ready, i - 1)
            if i < 2:
                pool.wait_ge(hy_prod if i == 0 else hy_gated, 4)
                pool.wait_ge(gate_stored[i], 48)
            if i == 2:
                for g in range(2):
                    pool.wait_ge(gate_stored[g], 64)
            for g in range(2):
                pool.dma_start(gate_in[i % 2][:, g],
                               gate_dram[:, g * D + i * CH:g * D + (i + 1) * CH].rearrange("(t p) n -> p t n", p=P)) \
                    .then_inc(gate_loaded[i % 2], 16)
        pool.dma_start(bias_o[:], a["b_o"][0].partition_broadcast(P)).then_inc(bias_o_in, 16)
        pool.wait_ge(half_used, end(ST["mix"]))
        pool.dma_start(res[:], a["x"][0].rearrange("(t p) n -> p t n", p=P)).then_inc(x_again, 16)
        pool.wait_ge(fm_full, 12)
        pool.wait_ge(mix_ready, 4)
        pool.dma_start(ln_g[:], a["ln1_g"][0].partition_broadcast(P)).then_inc(ln_consts, 16)
        pool.dma_start(ln_b[:], a["ln1_b"][0].partition_broadcast(P)).then_inc(ln_consts, 16)

        def pre_add(bias, gate, ready):
            then(nc.gpsimd.tensor_tensor(bias[:], bias[:], gate[:], ALU.mult))
            for t in range(2):
                then(nc.gpsimd.tensor_scalar(res[:, t], res[:, t], ALPHA, 1.0, ALU.mult, ALU.mult))
                nc.gpsimd.tensor_tensor(res[:, t], res[:, t], bias[:], ALU.add).then_inc(pre_ready, 1)
        pool.wait_ge(mod_ready, 4)
        pool.wait_ge(bias_o_in, 16)
        pool.wait_ge(x_again, 16)
        pre_add(bias_o, acc[0], 0)
        pool.wait_ge(ln_consts, 32)
        pool.wait_ge(wide_empty, 2)
        start_acc(5)
        for t in range(2):
            pool.wait_ge(normed_ready, t + 1)
            then(nc.gpsimd.tensor_tensor(res[:, t], normed[:, t], ln_g[:], ALU.mult))
            nc.gpsimd.tensor_tensor(res[:, t], res[:, t], ln_b[:], ALU.add).then_inc(x1_ready, 1)
        pool.wait_ge(x1_ready, 2)
        pool.wait_ge(fm_lo, 16)
        pool.dma_start(bias_ff[:], a["b_m2"][0].partition_broadcast(P)).then_inc(bias_ff_in, 16)
        pool.wait_ge(g2_ready, 1)
        pool.wait_ge(bias_ff_in, 16)
        pre_add(bias_ff, acc[0], 2)
        pool.wait_ge(fm_lo, 20)
        pool.dma_start(ln2_g[:], a["ln2_g"][0].partition_broadcast(P)).then_inc(ln2_in, 16)
        pool.dma_start(ln2_b[:], a["ln2_b"][0].partition_broadcast(P)).then_inc(ln2_in, 16)
        pool.wait_ge(wide_empty, 4)
        pool.dma_start(pool_m[:], a["k_pool"].rearrange("g (t p) n -> p g t n", p=P)).then_inc(pool_in, 16)
        pool.wait_ge(normed_ready, 4)
        pool.dma_start(post_g[:], a["post_norm_2"][0].partition_broadcast(P)).then_inc(post_in[0], 16)
        pool.wait_ge(fm_full, 44)
        pool.dma_start(p_tm[:].rearrange("p (l t) n -> p l t n", t=2),
                       a["p_2"][:, 0].rearrange("l (t p) n -> p l t n", p=P)).then_inc(p_loaded, 16)
        pool.wait_ge(half_used, ST["w_ukv"].half(0, 7) + 2)
        then(nc.gpsimd.memset(mask[:], 0.0))
        for b in (0, 2):
            nc.gpsimd.affine_select(out=mask[:, b], in_=mask[:, b], compare_op=ALU.is_ge, fill=NEG, base=0,
                                    pattern=[[-1, P]], channel_multiplier=1).then_inc(mask_ready, 1)
        for g in range(2):
            pool.wait_ge(mla_gate_stored[g], 32)
        pool.dma_start(g_tm[:], gate_dram[:, 0:D].rearrange("(t p) n -> p t n", p=P)).then_inc(g_loaded, 16)
        pool.wait_ge(fm_full, 67)
        pool.dma_start(post_g1[:], a["post_norm_2"][1].partition_broadcast(P)).then_inc(post_in[1], 16)

    @block.tensor
    def _(pe):
        mm = nc.tensor.matmul

        def products(st, i, j, half, kt, hi, lo, banks, first, last, tiles=(0, 1)):
            slot = st.half_slot(j, half)
            pe.wait_ge(lo_split, st.half(i, j) + half + 1)
            for c in range(2):
                wh, wl = (w[slot][:, c * CH:(c + 1) * CH] for w in (w_hi, w_lo))
                k = kt + c if isinstance(kt, int) else kt[0]
                start, stop = (first and c == 0, last and c == 1) if isinstance(kt, int) else (first, last)
                for t in tiles:
                    bank = banks(c, t)
                    xh, xl = (x[:, k, t * P:(t + 1) * P] for x in (hi, lo))
                    mm(bank, xh, wl, start=start, stop=False)
                    mm(bank, xh, wh, start=False, stop=False)
                    ins = mm(bank, xl, wh, start=False, stop=stop)
            if 1 in tiles:
                ins.then_inc(half_used, 1)
            elif last and half == 1:
                ins.then_inc(first_done, 1)

        def pair(m):
            return lambda c, t: ps[:, 2 * m + t, :]

        def wide(half):
            return lambda c, t: ps[:, 4 * t + 2 * half + c, :]

        def chunk(st, i, c, m, m_static, hi, lo, kts=KT):
            j = sum(len(f + r) for f, r in st.chunks[:c])
            if not isinstance(m, int) or m >= 2:
                pe.wait_ge(pair_empty, m - 1)
            kt = 0
            for kind in "".join(st.chunks[c]):
                if kind == "w":
                    for half in range(2):
                        products(st, i, j, half, kt, hi, lo, pair(m_static % 2), kt == 0, kt + 2 == kts)
                        kt += 2
                j += 1

        def turn(g, src, q, slot=None):
            slot = g % 2 if slot is None else slot
            if not isinstance(g, int) or g >= 2:
                pe.wait_ge(fm_empty, g - 1)
            for k in range(4):
                for t in range(2):
                    ins = nc.tensor.transpose(fm_ps[slot][:, k, t * P:(t + 1) * P],
                                              src[:, t, (4 * q + k) * P:(4 * q + k + 1) * P], ident[:])
            ins.then_inc(fm_full, 1)

        def wide_products(st, s, hi, lo, kts, jit=False, kt0=0):
            def body(i):
                j = 0
                for c, kinds in enumerate(st.chunks):
                    n = i * len(st.chunks) + c
                    if s is not None:
                        pe.wait_ge(fm_lo, n + s + 1)
                    ends = isinstance(i, int) and i == st.rounds - 1 and c == len(st.chunks) - 1
                    kinds = "".join(kinds)
                    loads = [q for q, kind in enumerate(kinds) if kind == "w"]
                    whole = len(loads) - 2 * ends
                    for q, tiles in ([(q, (0, 1)) for q in range(whole)] +
                                     [(q, (t,)) for t in range(2) for q in range(whole, len(loads))]):
                        kt = 4 * (c % 2) + q if jit else kt0 + 4 * n + q
                        for half in range(2):
                            products(st, i, j + loads[q], half, [kt], hi, lo, wide(half),
                                     isinstance(i, int) and i == 0 and j + q == 0,
                                     ends and q == len(loads) - 1, tiles)
                    j += len(kinds)
            if jit:
                rounds(pe, st, body, last=True)
            else:
                for i in range(st.rounds):
                    body(i)

        def turn_heads(g, q):
            pe.wait_ge(fm_empty, g - 1)
            for k in range(4):
                for t in range(2):
                    ins = nc.tensor.transpose(fm_ps[g % 2][:, k, t * P:(t + 1) * P],
                                              q_tm[:, t, 4 * q + k, 0:VD], ident[:])
            ins.then_inc(fm_full, 1)

        pe.wait_ge(vectors_in, 16 * N_VECTORS)
        nc.tensor.transpose(ps[:, 4, 0:P], rows_a[:], ident[:])
        nc.tensor.transpose(ps[:, 4, P:2 * P], rows_b[:], ident[:])
        pe.wait_ge(pos_ready, 1)
        nc.tensor.transpose(ps[:, 4, 2 * P:2 * P + 2], pos_f[0:2, :], ident[0:2, 0:2]).then_inc(setup_tr, 1)
        pe.wait_ge(hidden_in, 64)
        mm(ps[0:HID, 0, 0:S], w1[0:EMB, :], feats[0:EMB, :], start=True, stop=True).then_inc(hid_mm, 1)
        pe.wait_ge(hid_sin, 1)
        mm(ps[0:HID, 0, 0:S], w2[0:HID, :], hid_arg[0:HID, :], start=True, stop=True).then_inc(hid_mm, 1)
        pe.wait_ge(matrices_in, 64)
        for g in range(8):
            ins = nc.tensor.transpose(ps[:, 5 + g // 4, (g % 4) * P:(g % 4 + 1) * P], sgu_raw[:, g], ident[:])
        ins.then_inc(sgu_turned, 1)
        pe.wait_ge(hid_sin, 2)
        pe.wait_ge(vectors_out, 1)
        pe.wait_ge(sgu_wT_out, 1)
        for it in range(4):
            o, c = it // 2, it % 2
            if it:
                pe.wait_ge(filt_win, it)
            for d in range(2):
                for t in range(2):
                    col = (2 * d + o) * W1 + c * CH
                    ins = mm(ps[:, 4 + 2 * d + t, :], hid_arg[0:HID, t * P:(t + 1) * P], w3[0:HID, col:col + CH],
                             start=True, stop=True)
            ins.then_inc(filt_mm, 1)
            pe.wait_ge(filt_sum, it + 1)
            if it:
                pe.wait_ge(spec_copied, it)
            for m, src in ((0, h_sum), (1, h_bwd)):
                for f in range(2):
                    for t in range(2):
                        ins = mm(ps[:, 2 * m + f, :], dft[:, m, t, f * P:(f + 1) * P], src[:, t, :],
                                 start=t == 0, stop=t == 1)
            ins.then_inc(spec_mm, 1)
        pe.wait_ge(x_loaded, 16)
        pe.wait_ge(filt_win, 4)
        turn(0, res, 0)
        turn(1, res, 1)

        def ada_sum(b, bank):
            pe.wait_ge(ada_added, 16 * (b + 1))
            for k in range(KT):
                ins = mm(ps[:, bank, k:k + 1], acc[ADA_ACC[b]][:, k * P:(k + 1) * P], ones[:, 0:1],
                         start=True, stop=True)
            ins.then_inc(ada_summed, 1)

        pe.wait_ge(spec_copied, 4)
        pe.wait_ge(ones_set, 2)
        ada_sum(0, 0)
        ada_sum(1, 1)
        turn(2, res, 2)
        turn(3, res, 3)

        def first_chunk(st, groups, kts=KT):
            for g in range(4):
                pe.wait_ge(fm_lo, groups + g + 1)
                for half in range(2):
                    products(st, 0, FIRST[st][g], half, 4 * g + 2 * half, x_hi, x_lo, pair(0),
                             g == 0 and half == 0, g == 3 and half == 1)

        FIRST = {st: [j for j, k in enumerate(st.pattern) if k == "w"][:4] for st in ST.values()}

        st = ST["in_vu"]
        pe.wait_ge(mod_ready, 2)
        first_chunk(st, 0)
        chunk(st, 0, 1, 1, 1, x_hi, x_lo)
        chunk(st, 1, 0, 2, 2, x_hi, x_lo)
        chunk(st, 1, 1, 3, 3, x_hi, x_lo)
        st = ST["in_h"]
        for i in range(2):
            for c in range(2):
                chunk(st, i, c, 4 + 2 * i + c, c, x_hi, x_lo)
        pe.wait_ge(vn_ready, 2)
        for t in range(2):
            for g in range(8):
                ins = mm(ps[:, 4 + 2 * t + g // 4, (g % 4) * P:(g % 4 + 1) * P], sgu_wT[:, g],
                         vu[:, 0, t, g * P:(g + 1) * P], start=True, stop=True)
            ins.then_inc(sgu_mm, 1)
        st = ST["in_h2"]
        for c in range(2):
            chunk(st, 0, c, 8 + c, c, x_hi, x_lo)
        pe.wait_ge(sgu_out, 1)
        turn(4, vu[:, 1], 0)
        turn(5, vu[:, 1], 1)
        pe.wait_ge(fm_empty, 5)
        ada_sum(2, 4)

        def forward(n):
            b, o = n // 2, n % 2
            if n == 0:
                pe.wait_ge(mod_ready, 3)
                pe.wait_ge(fm_empty, 6)
            else:
                pe.wait_ge(hy_gated, n)
            if o == 0:
                pe.wait_ge(hy_v_in, 16 * (b + 1))
            for m in range(2):
                for f in range(2):
                    for t in range(2):
                        ins = mm(ps[:, 4 + 2 * m + f, :], dft[:, m, t, f * P:(f + 1) * P], hy_v[b][:, t, :],
                                 start=t == 0, stop=t == 1)
            ins.then_inc(hy_f, 1)

        def inverse(n):
            pe.wait_ge(hy_prod, n + 1)
            for t in range(2):
                for m in range(2):
                    for f in range(2):
                        ins = mm(ps[:, 4 + t, :], dft[:, 2 + m, f, t * P:(t + 1) * P], prod[:, 2 * m + f, :],
                                 start=m + f == 0, stop=m + f == 2)
            ins.then_inc(hy_i, 1)

        st = ST["in_g"]
        for n in range(8):
            chunk(st, n // 2, n % 2, 10 + n, n, x_hi, x_lo)
            if n % 2 == 0:
                forward(n // 2)
            else:
                inverse(n // 2)
        turn(6, hy_v[0], 0, slot=1)

        st = ST["mix"]
        pe.wait_ge(fm_lo, 6)
        for i in range(4):
            chunk(st, 0, 2 * i, i * 2 + 18, 0, ya_hi, ya_lo, W1 // P)
            if i == 0:
                pe.wait_ge(hy_gated, 4)
                turn(7, hy_v[1], 0, slot=0)
                pe.wait_ge(fm_lo, 8)
            chunk(st, 0, 2 * i + 1, i * 2 + 19, 1, yb_hi, yb_lo, W1 // P)
            if i:
                pe.wait_ge(mix_ready, i)
                turn(8 + i - 1, mixed[(i - 1) % 2], 0)
        pe.wait_ge(mix_ready, 4)
        turn(11, mixed[1], 0)
        pe.wait_ge(pair_empty, 26)
        pe.wait_ge(ada_added, 16 * 4)
        for n in range(4):
            ins = mm(ps[:, n, :], ones_m[:], acc[0][:, n * CH:(n + 1) * CH], start=True, stop=True)
        ins.then_inc(ada_summed, 1)

        st = ST["w_o"]
        pe.wait_ge(mod_ready, 4)
        pe.wait_ge(fm_empty, 12)
        wide_products(st, 8, x_hi, x_lo, KT)
        pe.wait_ge(wide_empty, 1)
        ada_sum(4, 3)

        pe.wait_ge(normed_ready, 2)
        for q in range(4):
            turn(12 + q, normed, q)
        st = ST["m1a"]
        pe.wait_ge(mod_ready, 5)

        def m1_round(st, before):
            def body(i):
                for c in range(2):
                    n = i * 2 + (before + c)
                    if isinstance(n, int) and n == 0:
                        first_chunk(st, 12)
                    else:
                        chunk(st, i, c, n + 26, c, x_hi, x_lo)
                    if not isinstance(n, int) or n > 0:
                        pe.wait_ge(pair_empty, n + 26)
                        turn(n + 15, ff_stage[1 - c], 0, slot=(1 + c) % 2)
            return body
        rounds(pe, st, m1_round(st, 0))
        rounds(pe, ST["m1b"], m1_round(ST["m1b"], 8))
        pe.wait_ge(pair_empty, 42)
        turn(31, ff_stage[1], 0)
        pe.wait_ge(ada_added, 96)
        for n in range(4):
            ins = mm(ps[:, n, :], ones_m[:], acc[0][:, n * CH:(n + 1) * CH], start=True, stop=True)
        ins.then_inc(ada_summed, 1)
        pe.wait_ge(g2_ready, 1)
        pe.wait_ge(fm_empty, 32)
        wide_products(ST["m2"], 16, x_hi, x_lo, FF // P, jit=True)

        pe.wait_ge(normed_ready, 4)
        for q in range(4):
            turn(32 + q, normed, q)
        st = ST["pool_u"]

        def pool_turn(g, n_group, c):
            pe.wait_ge(fm_empty, g - 1)
            slot = (g % 2) if isinstance(g, int) else c
            u = u_stage[c]
            for k in range(4):
                f = slice(k * P, (k + 1) * P)
                m = pool_m[:, ds(n_group, 1)].rearrange("p a t s -> p (a t) s")
                mm(fm_ps[slot][:, k, 0:P], u[:, 0, f], m[:, 0, 0:P], start=True, stop=True)
                mm(fm_ps[slot][:, k, P:S], u[:, 0, f], m[:, 0, P:S], start=True, stop=False)
                ins = mm(fm_ps[slot][:, k, P:S], u[:, 1, f], m[:, 1, P:S], start=False, stop=True)
            ins.then_inc(fm_full, 1)

        def pool_u_round(i):
            for c in range(2):
                n = i * 2 + c
                if isinstance(n, int) and n == 0:
                    first_chunk(st, 32)
                    pe.wait_ge(pool_in, 16)
                else:
                    chunk(st, i, c, n + 42, c, x_hi, x_lo)
                    pe.wait_ge(pair_empty, n + 42)
                    pool_turn(n + 35, i if c else i - 1, 1 - c)
        rounds(pe, st, pool_u_round)
        pe.wait_ge(pair_empty, 50)
        pool_turn(43, 3, 1)
        st_g = ST["pool_g"]

        def pool_g_round(i):
            pe.wait_ge(fm_lo, i * 2 + 38)
            for c in range(4):
                m = i * 4 + (50 + c)
                if c % 2 == 0:
                    chunk(st_g, i, c, m, c, g_hi, g_lo, 8)
                else:
                    chunk(st_g, i, c, m, c, x_hi, x_lo)
                    if c == 3 or not isinstance(i, int) or i > 0:
                        n = i * 2 + (0 if c == 3 else -1)
                        pe.wait_ge(product_ready, n + 1)
                        turn(n + 44, pool_stage[0 if c == 3 else 1], 0, slot=0 if c == 3 else 1)
        rounds(pe, st_g, pool_g_round)
        pe.wait_ge(product_ready, 8)
        turn(51, pool_stage[1], 0)
        pe.wait_ge(p_loaded, 16)
        pe.wait_ge(fm_empty, 51)
        for layer in range(2):
            for k in range(2):
                for t in range(2):
                    ins = nc.tensor.transpose(fm_ps[0][:, 2 * layer + k, t * P:(t + 1) * P],
                                              p_tm[:, 2 * layer + t, k * P:(k + 1) * P], ident[:])
        ins.then_inc(fm_full, 1)
        pe.wait_ge(pair_empty, 66)
        pe.wait_ge(fm_empty, 53)
        wide_products(ST["pool_out"], 45, x_hi, x_lo, E_POOL // P, jit=True)
        pe.wait_ge(wide_empty, 6)
        wide_products(ST["proj0"], None, p_hi, p_lo, 2)
        pe.wait_ge(wide_empty, 7)
        pe.wait_ge(proj_out, 1)
        pe.wait_ge(normed_ready, 6)
        for q in range(4):
            turn(53 + q, normed, q)
        pe.wait_ge(fm_empty, 57)
        wide_products(ST["gate0"], 53, x_hi, x_lo, KT)

        pe.wait_ge(wide_empty, 9)
        pe.wait_ge(normed_ready, 8)
        for q in range(4):
            turn(57 + q, normed, q)
        st = ST["mla_in"]
        first_chunk(st, 57)
        for n in range(1, 6):
            chunk(st, n // 2, n % 2, 66 + n, n, x_hi, x_lo)
        st = ST["k_pe"]
        pe.wait_ge(pair_empty, 71)
        for half in range(2):
            pe.wait_ge(lo_split, st.half(0, 0) + half + 1)
            slot = st.half_slot(0, half)
            for q in range(8):
                wh, wl = (w[slot][:, q * ROPE:(q + 1) * ROPE] for w in (w_hi, w_lo))
                k = 8 * half + q
                for t in range(2):
                    xh, xl = (x[:, k, t * P:(t + 1) * P] for x in (x_hi, x_lo))
                    bank = ps[:, t, 0:ROPE]
                    mm(bank, xh, wl, start=k == 0, stop=False)
                    mm(bank, xh, wh, start=False, stop=False)
                    ins = mm(bank, xl, wh, start=False, stop=k == KT - 1)
            ins.then_inc(half_used, 1)
        pe.wait_ge(lat_ready, 2)
        for which in range(2):
            turn(61 + which, lat[:, :, which], 0)
        for name, which, kts, m in (("w_uq", 0, 6, 73), ("w_ukv", 1, 8, 79)):
            st = ST[name]
            pe.wait_ge(fm_lo, 62 + which)
            for n in range(kts):
                pe.wait_ge(pair_empty, m + n - 1)
                for half in range(2):
                    products(st, 0, n, half, 4 * which + 2 * half, x_hi, x_lo, pair((m + n) % 2),
                             half == 0, half == 1)

        def head_turn(h):
            if h >= 2:
                pe.wait_ge(qk_out, h - 1)
            for t in range(2):
                nc.tensor.transpose(ps[:, h % 2, t * P:(t + 1) * P], q_tm[:, t, h, 0:NOPE], ident[:])
                nc.tensor.transpose(ps[:, h % 2, (2 + t) * P:(3 + t) * P], kv_tm[:, t, h, 0:NOPE], ident[:])
            if h >= 1:
                pe.wait_ge(qpe_out, h)
            for t in range(2):
                ins = nc.tensor.transpose(ps[0:ROPE, 2, t * P:(t + 1) * P], q_tm[:, t, h, NOPE:QK],
                                          ident[:])
            ins.then_inc(qk_turned, 1)

        def head_score(h):
            pe.wait_ge(qk_out, h + 1)
            pe.wait_ge(qpe_out, h + 1)
            if h >= 2:
                pe.wait_ge(score_ready, h - 1)
            qk, qp = qk_fm[h % 2], q_peT[h % 2]
            for t in range(2):
                keys = slice(0, (t + 1) * P)
                bank = ps[:, 3 + h % 2, t * P:(2 * t + 1) * P]
                mm(bank, qk[:, 0, t * P:(t + 1) * P], qk[:, 1, keys], start=True, stop=False)
                ins = mm(bank, qp[0:ROPE, t * P:(t + 1) * P], k_peT[0:ROPE, keys], start=False, stop=True)
            ins.then_inc(scored, 1)

        def head_prob(h):
            pe.wait_ge(prob_ready, 2 * (h + 1))
            if h >= 2:
                pe.wait_ge(probT_out, h - 1)
            for b in range(3):
                ins = nc.tensor.transpose(ps[:, 5 + h % 2, b * P:(b + 1) * P], prob[h % 2][:, b], ident[:])
            ins.then_inc(prob_turned, 1)

        def head_value(h):
            pe.wait_ge(probT_out, h + 1)
            if h >= 1:
                pe.wait_ge(o_ready, h)
            v = kv_tm[:, :, h, NOPE:NOPE + VD]
            pt = probT[h % 2]
            mm(ps[:, 7, 0:P], pt[:, 0], v[:, 0], start=True, stop=True)
            mm(ps[:, 7, P:2 * P], pt[:, 1], v[:, 0], start=True, stop=False)
            mm(ps[:, 7, P:2 * P], pt[:, 2], v[:, 1], start=False, stop=True).then_inc(o_mm, 1)

        pe.wait_ge(pair_empty, 87)
        pe.wait_ge(fm_empty, 63)
        for t in range(2):
            ins = nc.tensor.transpose(ps[0:ROPE, 7, t * P:(t + 1) * P], k_pe[:, t, :], ident[:])
        ins.then_inc(k_peT_ready, 1)
        for step in range(HEADS + 3):
            if step < HEADS:
                head_turn(step)
            if step == 0:
                pe.wait_ge(k_peT_out, 1)
            if 0 <= step - 1 < HEADS:
                head_score(step - 1)
            if 0 <= step - 2 < HEADS:
                head_prob(step - 2)
            if 0 <= step - 3 < HEADS:
                head_value(step - 3)
        pe.wait_ge(o_ready, HEADS)
        for q in range(4):
            turn_heads(63 + q, q)
        pe.wait_ge(fm_empty, 67)
        wide_products(ST["w_out"], 63, x_hi, x_lo, KT)
        pe.wait_ge(wide_empty, 11)
        wide_products(ST["proj1"], None, p_hi, p_lo, 2, kt0=2)
        pe.wait_ge(wide_empty, 12)
        pe.wait_ge(proj_out, 2)
        pe.wait_ge(normed_ready, 10)
        for q in range(4):
            turn(67 + q, normed, q)
        pe.wait_ge(fm_empty, 71)
        wide_products(ST["gate1"], 67, x_hi, x_lo, KT)

    @block.scalar
    def _(act):
        steps = [0]

        def then(ins):
            steps[0] += 1
            ins.then_inc(s_step, 1)
            act.wait_ge(s_step, steps[0])

        def round_unit(st, i, j):
            for half in range(2):
                h = st.half(i, j) + half
                if half == 0:
                    act.wait_ge(raw_full[st.slot(j)], st.landed(i, j))
                if not isinstance(h, int) or h >= SLOTS:
                    act.wait_ge(half_used, h - (SLOTS - 1))
                n = st.size // 2
                nc.scalar.copy(w_hi[st.half_slot(j, half)][:, 0:n], raw[st.slot(j)][:, half * n:(half + 1) * n]) \
                    .then_inc(hi_split, 1)

        def run(st, i, hook, before=None):
            j = 0
            if before and isinstance(i, int) and i == 0:
                before()
            for c, (front, rest) in enumerate(st.chunks):
                for n, kind in enumerate(front + rest):
                    if n == len(front):
                        hook(i, c)
                    if kind == "w":
                        round_unit(st, i, j)
                    j += 1
                if not rest:
                    hook(i, c)

        def no(i, c):
            pass

        def group(g, s, hi, read):
            group_read(g, s, read)
            group_round(g, s, hi)

        def group_read(g, s, read):
            y = y_fm[s % 2]
            act.wait_ge(fm_full, g + 1)
            if s >= 2:
                act.wait_ge(fm_lo, s - 1)
            ps_g = fm_ps[1 - g % 2 if g in (6, 7) else g % 2]
            if read is None:
                ins = nc.scalar.copy(y[:], ps_g)
            else:
                for k in range(4):
                    ins = read(k, y[:, k], ps_g[:, k])
            ins.then_inc(fm_empty, 1)

        def group_round(g, s, hi):
            act.wait_ge(fm_empty, g + 1)
            nc.scalar.copy(hi, y_fm[s % 2][:]).then_inc(fm_hi, 1)

        def affine(scale, bias, q):
            def read(k, o, i):
                n = 4 * q + k
                if bias is None:
                    return nc.scalar.activation(o, i, ACT.Copy, scale=scale[:, n:n + 1])
                return nc.scalar.activation(o, i, ACT.Identity, scale=scale[:, n:n + 1], bias=bias[:, n:n + 1])
            return read

        def rows(name):
            return a[name].rearrange("a (k p) -> (a k) p", p=P)

        vectors = [
            (ident[:], a["k_ident"]), (rows_a[0:64, :], rows("b_m1")), (rows_a[64:96, :], rows("pre_norm_2")),
            (rows_a[96:128, :], rows("ple_norm_2")), (pos_i[0:2, :], rows("positions_2")),
            (rows_b[0:32, :], rows("pool_scale_2")), (rows_b[32:36, :], rows("mla_q_norm_2")),
            (rows_b[36:40, :], rows("mla_kv_norm_2")), (rows_b[40:48, :], a["sgu_b"][0]),
            (rows_b[48:64, :], rows("c")), (rows_b[64:80, :], rows("ln1_g")), (rows_b[80:96, :], rows("ln1_b")),
            (rows_b[96:97, 0:HID], a["hy_b1"]), (rows_b[97:98, 0:HID], a["hy_b2"]),
            (rows_b[98:99, 0:HID], a["hy_freq"]),
        ]
        matrices = [
            (feats[0:EMB, :], a["k_feats"]), (w1[0:EMB, :], a["hy_w1"][0]), (w2[0:HID, :], a["hy_w2"][0]),
            (freq[:], a["k_freq"][0].partition_broadcast(P)), (w3[0:HID, :], a["hy_w3"][0]),
            (sgu_raw[:], a["sgu_w"][0].rearrange("g q p -> q g p")),
            (window[:], a["k_window"].rearrange("(t p) n -> p t n", p=P)),
            (dft[:], a["k_dft"].rearrange("m (t p) n -> p m t n", p=P)),
        ]
        assert len(vectors) == N_VECTORS
        act.wait_ge(rows_zeroed, 1)
        for dst, src in vectors:
            act.dma_start(dst, src).then_inc(vectors_in, 16)
        for n, (dst, src) in enumerate(matrices):
            act.dma_start(dst, src).then_inc(hidden_in if n < 4 else matrices_in, 16)

        act.wait_ge(vectors_out, 1)
        nc.scalar.activation(sig_c[:], fm_b[:, COL["c"]:COL["c"] + KT], ACT.Sigmoid).then_inc(c_sig, 1)
        for layer in range(2):
            act.wait_ge(hid_red, layer + 1)
            nc.scalar.activation(hid_arg[0:HID, :], hid_arg[0:HID, :], ACT.Sin).then_inc(hid_sin, 1)
        act.wait_ge(sgu_turned, 1)
        nc.scalar.copy(sgu_wT[:].rearrange("p g q -> p (g q)"),
                       ps[:, 5:7, :].rearrange("p a n -> p (a n)")).then_inc(sgu_wT_out, 1)
        act.wait_ge(angles, 1)
        for table in (rope_cos, rope_sin):
            nc.scalar.activation(table[:], table[:], ACT.Sin).then_inc(sines, 1)
        for it in range(4):
            act.wait_ge(spec_mm, it + 1)
            if it:
                act.wait_ge(spec_stored, 16 * it)
            nc.scalar.copy(spec_out[:].rearrange("p a n -> p (a n)"), ps[:, 0:4, :].rearrange("p a n -> p (a n)")) \
                .then_inc(spec_copied, 1)
            act.wait_ge(spec_copied, it + 1)
            act.dma_start(spec_dram[it // 2, it % 2], spec_out[:].rearrange("p a n -> p (a n)")) \
                .then_inc(spec_stored, 16)
        act.wait_ge(mod_ready, 2)
        for q in range(4):
            group(q, q, x_hi[:, 4 * q:4 * q + 4, :], affine(mod[:, 1], mod[:, 0], q))

        def gelu(n):
            act.wait_ge(pair_empty, n + 1)
            part = vu[:, n // 2, :, (n % 2) * CH:(n % 2 + 1) * CH]
            nc.scalar.activation(part, part, ACT.Gelu).then_inc(gelu_done, 1)

        st = ST["in_vu"]
        for i in range(2):
            run(st, i, lambda i, c: gelu(2 * i + c - 1) if i or c else None)

        def zh_store(n):
            col = IN_COLS[4 + n] - 2 * W1
            act.wait_ge(pair_empty, 4 + n + 1)
            act.dma_start(zh_dram[1:S + 1, col:col + CH].rearrange("(t p) n -> p t n", p=P), zh_out[n % 2][:]) \
                .then_inc(zh_stored[n % 2], 16)

        def sgu_std(i, c):
            n = 2 * i + c
            if n == 0:
                gelu(3)
            else:
                zh_store(n - 1)
            if n == 2:
                act.wait_ge(var_ready, 1)
                nc.scalar.activation(rstd[:, 0], rstd[:, 0], ACT.Sqrt).then_inc(std_ready, 1)
        st = ST["in_h"]
        for i in range(2):
            run(st, i, sgu_std)
        run(ST["in_h2"], 0, lambda i, c: zh_store(3 + c))

        def gate(n):
            act.wait_ge(pair_empty, 10 + n + 1)
            nc.scalar.activation(gate_out[n % 2][:], gate_out[n % 2][:], ACT.Sigmoid).then_inc(gate_sig, 1)
            act.wait_ge(gate_sig, n + 1)
            act.dma_start(gate_dram[:, n * CH:(n + 1) * CH].rearrange("(t p) n -> p t n", p=P), gate_out[n % 2][:]) \
                .then_inc(gate_stored[n % 2], 16)

        def in_g(i, c):
            n = 2 * i + c
            if n == 0:
                zh_store(5)
                for q in range(2):
                    group_read(4 + q, 4 + q, None)
            else:
                gate(n - 1)
            if n == 3:
                act.wait_ge(conv_stored, 96)
                for q in range(2):
                    group_round(4 + q, 4 + q, ya_hi[:, 4 * q:4 * q + 4, :])
        st = ST["in_g"]
        for i in range(4):
            run(st, i, in_g)
        gate(7)

        def mix_hook(_, c):
            if c < 2:
                group(6 + c, 6 + c, yb_hi[:, 4 * c:4 * c + 4, :], None)
            elif c % 2 == 0 and c >= 4:
                i = c // 2 - 2
                group(8 + i, 8 + i, x_hi[:, 4 * i:4 * i + 4, :], None)
        run(ST["mix"], 0, mix_hook)
        st = ST["w_o"]
        run(st, 0, lambda i, c: [group(g, g, x_hi[:, 4 * (g - 8):4 * (g - 7), :], None) for g in (10, 11)]
            if c == 0 else None)
        run(st, 1, no)

        sums = [0]

        def root(t, src):
            sums[0] += 1
            nc.scalar.activation(normed[:, t], src, ACT.Square, accum_out=ss[:, t, 0:1]).then_inc(squares, 1)
            act.wait_ge(squares, sums[0])
            nc.scalar.activation(ss[:, t, 1:2], ss[:, t, 0:1], ACT.Sqrt, scale=1.0 / D, bias=eps[:, 0:1]) \
                .then_inc(roots, 1)

        def root_of_var(n):
            for t in range(2):
                act.wait_ge(var_ready, n + t + 1)
                nc.scalar.activation(rstd[:, 0, t:t + 1], mv[:, t, 1:2], ACT.Sqrt, bias=eps[:, 1:2]) \
                    .then_inc(std_ready, 1)

        def root_of_res(n):
            for t in range(2):
                act.wait_ge(res_ready, n + t + 1)
                root(t, res[:, t])

        def four_groups(g, scale, bias):
            for q in range(4):
                group(g + q, g + q, x_hi[:, 4 * q:4 * q + 4, :], affine(scale, bias, q))

        def relu2(n, c):
            wait_apart(act, fm_full, n + 17)
            for k in range(4):
                ins = nc.scalar.activation(ff[:, ds(n * 4 + k, 1)], fm_ps[c][:, k:k + 1], ACT.Relu,
                                           bias=fm_a[:, ds(n * 4 + k, 1)])
            ins.then_inc(fm_empty, 1)
            wait_apart(act, fm_empty, n + 17)
            nc.scalar.activation(ff[:, ds(n * 4, 4)], ff[:, ds(n * 4, 4)], ACT.Square).then_inc(ff_ready, 1)

        def m1_hook(base):
            def hook(i, c):
                if base == 0 and isinstance(i, int) and i == 0:
                    if c == 0:
                        four_groups(12, mod[:, 4], mod[:, 5])
                        act.wait_ge(x1_ready, 2)
                    return
                relu2(i * 2 + (base + c - 2), c)
            return hook
        rounds(act, ST["m1a"], lambda i: run(ST["m1a"], i, m1_hook(0), lambda: root_of_var(1)))
        rounds(act, ST["m1b"], lambda i: run(ST["m1b"], i, m1_hook(8)))

        def jit(src, n, c):
            nc.scalar.copy(x_hi[:, 4 * c:4 * c + 4], src[:, ds(n * 4, 4)]).then_inc(fm_hi, 1)

        def m2_hook(i, c):
            if isinstance(i, int) and i == 0 and c == 0:
                relu2(14, 0)
                jit(ff, 0, 0)
                relu2(15, 1)
            if not (isinstance(i, int) and i == 7 and c == 1):
                wait_apart(act, ff_ready, i * 2 + (c + 2))
                jit(ff, i * 2 + (c + 1), 1 - c)
        rounds(act, ST["m2"], lambda i: run(ST["m2"], i, m2_hook), last=True)

        def pool_copy(n, c):
            wait_apart(act, fm_full, n + 37)
            nc.scalar.copy(pooled[:, ds(n * 4, 4)], fm_ps[c]).then_inc(fm_empty, 1)

        def pool_u_hook(i, c):
            if isinstance(i, int) and i == 0:
                if c == 0:
                    four_groups(32, fm_a[:, 64:80], None)
                return
            pool_copy(i * 2 + (c - 2), c)

        def m2_norms():
            root_of_var(3)
            root_of_res(0)
        rounds(act, ST["pool_u"], lambda i: run(ST["pool_u"], i, pool_u_hook, m2_norms))

        def jit_group(i):
            for c in range(2):
                nc.scalar.copy(g_hi[:, 4 * c:4 * c + 4], pooled[:, ds(i * 8 + 4 * c, 4)]).then_inc(fm_hi, 1)

        def pool_sigmoid(i, c):
            n = i * 2 + c
            act.wait_ge(half_used, chunk_end(ST["pool_g"], i, 2 * c + 1))
            if not isinstance(n, int) or n >= 1:
                act.wait_ge(product_ready, n)
            nc.scalar.activation(pool_gate[:], ps[:, 2:4, :], ACT.Sigmoid).then_inc(silu_ready, 1)

        def pool_scaled(i, c):
            n = i * 2 + c
            act.wait_ge(fm_full, n + 45)
            wait_apart(act, fm_lo, i * 2 + 38)
            for k in range(4):
                ins = nc.scalar.activation(pooled[:, ds(n * 4 + k, 1)], fm_ps[c][:, k:k + 1], ACT.Copy,
                                           scale=fm_b[:, ds(n * 4 + (COL["pool_scale"] + k), 1)])
            ins.then_inc(fm_empty, 1)

        def pool_g_hook(i, c):
            first = isinstance(i, int) and i == 0
            if c == 0:
                if first:
                    pool_copy(6, 0)
                    jit_group(0)
                    pool_copy(7, 1)
                else:
                    pool_sigmoid(i - 1, 1)
                    pool_scaled(i - 1, 0)
            if c == 2:
                pool_sigmoid(i, 0)
                if not first:
                    pool_scaled(i - 1, 1)
            if c == 3 and not (isinstance(i, int) and i == 3):
                wait_apart(act, half_used, chunk_end(ST["pool_g"], i, 2))
                jit_group(i + 1)
        rounds(act, ST["pool_g"], lambda i: run(ST["pool_g"], i, pool_g_hook), last=True)

        def pool_out_hook(i, c):
            if isinstance(i, int) and i == 0 and c == 0:
                pool_sigmoid(3, 1)
                pool_scaled(3, 0)
                pool_scaled(3, 1)
                group(52, 44, p_hi[:], None)
                jit(pooled, 0, 0)
            if not (isinstance(i, int) and i == 3 and c == 1):
                jit(pooled, i * 2 + (c + 1), 1 - c)
        rounds(act, ST["pool_out"], lambda i: run(ST["pool_out"], i, pool_out_hook), last=True)

        def mixer_root(mixer, t):
            wait_product(act, mixer, t)
            root(t, wide_bank(t))

        def mixer_out(mixer, n, proj_st):
            mixer_root(mixer, 1)
            root_of_res(n)
            wait_product(act, proj_st, 0)
            nc.scalar.copy(proj[:, 0], wide_bank(0)).then_inc(proj_out, 1)

        def gate_sigmoid(st):
            for t in range(2):
                wait_product(act, st, t)
                nc.scalar.activation(tmp[:, t], wide_bank(t), ACT.Sigmoid).then_inc(gate_read, 1)

        run(ST["proj0"], 0, lambda i, c: mixer_out(ST["pool_out"], 2, ST["proj0"]),
            lambda: mixer_root(ST["pool_out"], 0))
        for i in range(2):
            run(ST["gate0"], i, lambda i, c: four_groups(53, fm_a[:, 96:112], None) if i + c == 0 else None)

        def mla_sigmoid(n):
            act.wait_ge(half_used, chunk_end(ST["mla_in"], n // 2, n % 2))
            if n >= 4:
                act.wait_ge(pair_empty, 66 + n - 1)
            nc.scalar.activation(mla_sig[n % 2][:], ps[:, 2 * (n % 2):2 * (n % 2) + 2, :], ACT.Sigmoid) \
                .then_inc(mla_silu, 1)

        def mla_gate_store(n):
            act.wait_ge(pair_empty, 66 + n + 1)
            act.dma_start(gate_dram[:, (n - 2) * CH:(n - 1) * CH].rearrange("(t p) n -> p t n", p=P),
                          mla_gate_out[n % 2][:]).then_inc(mla_gate_stored[n % 2], 16)

        def mla_in_hook(i, c):
            n = 2 * i + c
            if n == 0:
                four_groups(57, fm_a[:, 80:96], None)
            if n == 3:
                act.wait_ge(pair_empty, 68)
                for w in range(4):
                    ins = nc.scalar.activation(lat_junk[:, w], lat[:, w % 2, w // 2], ACT.Square,
                                               accum_out=lat_ss[:, 0, w:w + 1])
                then(ins)
                nc.scalar.activation(lat_ss[:, 1], lat_ss[:, 0], ACT.Sqrt, scale=1.0 / CH, bias=eps[:, 0:1]) \
                    .then_inc(lat_sq, 1)
            if n >= 3:
                mla_sigmoid(n - 1)
            if n >= 4:
                mla_gate_store(n - 2)

        def gate_norms():
            gate_sigmoid(ST["gate0"])
            root_of_res(4)
        for i in range(3):
            run(ST["mla_in"], i, mla_in_hook, gate_norms)

        def k_pe_hook(i, c):
            mla_sigmoid(5)
            mla_gate_store(4)
            mla_gate_store(5)
        run(ST["k_pe"], 0, k_pe_hook)

        def w_uq_hook(i, c):
            if c == 0:
                group(61, 61, x_hi[:, 0:4, :], affine(fm_b[:, COL["q_norm"]:COL["q_norm"] + 4], None, 0))
                group(62, 62, x_hi[:, 4:8, :], affine(fm_b[:, COL["kv_norm"]:COL["kv_norm"] + 4], None, 0))
        run(ST["w_uq"], 0, w_uq_hook)
        run(ST["w_ukv"], 0, no)

        def head_turned(h):
            act.wait_ge(qk_turned, h + 1)
            if h >= 2:
                act.wait_ge(scored, h - 1)
            nc.scalar.copy(qk_fm[h % 2][:].rearrange("p a s -> p (a s)"), ps[:, h % 2, :]).then_inc(qk_out, 1)

        def head_exp(h):
            act.wait_ge(score_ready, h + 1)
            if h >= 2:
                act.wait_ge(prob_turned, h - 1)
            for t in range(2):
                blocks = slice(t, 2 * t + 1)
                nc.scalar.activation(prob[h % 2][:, blocks], score[h % 2][:, blocks], ACT.Exp,
                                     bias=sm_max[:, h % 4, t:t + 1], accum_out=sm_sum[:, h % 4, t:t + 1]) \
                    .then_inc(prob_ready, 1)

        def head_probT(h):
            act.wait_ge(prob_turned, h + 1)
            if h >= 2:
                act.wait_ge(o_mm, h - 1)
            nc.scalar.copy(probT[h % 2][:].rearrange("p b k -> p (b k)"), ps[:, 5 + h % 2, 0:3 * P]) \
                .then_inc(probT_out, 1)

        def w_out_hook(i, c):
            if i or c:
                return
            act.wait_ge(pair_empty, 87)
            for step in range(HEADS + 2):
                if step < HEADS:
                    head_turned(step)
                if 0 <= step - 1 < HEADS:
                    head_exp(step - 1)
                if 0 <= step - 2 < HEADS:
                    head_probT(step - 2)
            for q in range(4):
                group(63 + q, 63 + q, x_hi[:, 4 * q:4 * q + 4, :], None)
        for i in range(2):
            run(ST["w_out"], i, w_out_hook)
        run(ST["proj1"], 0, lambda i, c: mixer_out(ST["w_out"], 6, ST["proj1"]),
            lambda: mixer_root(ST["w_out"], 0))
        for i in range(2):
            run(ST["gate1"], i, lambda i, c: four_groups(67, fm_a[:, 112:128], None) if i + c == 0 else None)
        gate_sigmoid(ST["gate1"])

    @block.vector
    def _(dve):
        steps = [0]
        tt, tsc, stt = nc.vector.tensor_tensor, nc.vector.tensor_scalar, nc.vector.scalar_tensor_tensor

        def then(ins):
            steps[0] += 1
            ins.then_inc(v_step, 1)
            dve.wait_ge(v_step, steps[0])

        def rest_unit(st, i, j):
            for half in range(2):
                dve.wait_ge(hi_split, st.half(i, j) + half + 1)
                n = st.size // 2
                slot = st.half_slot(j, half)
                tt(w_lo[slot][:, 0:n], raw[st.slot(j)][:, half * n:(half + 1) * n],
                   w_hi[slot][:, 0:n].bitcast(F32), ALU.subtract).then_inc(lo_split, 1)

        def add_ada(st, i, j, block_n, kk):
            dve.wait_ge(raw_full[st.slot(j)], st.landed(i, j))
            done = st.before("a", i, j)
            if isinstance(done, int) and done % 16 == 0:
                dve.wait_ge(acc_ready[ADA_ACC[block_n]], 16 * ADA_NTH[block_n])
            if not isinstance(done, int) or done > 0:
                dve.wait_ge(ada_added, done)
            buf = acc[ADA_ACC[block_n]]
            stt(out=buf[:], in0=raw[st.slot(j)][:], scalar=cond[:, ds(kk, 1)], in1=buf[:], op0=ALU.mult,
                op1=ALU.add).then_inc(ada_added, 1)

        def run(st, i, hook, ada=None, before=None):
            j = n_a = 0
            if before and isinstance(i, int) and i == 0:
                before()
            for c, (front, rest) in enumerate(st.chunks):
                for n, kind in enumerate(front + rest):
                    if n == len(front):
                        hook(i, c)
                    if kind == "w":
                        rest_unit(st, i, j)
                    else:
                        block_n, kk = ada(i, n_a)
                        add_ada(st, i, j, block_n, kk)
                        n_a += 1
                    j += 1
                if not rest:
                    hook(i, c)

        def no(i, c):
            pass

        def group_rest(s, hi, lo):
            dve.wait_ge(fm_hi, s + 1)
            tt(lo, y_fm[s % 2][:], hi.bitcast(F32), ALU.subtract).then_inc(fm_lo, 1)

        dve.wait_ge(vectors_in, 16 * N_VECTORS)
        nc.vector.tensor_copy(pos_f[0:2, :], pos_i[0:2, :]).then_inc(pos_ready, 1)
        dve.wait_ge(setup_tr, 1)
        then(nc.vector.tensor_copy(pos[:], ps[:, 4, 2 * P:2 * P + 2]))
        nc.vector.tensor_copy(fm_a[:], ps[:, 4, 0:P])
        nc.vector.tensor_copy(fm_b[:], ps[:, 4, P:2 * P]).then_inc(vectors_out, 1)
        dve.wait_ge(vectors_out, 1)
        dve.wait_ge(c_sig, 1)
        then(tt(cond[:], sig_c[:], fm_b[:, COL["c"]:COL["c"] + KT], ALU.mult))

        def sine_arg(buf, n, k):
            then(tsc(n, buf, INV_2PI, MAGIC, ALU.mult, ALU.add))
            then(tsc(n, n, MAGIC, None, ALU.subtract))
            for c in TWO_PI:
                then(stt(out=buf, in0=n, scalar=-c, in1=buf, op0=ALU.mult, op1=ALU.add))
            return tsc(buf, buf, SIN_MAX, -SIN_MAX, ALU.min, ALU.max)

        def hidden(layer):
            dve.wait_ge(hid_mm, layer + 1)
            bias = fm_b[0:HID, COL["b1"] + layer:COL["b1"] + layer + 1]
            freq = fm_b[0:HID, COL["freq"]:COL["freq"] + 1]
            then(tsc(hid_arg[0:HID, :], ps[0:HID, 0, 0:S], bias, freq, ALU.add, ALU.mult))
            sine_arg(hid_arg[0:HID, :], hid_n[0:HID, :], layer).then_inc(hid_red, 1)

        def filters(it):
            c = it % 2
            dve.wait_ge(filt_mm, it + 1)
            if it:
                dve.wait_ge(spec_mm, it)
            win = window[:, :, c * CH:(c + 1) * CH]
            tt(h_fwd[:], ps[:, 4:6, :], win, ALU.mult)
            tt(h_bwd[:], ps[:, 6:8, :], win, ALU.mult).then_inc(filt_win, 1)

        dve.wait_ge(hidden_in, 64)
        for t in range(2):
            then(tsc(rope_sin[:, t], freq[:], pos[:, t:t + 1], None, ALU.mult))
        then(sine_arg(rope_sin[:], ang_n[:], 0))
        then(tsc(rope_cos[:], rope_sin[:], math.pi / 2, None, ALU.add))
        sine_arg(rope_cos[:], ang_n[:], 0).then_inc(angles, 1)
        st = ST["ada"]
        for i in range(8):
            for j in range(4):
                add_ada(st, i, j, i // 4, 4 * (i % 4) + j)
                if i == 0 and j in (0, 2):
                    hidden(j // 2)
            if i in (1, 3, 5, 6):
                filters((1, 3, 5, 6).index(i))
        dve.wait_ge(ada_summed, 1)
        nc.vector.tensor_copy(mod[:, 0], ps[:, 0, 0:KT]).then_inc(mod_ready, 1)
        dve.wait_ge(ada_summed, 2)
        tsc(mod[:, 1], ps[:, 1, 0:KT], 1.0, None, ALU.add).then_inc(mod_ready, 1)
        for q in range(4):
            group_rest(q, x_hi[:, 4 * q:4 * q + 4, :], x_lo[:, 4 * q:4 * q + 4, :])

        def out_of_pair(st, i, c, m, out_):
            dve.wait_ge(half_used, chunk_end(st, i, c))
            dve.wait_ge(bias_full[m % 2], 16 * (m // 2 + 1))
            bias = bias_bc[m % 2][:].unsqueeze(1).to_broadcast([P, 2, CH])
            tt(out_, ps[:, 2 * (m % 2):2 * (m % 2) + 2, :], bias, ALU.add).then_inc(pair_empty, 1)

        def vu_out(m):
            out_of_pair(ST["in_vu"], m // 2, m % 2, m, vu[:, m // 2, :, (m % 2) * CH:(m % 2 + 1) * CH])

        def zh_out_(n):
            st, i = (ST["in_h"], n // 2) if n < 4 else (ST["in_h2"], 0)
            if n >= 2:
                dve.wait_ge(zh_stored[n % 2], 16 * (n // 2))
            out_of_pair(st, i, n % 2, 4 + n, zh_out[n % 2][:])

        def gate_out_(n):
            if n >= 2:
                dve.wait_ge(gate_stored[n % 2], 16 * (n // 2))
            out_of_pair(ST["in_g"], n // 2, n % 2, 10 + n, gate_out[n % 2][:])

        st = ST["in_vu"]
        for i in range(2):
            run(st, i, lambda i, c: vu_out(2 * i + c - 1) if i or c else None,
                lambda i, n: (2, 4 * i + n))

        def moments(src, width, t):
            for n in range(width // CH):
                ins = nc.vector.bn_stats(stats[:, t, n, :], src[:, t, n * CH:(n + 1) * CH])
            then(ins)
            then(nc.vector.bn_aggr(mv[:, t], stats[:, t, 0:width // CH, :].rearrange("p a b -> p (a b)")))

        def sgu_norm():
            dve.wait_ge(gelu_done, 2)
            for t in range(2):
                moments(vu[:, 0], W1, t)
            tsc(rstd[:, 0], mv[:, :, 1], LN_EPS, None, ALU.add).then_inc(var_ready, 1)

        def sgu_norm2():
            dve.wait_ge(std_ready, 1)
            then(nc.vector.reciprocal(rstd[:, 1], rstd[:, 0]))
            dve.wait_ge(sgu_consts, 32)
            for t in range(2):
                v = vu[:, 0, t]
                then(tsc(v, v, mv[:, t, 0:1], rstd[:, 1, t:t + 1], ALU.subtract, ALU.mult))
                then(tt(v, v, sgu_g[:], ALU.mult))
                tt(v, v, sgu_b[:], ALU.add).then_inc(vn_ready, 1)

        def in_h(i, c):
            n = 2 * i + c
            if n == 0:
                vu_out(3)
            else:
                zh_out_(n - 1)
            if n == 1:
                sgu_norm()
            if n == 3:
                sgu_norm2()
        st = ST["in_h"]
        for i in range(2):
            run(st, i, in_h, lambda i, n: (2, 8 + 4 * i + n))

        def sgu_gate():
            dve.wait_ge(gelu_done, 4)
            for t in range(2):
                dve.wait_ge(sgu_mm, t + 1)
                for g in range(8):
                    u = vu[:, 1, t, g * P:(g + 1) * P]
                    ins = stt(out=u, in0=ps[:, 4 + 2 * t + g // 4, (g % 4) * P:(g % 4 + 1) * P],
                              scalar=fm_b[:, COL["sgu_b"] + g:COL["sgu_b"] + g + 1], in1=u, op0=ALU.add, op1=ALU.mult)
            ins.then_inc(sgu_out, 1)

        def in_h2(i, c):
            zh_out_(3 + c)
            if c == 0:
                sgu_gate()
        run(ST["in_h2"], 0, in_h2)

        def multiply(n):
            dve.wait_ge(hy_f, n + 1)
            dve.wait_ge(spec_in, 16 * (n + 1))
            re, im = ps[:, 4:6, :], ps[:, 6:8, :]
            k_re, k_im, o_re, o_im = spec[:, 0:2], spec[:, 2:4], prod[:, 0:2], prod[:, 2:4]
            tt(o_re, re, k_re, ALU.mult)
            then(tt(part[:], im, k_im, ALU.mult))
            then(tt(o_re, o_re, part[:], ALU.subtract))
            tt(o_im, re, k_im, ALU.mult)
            then(tt(part[:], im, k_re, ALU.mult))
            tt(o_im, o_im, part[:], ALU.add).then_inc(hy_prod, 1)

        def regate(n):
            dve.wait_ge(hy_i, n + 1)
            dve.wait_ge(skip_in, 16 * (n + 1))
            dve.wait_ge(hy_x_in[n % 2], 16 * (n // 2 + 1))
            y = hy_v[n // 2][:]
            then(tt(y, y, skip[:].unsqueeze(1).to_broadcast([P, 2, CH]), ALU.mult))
            then(tt(y, y, ps[:, 4:6, :], ALU.add))
            tt(y, y, hy_x[n % 2][:], ALU.mult).then_inc(hy_gated, 1)

        def in_g(i, c):
            n = 2 * i + c
            if n == 0:
                zh_out_(5)
                dve.wait_ge(ada_summed, 3)
                nc.vector.tensor_copy(mod[:, 2], ps[:, 4, 0:KT]).then_inc(mod_ready, 1)
            else:
                gate_out_(n - 1)
            if n % 2:
                multiply(n // 2)
            elif n:
                regate(n // 2 - 1)
            if n == 3:
                for q in range(2):
                    group_rest(4 + q, ya_hi[:, 4 * q:4 * q + 4, :], ya_lo[:, 4 * q:4 * q + 4, :])
        st = ST["in_g"]
        for i in range(4):
            run(st, i, in_g, lambda i, n: (3, 4 * i + n))
        gate_out_(7)
        regate(3)

        st = ST["mix"]

        def mix_out(i, branch):
            n = i % 2
            dve.wait_ge(half_used, chunk_end(ST["mix"], 0, 2 * i + branch))
            banks = ps[:, 2 * branch:2 * branch + 2, :]
            if branch == 0:
                dve.wait_ge(gate_loaded[n], 32 * (i // 2 + 1))
                if i >= 2:
                    dve.wait_ge(fm_full, 8 + i - 1)
                tt(mixed[n][:], banks, gate_in[n][:, 0], ALU.mult).then_inc(pair_empty, 1)
            else:
                tt(mix_b[:], banks, gate_in[n][:, 1], ALU.mult).then_inc(pair_empty, 1)
                dve.wait_ge(pair_empty, 18 + 2 * i + 2)
                tt(mixed[n][:], mixed[n][:], mix_b[:], ALU.add).then_inc(mix_ready, 1)

        def mix_hook(_, n):
            i, c = n // 2, n % 2
            if n < 2:
                dve.wait_ge(gate_stored[n], 64)
                group_rest(6 + n, yb_hi[:, 4 * n:4 * n + 4, :], yb_lo[:, 4 * n:4 * n + 4, :])
            if c == 1:
                mix_out(i, 0)
            elif i:
                mix_out(i - 1, 1)
                if i >= 2:
                    group_rest(8 + i - 2, x_hi[:, 4 * (i - 2):4 * (i - 1), :], x_lo[:, 4 * (i - 2):4 * (i - 1), :])
        run(ST["mix"], 0, mix_hook, lambda i, n: (4, n))

        def w_o_hook(i, c):
            n = 2 * i + c
            if n == 0:
                mix_out(3, 1)
                group_rest(10, x_hi[:, 8:12, :], x_lo[:, 8:12, :])
                group_rest(11, x_hi[:, 12:16, :], x_lo[:, 12:16, :])
                dve.wait_ge(ada_summed, 4)
                nc.vector.tensor_copy(acc[0][:], wide_bank(0)).then_inc(mod_ready, 1)

        def branch_out(st, n):
            dve.wait_ge(pre_ready, n + 2)
            for t in range(2):
                wait_product(dve, st, t)
                tt(tmp[:, t], wide_bank(t), acc[0][:], ALU.mult).then_inc(wide_empty, 1)
                dve.wait_ge(wide_empty, n + t + 1)
                then(tt(res[:, t], res[:, t], tmp[:, t], ALU.add))
                for k in range(D // CH):
                    ins = nc.vector.bn_stats(stats[:, t, k, :], res[:, t, k * CH:(k + 1) * CH])
                then(ins)
                nc.vector.bn_aggr(mv[:, t], stats[:, t].rearrange("p a b -> p (a b)")).then_inc(var_ready, 1)

        def normalized(n, t, to):
            dve.wait_ge(std_ready, n + t + 2)
            then(nc.vector.reciprocal(rstd[:, 1, t:t + 1], rstd[:, 0, t:t + 1]))
            return tsc(to, res[:, t], mv[:, t, 0:1], rstd[:, 1, t:t + 1], ALU.subtract, ALU.mult)

        def four_rests(g):
            for q in range(4):
                group_rest(g + q, x_hi[:, 4 * q:4 * q + 4, :], x_lo[:, 4 * q:4 * q + 4, :])

        def copy_pair(st, i, c, slot, to, free=None):
            dve.wait_ge(half_used, chunk_end(st, i, c))
            if free is not None:
                dve.wait_ge(fm_full, free)
            nc.vector.tensor_copy(to, ps[:, 2 * slot:2 * slot + 2, :]).then_inc(pair_empty, 1)

        def m1_out(st, i, c, n):
            copy_pair(st, i, c, c, ff_stage[c][:], n + 15 if not isinstance(n, int) or n >= 2 else None)

        st = ST["w_o"]
        for i in range(2):
            run(st, i, w_o_hook, lambda i, n: (4, 8 + 4 * i + n))

        def m1_hook(st, base):
            def hook(i, c):
                if c:
                    m1_out(st, i, 0, i * 2 + base)
                elif not isinstance(i, int) or i:
                    m1_out(st, i - 1, 1, i * 2 + (base - 1))
                elif base:
                    m1_out(ST["m1a"], 3, 1, 7)
                else:
                    four_rests(12)
            return hook

        def first_norm():
            branch_out(ST["w_o"], 0)
            dve.wait_ge(ada_summed, 5)
            tsc(mod[:, 3], ps[:, 3, 0:KT], 1.0, None, ALU.add).then_inc(mod_ready, 1)
            dve.wait_ge(mod_ready, 5)
            tt(mod[:, 4], mod[:, 3], fm_b[:, COL["ln1_g"]:COL["ln1_g"] + KT], ALU.mult)
            then(tt(mod[:, 5], mod[:, 3], fm_b[:, COL["ln1_b"]:COL["ln1_b"] + KT], ALU.mult))
            then(tt(mod[:, 5], mod[:, 5], mod[:, 2], ALU.add))
            for t in range(2):
                normalized(0, t, normed[:, t]).then_inc(normed_ready, 1)
        rounds(dve, ST["m1a"], lambda i: run(ST["m1a"], i, m1_hook(ST["m1a"], 0), lambda i, n: (5, i * 4 + n),
                                             first_norm))
        rounds(dve, ST["m1b"], lambda i: run(ST["m1b"], i, m1_hook(ST["m1b"], 8)))

        def jit_rest(s, src, n, c):
            dve.wait_ge(fm_hi, n + (s + 1))
            tt(x_lo[:, 4 * c:4 * c + 4], src[:, ds(n * 4, 4)], x_hi[:, 4 * c:4 * c + 4].bitcast(F32),
               ALU.subtract).then_inc(fm_lo, 1)

        def m2_hook(i, c):
            if isinstance(i, int) and i == 0 and c == 0:
                m1_out(ST["m1b"], 3, 1, 15)
                jit_rest(16, ff, 0, 0)
                dve.wait_ge(ada_summed, 6)
                nc.vector.tensor_copy(acc[0][:], wide_bank(0)).then_inc(g2_ready, 1)
            if not (isinstance(i, int) and i == 7 and c == 1):
                jit_rest(16, ff, i * 2 + (c + 1), 1 - c)
        rounds(dve, ST["m2"], lambda i: run(ST["m2"], i, m2_hook), last=True)

        root_n = [0]

        def inv_rms(t):
            root_n[0] += 1
            dve.wait_ge(roots, root_n[0])
            then(nc.vector.reciprocal(rstd[:, 1, t:t + 1], ss[:, t, 1:2]))
            return rstd[:, 1, t:t + 1]

        def norm_res():
            for t in range(2):
                tsc(normed[:, t], res[:, t], inv_rms(t), None, ALU.mult).then_inc(normed_ready, 1)

        def pool_u_hook(i, c):
            st = ST["pool_u"]
            if c:
                copy_pair(st, i, 0, 0, u_stage[0][:], i * 2 + 35 if not isinstance(i, int) or i else None)
            elif not isinstance(i, int) or i:
                copy_pair(st, i - 1, 1, 1, u_stage[1][:], i * 2 + 34 if not isinstance(i, int) or i > 1 else None)
            else:
                four_rests(32)

        def second_norm():
            branch_out(ST["m2"], 2)
            dve.wait_ge(ln2_in, 32)
            for t in range(2):
                then(normalized(2, t, tmp[:, t]))
                then(tt(tmp[:, t], tmp[:, t], ln2_g[:], ALU.mult))
                tt(res[:, t], tmp[:, t], ln2_b[:], ALU.add).then_inc(res_ready, 1)
            norm_res()
        rounds(dve, ST["pool_u"], lambda i: run(ST["pool_u"], i, pool_u_hook, before=second_norm))

        def jit_group_rest(i):
            for c in range(2):
                dve.wait_ge(fm_hi, i * 2 + (37 + c))
                tt(g_lo[:, 4 * c:4 * c + 4], pooled[:, ds(i * 8 + 4 * c, 4)], g_hi[:, 4 * c:4 * c + 4].bitcast(F32),
                   ALU.subtract).then_inc(fm_lo, 1)

        def pool_product(i, c):
            n = i * 2 + c
            dve.wait_ge(silu_ready, n + 1)
            gate = pool_gate[:]
            if not isinstance(n, int) or n >= 2:
                dve.wait_ge(fm_full, n + 43)
            tt(pool_stage[c][:], ps[:, 2:4, :], gate, ALU.mult).then_inc(pair_empty, 1)
            dve.wait_ge(pair_empty, i * 4 + (52 + 2 * c))
            tt(pool_stage[c][:], pool_stage[c][:], group_out[:], ALU.mult).then_inc(product_ready, 1)

        def pool_g_hook(i, c):
            st = ST["pool_g"]
            first = isinstance(i, int) and i == 0
            if c == 0:
                if first:
                    copy_pair(ST["pool_u"], 3, 1, 1, u_stage[1][:], 42)
                    jit_group_rest(0)
                else:
                    pool_product(i - 1, 1)
            if c == 1:
                if first:
                    dve.wait_ge(fm_full, 44)
                copy_pair(st, i, 0, 0, group_out[:])
            if c == 2:
                pool_product(i, 0)
            if c == 3:
                copy_pair(st, i, 2, 0, group_out[:])
                if not (isinstance(i, int) and i == 3):
                    jit_group_rest(i + 1)
        rounds(dve, ST["pool_g"], lambda i: run(ST["pool_g"], i, pool_g_hook), last=True)

        def pool_out_hook(i, c):
            if isinstance(i, int) and i == 0 and c == 0:
                pool_product(3, 1)
                group_rest(44, p_hi[:], p_lo[:])
                jit_rest(45, pooled, 0, 0)
            if not (isinstance(i, int) and i == 3 and c == 1):
                jit_rest(45, pooled, i * 2 + (c + 1), 1 - c)
        rounds(dve, ST["pool_out"], lambda i: run(ST["pool_out"], i, pool_out_hook), last=True)

        wide = [4]

        def wide_read(ins):
            wide[0] += 1
            ins.then_inc(wide_empty, 1)

        def mixer_scaled(layer, gain, t):
            dve.wait_ge(post_in[layer], 16)
            wide_read(stt(out=tmp[:, t], in0=wide_bank(t), scalar=inv_rms(t), in1=gain[:], op0=ALU.mult,
                          op1=ALU.mult))

        def mixer_out(layer, gain, proj_st):
            mixer_scaled(layer, gain, 1)
            for t in range(2):
                dve.wait_ge(wide_empty, wide[0] - 1 + t)
                tt(res[:, t], res[:, t], tmp[:, t], ALU.add).then_inc(res_ready, 1)
            norm_res()
            wait_product(dve, proj_st, 1)
            wide_read(nc.vector.tensor_copy(proj[:, 1], wide_bank(1)))

        def gate_out_wide(n):
            for t in range(2):
                dve.wait_ge(gate_read, n + t + 1)
                if t == 0:
                    dve.wait_ge(wide_empty, wide[0])
                wide_read(tt(proj[:, t], proj[:, t], tmp[:, t], ALU.mult))
                dve.wait_ge(wide_empty, wide[0])
                tt(res[:, t], res[:, t], proj[:, t], ALU.add).then_inc(res_ready, 1)

        run(ST["proj0"], 0, lambda i, c: mixer_out(0, post_g, ST["proj0"]),
            before=lambda: mixer_scaled(0, post_g, 0))
        for i in range(2):
            run(ST["gate0"], i, lambda i, c: four_rests(53) if i + c == 0 else None)

        def latent_norm():
            dve.wait_ge(lat_sq, 1)
            then(nc.vector.reciprocal(lat_ss[:, 2], lat_ss[:, 1]))
            for w in range(4):
                part_w = lat[:, w % 2, w // 2]
                ins = tsc(part_w, part_w, lat_ss[:, 2, w:w + 1], None, ALU.mult)
                if w % 2:
                    ins.then_inc(lat_ready, 1)

        def mla_out(n):
            if n < 2:
                copy_pair(ST["mla_in"], n // 2, n % 2, n % 2, lat[:, :, n])
                return
            dve.wait_ge(mla_silu, n - 1)
            if n >= 4:
                dve.wait_ge(mla_gate_stored[n % 2], 16)
            tt(mla_gate_out[n % 2][:], ps[:, 2 * (n % 2):2 * (n % 2) + 2, :], mla_sig[n % 2][:], ALU.mult) \
                .then_inc(pair_empty, 1)

        def mla_in_hook(i, c):
            n = 2 * i + c
            if n == 0:
                four_rests(57)
            else:
                mla_out(n - 1)
            if n == 4:
                latent_norm()

        def gate_norm():
            gate_out_wide(0)
            norm_res()
        for i in range(3):
            run(ST["mla_in"], i, mla_in_hook, before=gate_norm)
        run(ST["k_pe"], 0, lambda i, c: mla_out(5))

        q_flat = q_tm[:].rearrange("p t h d -> p t (h d)")
        kv_flat = kv_tm[:].rearrange("p t h d -> p t (h d)")

        def latent_out(st, n, m, to):
            copy_pair(st, 0, n, m % 2, to[:, :, n * CH:(n + 1) * CH])

        def rotate(x1, x2, cos, sin, scratch):
            for out_, x, table in ((0, x1, cos), (1, x2, sin), (2, x2, cos), (3, x1, sin)):
                ins = tt(scratch(out_), x, table, ALU.mult)
            then(ins)
            tt(x1, scratch(0), scratch(1), ALU.subtract)
            then(tt(x2, scratch(2), scratch(3), ALU.add))

        def rotate_heads(t):
            x = q_tm[:, t, :, NOPE:QK]
            cos, sin = (tb[:, t].unsqueeze(1).to_broadcast([P, HEADS, ROPE // 2]) for tb in (rope_cos, rope_sin))
            rotate(x[:, :, 0:ROPE // 2], x[:, :, ROPE // 2:ROPE], cos, sin, lambda n: rope_t[:, n])

        def w_uq_hook(i, c):
            if c == 0:
                dve.wait_ge(half_used, end(ST["k_pe"]))
                nc.vector.tensor_copy(k_pe[:], ps[:, 0:2, 0:ROPE]).then_inc(pair_empty, 1)
                group_rest(61, x_hi[:, 0:4, :], x_lo[:, 0:4, :])
                group_rest(62, x_hi[:, 4:8, :], x_lo[:, 4:8, :])
            else:
                latent_out(ST["w_uq"], c - 1, 73 + c - 1, q_flat)
        run(ST["w_uq"], 0, w_uq_hook)

        def w_ukv_hook(i, c):
            if c == 0:
                latent_out(ST["w_uq"], 5, 78, q_flat)
                for slot in mla_gate_stored:
                    dve.wait_ge(slot, 32)
                dve.wait_ge(sines, 2)
            else:
                latent_out(ST["w_ukv"], c - 1, 79 + c - 1, kv_flat)
            if c in (2, 4):
                dve.wait_ge(pair_empty, 79)
                rotate_heads(c // 2 - 1)
            if c == 6:
                rotate(k_pe[:, :, 0:ROPE // 2], k_pe[:, :, ROPE // 2:ROPE], rope_cos[:], rope_sin[:],
                       lambda n: rope_t[:, n, 0:2])
        run(ST["w_ukv"], 0, w_ukv_hook)

        def head_qpe(h):
            dve.wait_ge(qk_turned, h + 1)
            if h >= 2:
                dve.wait_ge(scored, h - 1)
            nc.vector.tensor_copy(q_peT[h % 2][0:ROPE, :], ps[0:ROPE, 2, 0:S]).then_inc(qpe_out, 1)

        def head_scores(h):
            dve.wait_ge(scored, h + 1)
            if h >= 2:
                dve.wait_ge(prob_ready, 2 * (h - 1))
            then(stt(out=score[h % 2][:].rearrange("p b k -> p (b k)"), in0=ps[:, 3 + h % 2, 0:3 * P],
                     scalar=SM_SCALE, in1=mask[:].rearrange("p b k -> p (b k)"), op0=ALU.mult, op1=ALU.add))
            nc.vector.reduce_max(sm_max[:, h % 4, 0:1], score[h % 2][:, 0], axis=AX.X)
            then(nc.vector.reduce_max(sm_max[:, h % 4, 1:2], score[h % 2][:, 1:3].rearrange("p b k -> p (b k)"),
                                      axis=AX.X))
            tsc(sm_max[:, h % 4], sm_max[:, h % 4], -1.0, None, ALU.mult).then_inc(score_ready, 1)

        def head_out(h):
            dve.wait_ge(o_mm, h + 1)
            then(nc.vector.reciprocal(sm_inv[:, h % 4], sm_sum[:, h % 4]))
            for t in range(2):
                ins = stt(out=q_tm[:, t, h, 0:VD], in0=ps[:, 7, t * P:(t + 1) * P], scalar=sm_inv[:, h % 4, t:t + 1],
                          in1=g_tm[:, t, h * VD:(h + 1) * VD], op0=ALU.mult, op1=ALU.mult)
            ins.then_inc(o_ready, 1)

        def w_out_hook(i, c):
            if i or c:
                return
            copy_pair(ST["w_ukv"], 0, 7, 0, kv_flat[:, :, 7 * CH:8 * CH])
            dve.wait_ge(pair_empty, 87)
            dve.wait_ge(k_peT_ready, 1)
            nc.vector.tensor_copy(k_peT[0:ROPE, :], ps[0:ROPE, 7, 0:S]).then_inc(k_peT_out, 1)
            dve.wait_ge(mask_ready, 2)
            for step in range(HEADS + 3):
                if step < HEADS:
                    head_qpe(step)
                if 0 <= step - 1 < HEADS:
                    head_scores(step - 1)
                if 0 <= step - 3 < HEADS:
                    if step == 3:
                        dve.wait_ge(g_loaded, 16)
                    head_out(step - 3)
            four_rests(63)
        for i in range(2):
            run(ST["w_out"], i, w_out_hook)
        run(ST["proj1"], 0, lambda i, c: mixer_out(1, post_g1, ST["proj1"]),
            before=lambda: mixer_scaled(1, post_g1, 0))
        for i in range(2):
            run(ST["gate1"], i, lambda i, c: four_rests(67) if i + c == 0 else None)
        gate_out_wide(2)


def kernel(**inputs):
    import numpy as _np
    import concourse.bacc as _bacc
    from concourse import mybir as _mybir
    from concourse.bass_utils import run_bass_kernel_spmd as _run

    nc = _bacc.Bacc("TRN2", target_bir_lowering=False, num_devices=1)
    arrays, aps = {}, {}
    for name, value in {**inputs, **tables()}.items():
        v = _np.ascontiguousarray(value)
        arrays[f"in_{name}"] = v
        aps[name] = nc.dram_tensor(f"in_{name}", v.shape, _mybir.dt.from_np(v.dtype), kind="ExternalInput").ap()
    out = nc.dram_tensor("out", (1, S, D), _mybir.dt.float32, kind="ExternalOutput").ap()
    block_kernel(nc, aps, out)
    return _run(nc, [arrays], core_ids=[0]).results[0]["out"]
```
